# Optimizing a Trainium2 kernel written in Bass

```python
import jax, jax.numpy as jnp
from jax import lax
import numpy as np

D_MODEL = 1024
BATCH = 1
SEQ = 512
DEPTH = 1

CHUNK = 64
N_MEM = 256
HEAD_DIM = 64
D_MIX = D_MODEL
FOX_HEADS = D_MIX // 2 // HEAD_DIM
CHK_HEADS = D_MIX // 2 // HEAD_DIM
D_FOX = FOX_HEADS * HEAD_DIM
D_CHK = CHK_HEADS * HEAD_DIM
LEFT_CHUNKS = 8
BAND = (LEFT_CHUNKS + 1) * CHUNK
MAX_REL = 128
N_REL = 2 * MAX_REL + 1
Q_BLOCK = 128
MEM_HEADS = 4
MEM_HEAD_DIM = D_MODEL // MEM_HEADS
D_FF = 4 * D_MODEL
EPS = 1e-6
D_IN = 3 * D_FOX + FOX_HEADS + 3 * D_CHK


def rmsnorm(x, g):
    xf = x.astype(jnp.float32)
    y = xf * lax.rsqrt(jnp.mean(xf * xf, axis=-1, keepdims=True) + EPS) * g.astype(jnp.float32)
    return y.astype(x.dtype)

def forgetting_attention(q, k, v, f_logit):
    S = q.shape[1]
    Dh = q.shape[-1]
    scale = Dh ** -0.5
    logf = jax.nn.log_sigmoid(f_logit.astype(jnp.float32))
    c = jnp.cumsum(logf, axis=1).transpose(0, 2, 1)
    pos = jnp.arange(S)
    outs = []
    for i in range(S // Q_BLOCK):
        q0, q1 = i * Q_BLOCK, (i + 1) * Q_BLOCK
        qb = q[:, q0:q1]
        kb = k[:, :q1]
        vb = v[:, :q1]
        logits = jnp.einsum('bqhd,bkhd->bhqk', qb, kb).astype(jnp.float32) * scale
        logits = logits + c[:, :, q0:q1, None] - c[:, :, None, :q1]
        causal = pos[q0:q1, None] >= pos[None, :q1]
        logits = jnp.where(causal[None, None], logits, -jnp.inf)
        p = jax.nn.softmax(logits, axis=-1).astype(v.dtype)
        outs.append(jnp.einsum('bhqk,bkhd->bqhd', p, vb))
    return jnp.concatenate(outs, axis=1)

def _rel_index():
    i = np.arange(CHUNK)[:, None]
    m = np.arange(BAND)[None, :]
    rel = i + LEFT_CHUNKS * CHUNK - m
    return np.clip(rel, -MAX_REL, MAX_REL) + MAX_REL

def chunked_relpos_attention(q, k, v, rel_table):
    B, S, H, Dh = q.shape
    NC = S // CHUNK
    scale = Dh ** -0.5
    qc = q.reshape(B, NC, CHUNK, H, Dh)
    pad = ((0, 0), (LEFT_CHUNKS * CHUNK, 0), (0, 0), (0, 0))
    kp = jnp.pad(k, pad).reshape(B, NC + LEFT_CHUNKS, CHUNK, H, Dh)
    vp = jnp.pad(v, pad).reshape(B, NC + LEFT_CHUNKS, CHUNK, H, Dh)
    kband = jnp.concatenate([kp[:, j:j + NC] for j in range(LEFT_CHUNKS + 1)], axis=2)
    vband = jnp.concatenate([vp[:, j:j + NC] for j in range(LEFT_CHUNKS + 1)], axis=2)
    bias = rel_table.astype(jnp.float32)[:, _rel_index()]
    key_pos = jnp.arange(NC)[:, None] * CHUNK + jnp.arange(BAND)[None, :] - LEFT_CHUNKS * CHUNK
    valid = key_pos >= 0
    logits = jnp.einsum('bcqhd,bckhd->bhcqk', qc, kband).astype(jnp.float32) * scale
    logits = logits + bias[None, :, None]
    logits = jnp.where(valid[None, None, :, None, :], logits, -jnp.inf)
    p = jax.nn.softmax(logits, axis=-1).astype(v.dtype)
    out = jnp.einsum('bhcqk,bckhd->bcqhd', p, vband)
    return out.reshape(B, S, H, Dh)

def memory_cross_attention(h, mem_n, w_mq, w_mk, w_mv, w_mo):
    B, S, _ = h.shape
    M = mem_n.shape[1]
    q = (h @ w_mq).reshape(B, S, MEM_HEADS, MEM_HEAD_DIM)
    k = (mem_n @ w_mk).reshape(B, M, MEM_HEADS, MEM_HEAD_DIM)
    v = (mem_n @ w_mv).reshape(B, M, MEM_HEADS, MEM_HEAD_DIM)
    logits = jnp.einsum('bshd,bmhd->bhsm', q, k).astype(jnp.float32) * (MEM_HEAD_DIM ** -0.5)
    p = jax.nn.softmax(logits, axis=-1).astype(v.dtype)
    o = jnp.einsum('bhsm,bmhd->bshd', p, v).reshape(B, S, D_MODEL)
    return o @ w_mo

def first_inputs(seed: int = 0) -> dict:
    key = jax.random.key(seed)
    ks = jax.random.split(key, 24)
    f32 = jnp.float32

    def w(k, shape, fan_in):
        return jax.random.normal(k, shape, f32) * fan_in ** -0.5

    def gain(k, n):
        return 1.0 + 0.05 * jax.random.normal(k, (DEPTH, n), f32)

    return {
        'x': jax.random.normal(ks[0], (BATCH, SEQ, D_MODEL), f32),
        'mem': jax.random.normal(ks[1], (BATCH, N_MEM, D_MODEL), f32),
        'w_in': w(ks[2], (DEPTH, D_MODEL, D_IN), D_MODEL),
        'b_fgt': 3.0 + 0.1 * jax.random.normal(ks[3], (DEPTH, FOX_HEADS), f32),
        'rel_bias': 0.2 * jax.random.normal(ks[4], (DEPTH, CHK_HEADS, N_REL), f32),
        'g_fox_out': gain(ks[5], D_FOX),
        'g_chk_out': gain(ks[6], D_CHK),
        'w_out': w(ks[7], (DEPTH, D_MIX, D_MODEL), D_MIX),
        'g_mix_pre': gain(ks[8], D_MODEL),
        'g_mix_post': gain(ks[9], D_MODEL),
        'g_mem_kv': gain(ks[10], D_MODEL),
        'w_mq': w(ks[11], (DEPTH, D_MODEL, D_MODEL), D_MODEL),
        'w_mk': w(ks[12], (DEPTH, D_MODEL, D_MODEL), D_MODEL),
        'w_mv': w(ks[13], (DEPTH, D_MODEL, D_MODEL), D_MODEL),
        'w_mo': w(ks[14], (DEPTH, D_MODEL, D_MODEL), D_MODEL),
        'g_mem_pre': gain(ks[15], D_MODEL),
        'g_mem_post': gain(ks[16], D_MODEL),
        'w_ff1': w(ks[17], (DEPTH, D_MODEL, D_FF), D_MODEL),
        'w_ff2': w(ks[18], (DEPTH, D_FF, D_MODEL), D_FF),
        'g_ff_pre': gain(ks[19], D_MODEL),
        'g_ff_post': gain(ks[20], D_MODEL),
    }

def first_block(x, mem, w_in, b_fgt, rel_bias, g_fox_out, g_chk_out, w_out, g_mix_pre, g_mix_post,
              g_mem_kv, w_mq, w_mk, w_mv, w_mo, g_mem_pre, g_mem_post,
              w_ff1, w_ff2, g_ff_pre, g_ff_post):
    B, S, _ = x.shape
    for l in range(DEPTH):
        h = rmsnorm(x, g_mix_pre[l])
        proj = h @ w_in[l]
        o0 = 0
        fq = proj[..., o0:o0 + D_FOX]; o0 += D_FOX
        fk = proj[..., o0:o0 + D_FOX]; o0 += D_FOX
        fv = proj[..., o0:o0 + D_FOX]; o0 += D_FOX
        f_logit = proj[..., o0:o0 + FOX_HEADS] + b_fgt[l]; o0 += FOX_HEADS
        cq = proj[..., o0:o0 + D_CHK]; o0 += D_CHK
        ck = proj[..., o0:o0 + D_CHK]; o0 += D_CHK
        cv = proj[..., o0:o0 + D_CHK]
        shp_f = (B, S, FOX_HEADS, HEAD_DIM)
        shp_c = (B, S, CHK_HEADS, HEAD_DIM)
        y_fox = forgetting_attention(fq.reshape(shp_f), fk.reshape(shp_f), fv.reshape(shp_f), f_logit)
        y_chk = chunked_relpos_attention(cq.reshape(shp_c), ck.reshape(shp_c), cv.reshape(shp_c), rel_bias[l])
        y = jnp.concatenate([rmsnorm(y_fox.reshape(B, S, D_FOX), g_fox_out[l]),
                             rmsnorm(y_chk.reshape(B, S, D_CHK), g_chk_out[l])], axis=-1)
        x = x + rmsnorm(y @ w_out[l], g_mix_post[l])
        h = rmsnorm(x, g_mem_pre[l])
        mem_n = rmsnorm(mem, g_mem_kv[l])
        y = memory_cross_attention(h, mem_n, w_mq[l], w_mk[l], w_mv[l], w_mo[l])
        x = x + rmsnorm(y, g_mem_post[l])
        h = rmsnorm(x, g_ff_pre[l])
        y = jnp.square(jax.nn.relu(h @ w_ff1[l])) @ w_ff2[l]
        x = x + rmsnorm(y, g_ff_post[l])
    return x


D_MIX_2 = D_MODEL
ATT_HEADS = 8
ATT_KV_HEADS = 2
ATT_HEAD_DIM = 64
WINDOW = 128
ATT_BLOCK = 128
GLA_HEADS = 4
GLA_DK = 64
GLA_DV = 128
GLA_GATE_RANK = 16
GLA_TAU = 16.0
GLA_CHUNK = 64
PEER_HEADS = 8
PEER_QDIM = 256
N_KEYS = 128
N_EXPERTS = N_KEYS * N_KEYS
PEER_TOPK = 16
PEER_BLOCK = 128
NORM_EPS = 1e-6

ATT_Q_W = ATT_HEADS * ATT_HEAD_DIM
ATT_KV_W = ATT_KV_HEADS * ATT_HEAD_DIM
GLA_QK_W = GLA_HEADS * GLA_DK
GLA_V_W = GLA_HEADS * GLA_DV
IN_SIZES = (ATT_Q_W, ATT_KV_W, ATT_KV_W, GLA_QK_W, GLA_QK_W, GLA_V_W, GLA_V_W, GLA_GATE_RANK)
IN_WIDTH = sum(IN_SIZES)


def rms_norm(x, w):
    xf = x.astype(jnp.float32)
    y = xf * lax.rsqrt(jnp.mean(xf * xf, axis=-1, keepdims=True) + NORM_EPS)
    return (y * w.astype(jnp.float32)).astype(x.dtype)

def sliding_window_attention(q, k, v, sinks):
    B, S = q.shape[0], q.shape[1]
    nb = S // ATT_BLOCK
    G = ATT_HEADS // ATT_KV_HEADS
    qb = q.reshape(B, nb, ATT_BLOCK, ATT_KV_HEADS, G, ATT_HEAD_DIM)

    def band(t):
        tb = t.reshape(B, nb, ATT_BLOCK, ATT_KV_HEADS, ATT_HEAD_DIM)
        prev = jnp.pad(tb, ((0, 0), (1, 0), (0, 0), (0, 0), (0, 0)))[:, :-1]
        return jnp.concatenate([prev, tb], axis=2)

    kb, vb = band(k), band(v)
    scores = jnp.einsum('bnqhgd,bnkhd->bnhgqk', qb, kb).astype(jnp.float32) * (ATT_HEAD_DIM ** -0.5)
    blk = jnp.arange(nb)[:, None, None]
    qpos = blk * ATT_BLOCK + jnp.arange(ATT_BLOCK)[None, :, None]
    kpos = (blk - 1) * ATT_BLOCK + jnp.arange(2 * ATT_BLOCK)[None, None, :]
    rel = qpos - kpos
    mask = (rel >= 0) & (rel < WINDOW) & (kpos >= 0)
    scores = jnp.where(mask[None, :, None, None], scores, -jnp.inf)
    sink = sinks.astype(jnp.float32).reshape(ATT_KV_HEADS, G)[None, None, :, :, None, None]
    sink = jnp.broadcast_to(sink, scores.shape[:-1] + (1,))
    probs = jax.nn.softmax(jnp.concatenate([scores, sink], axis=-1), axis=-1)[..., :-1]
    out = jnp.einsum('bnhgqk,bnkhd->bnqhgd', probs.astype(v.dtype), vb)
    return out.reshape(B, S, ATT_Q_W)

def gla_chunked(q, k, v, log_a):
    B, S = q.shape[0], q.shape[1]
    nc = S // GLA_CHUNK

    def chunks(t):
        return t.astype(jnp.float32).reshape(B, nc, GLA_CHUNK, GLA_HEADS, t.shape[-1]).transpose(1, 0, 3, 2, 4)

    qc = chunks(q) * (GLA_DK ** -0.5)
    kc, vc, gc = chunks(k), chunks(v), chunks(log_a)
    causal = jnp.tril(jnp.ones((GLA_CHUNK, GLA_CHUNK), dtype=bool))

    def step(state, inp):
        qt, kt, vt, gt = inp
        b = jnp.cumsum(gt, axis=2)
        inter = jnp.einsum('bhtd,bhde->bhte', qt * jnp.exp(b), state)
        diff = b[:, :, :, None, :] - b[:, :, None, :, :]
        decay = jnp.exp(jnp.where(causal[:, :, None], diff, -jnp.inf))
        att = jnp.einsum('bhtd,bhsd,bhtsd->bhts', qt, kt, decay)
        intra = jnp.einsum('bhts,bhse->bhte', att, vt)
        b_last = b[:, :, -1:, :]
        new_state = jnp.exp(b_last[:, :, 0, :, None]) * state + jnp.einsum(
            'bhsd,bhse->bhde', kt * jnp.exp(b_last - b), vt)
        return new_state, inter + intra

    state0 = jnp.zeros((B, GLA_HEADS, GLA_DK, GLA_DV), jnp.float32)
    _, out = lax.scan(step, state0, (qc, kc, vc, gc))
    return out.transpose(1, 0, 3, 2, 4).reshape(B, S, GLA_HEADS, GLA_DV)

def peer_ffn(h, wq, subkeys, u, v):
    B, S, D = h.shape
    q = (h @ wq).reshape(B, S, PEER_HEADS, 2, PEER_QDIM // 2)
    sub_scores = jnp.einsum('bshpk,hpnk->bshpn', q, subkeys).astype(jnp.float32)
    top_v, top_i = lax.top_k(sub_scores, PEER_TOPK)
    cand = (top_v[..., 0, :, None] + top_v[..., 1, None, :]).reshape(B, S, PEER_HEADS, PEER_TOPK * PEER_TOPK)
    cand_i = (top_i[..., 0, :, None] * N_KEYS + top_i[..., 1, None, :]).reshape(B, S, PEER_HEADS, PEER_TOPK * PEER_TOPK)
    best_v, best_pos = lax.top_k(cand, PEER_TOPK)
    expert = jnp.take_along_axis(cand_i, best_pos, axis=-1)
    gates = jax.nn.softmax(best_v, axis=-1).astype(h.dtype)
    nblk = (B * S) // PEER_BLOCK
    xs = h.reshape(nblk, PEER_BLOCK, D)
    es = expert.reshape(nblk, PEER_BLOCK, PEER_HEADS * PEER_TOPK)
    gs = gates.reshape(nblk, PEER_BLOCK, PEER_HEADS * PEER_TOPK)

    def block(args):
        xb, eb, gb = args
        ub = jnp.take(u, eb, axis=0)
        hid = jax.nn.gelu(jnp.einsum('tkd,td->tk', ub, xb), approximate=False) * gb
        vb = jnp.take(v, eb, axis=0)
        return jnp.einsum('tk,tkd->td', hid, vb)

    return lax.map(block, (xs, es, gs)).reshape(B, S, D)

def second_inputs(seed: int = 0) -> dict:
    key = jax.random.key(seed)
    ks = jax.random.split(key, 20)
    f32 = jnp.float32
    nrm = lambda k, shape, s: jax.random.normal(k, shape, f32) * s
    L = DEPTH
    return {
        "x": nrm(ks[0], (BATCH, SEQ, D_MODEL), 1.0),
        "c": nrm(ks[1], (BATCH, D_MODEL), 1.0),
        "w_ada": nrm(ks[2], (L, D_MODEL, 6 * D_MODEL), 0.5 * D_MODEL ** -0.5),
        "b_ada": nrm(ks[3], (L, 6 * D_MODEL), 0.02),
        "norm1_w": 1.0 + nrm(ks[4], (L, D_MODEL), 0.02),
        "w_in": nrm(ks[5], (L, D_MODEL, IN_WIDTH), D_MODEL ** -0.5),
        "attn_sinks": nrm(ks[6], (L, ATT_HEADS), 0.5),
        "gla_gate_up": nrm(ks[7], (L, GLA_GATE_RANK, GLA_QK_W), GLA_GATE_RANK ** -0.5),
        "gla_gate_bias": nrm(ks[8], (L, GLA_QK_W), 0.1),
        "gla_norm_w": 1.0 + nrm(ks[9], (L, GLA_DV), 0.02),
        "w_out": nrm(ks[10], (L, D_MIX_2, D_MODEL), D_MIX_2 ** -0.5),
        "norm2_w": 1.0 + nrm(ks[11], (L, D_MODEL), 0.02),
        "peer_wq": nrm(ks[12], (L, D_MODEL, PEER_HEADS * PEER_QDIM), D_MODEL ** -0.5),
        "peer_subkeys": nrm(ks[13], (L, PEER_HEADS, 2, N_KEYS, PEER_QDIM // 2), (PEER_QDIM // 2) ** -0.5),
        "peer_u": nrm(ks[14], (L, N_EXPERTS, D_MODEL), D_MODEL ** -0.5),
        "peer_v": nrm(ks[15], (L, N_EXPERTS, D_MODEL), (PEER_HEADS * PEER_TOPK) ** -0.5),
        "final_norm_w": 1.0 + nrm(ks[16], (D_MODEL,), 0.02),
    }

def second_block(x, c, w_ada, b_ada, norm1_w, w_in, attn_sinks, gla_gate_up, gla_gate_bias, gla_norm_w,
              w_out, norm2_w, peer_wq, peer_subkeys, peer_u, peer_v, final_norm_w):
    B, S, _ = x.shape
    split_points = np.cumsum(np.array(IN_SIZES))[:-1].tolist()
    for l in range(DEPTH):
        mod = jax.nn.silu(c) @ w_ada[l] + b_ada[l]
        shift1, scale1, gate1, shift2, scale2, gate2 = jnp.split(mod[:, None, :], 6, axis=-1)

        h = rms_norm(x, norm1_w[l]) * (1.0 + scale1) + shift1
        proj = h @ w_in[l]
        aq, ak, av, gq, gk, gv, gg, glr = jnp.split(proj, split_points, axis=-1)
        att = sliding_window_attention(
            aq.reshape(B, S, ATT_HEADS, ATT_HEAD_DIM),
            ak.reshape(B, S, ATT_KV_HEADS, ATT_HEAD_DIM),
            av.reshape(B, S, ATT_KV_HEADS, ATT_HEAD_DIM),
            attn_sinks[l])
        log_a = jax.nn.log_sigmoid((glr @ gla_gate_up[l] + gla_gate_bias[l]).astype(jnp.float32)) / GLA_TAU
        go = gla_chunked(
            gq.reshape(B, S, GLA_HEADS, GLA_DK),
            gk.reshape(B, S, GLA_HEADS, GLA_DK),
            gv.reshape(B, S, GLA_HEADS, GLA_DV),
            log_a.reshape(B, S, GLA_HEADS, GLA_DK))
        go = rms_norm(go, gla_norm_w[l]).reshape(B, S, GLA_V_W).astype(x.dtype) * jax.nn.silu(gg)
        mixed = jnp.concatenate([att, go], axis=-1) @ w_out[l]
        x = x + gate1 * mixed

        h2 = rms_norm(x, norm2_w[l]) * (1.0 + scale2) + shift2
        x = x + gate2 * peer_ffn(h2, peer_wq[l], peer_subkeys[l], peer_u[l], peer_v[l])
    return rms_norm(x, final_norm_w)


def setup_inputs(seed=0):
    out = dict(first_inputs(seed))
    for name, value in second_inputs(seed + 1).items():
        if name != "x":
            out[name + "_2"] = value
    return out


def reference(
    x, mem, w_in, b_fgt, rel_bias, g_fox_out, g_chk_out, w_out, g_mix_pre, g_mix_post, g_mem_kv,
    w_mq, w_mk, w_mv, w_mo, g_mem_pre, g_mem_post, w_ff1, w_ff2, g_ff_pre, g_ff_post, c_2,
    w_ada_2, b_ada_2, norm1_w_2, w_in_2, attn_sinks_2, gla_gate_up_2, gla_gate_bias_2,
    gla_norm_w_2, w_out_2, norm2_w_2, peer_wq_2, peer_subkeys_2, peer_u_2, peer_v_2,
    final_norm_w_2,
):
    x = first_block(
        x, mem, w_in, b_fgt, rel_bias, g_fox_out, g_chk_out, w_out, g_mix_pre, g_mix_post,
        g_mem_kv, w_mq, w_mk, w_mv, w_mo, g_mem_pre, g_mem_post, w_ff1, w_ff2, g_ff_pre,
        g_ff_post,
    )
    return second_block(
        x, c_2, w_ada_2, b_ada_2, norm1_w_2, w_in_2, attn_sinks_2, gla_gate_up_2,
        gla_gate_bias_2, gla_norm_w_2, w_out_2, norm2_w_2, peer_wq_2, peer_subkeys_2, peer_u_2,
        peer_v_2, final_norm_w_2,
    )


_drawn_inputs = setup_inputs


def setup_inputs(seed=0):
    import zlib

    import numpy as np

    out = dict(_drawn_inputs(seed))
    spreads = {}
    factors = {'b_ada_2': 6.126,
     'norm1_w_2': 8.0,
     'attn_sinks_2': 8.0,
     'gla_gate_bias_2': 8.0,
     'gla_norm_w_2': 8.0,
     'norm2_w_2': 8.0,
     'peer_wq_2': 7.655,
     'peer_subkeys_2': 7.643,
     'peer_u_2': 8.0,
     'peer_v_2': 7.606,
     'final_norm_w_2': 2.736}
    for name, (base, spread) in spreads.items():
        noise = np.random.default_rng([zlib.crc32(name.encode()), seed]).standard_normal(out[name].shape)
        drawn = base * np.exp(spread * noise) if base else spread * noise
        out[name] = __import__('jax').numpy.asarray(drawn.astype(out[name].dtype))
    for name, factor in factors.items():
        out[name] = (out[name] * factor).astype(out[name].dtype)
    return out
```

```python
from contextlib import ExitStack

import numpy as np

import concourse.bass as bass
from concourse import mybir

F32 = mybir.dt.float32
BF16 = mybir.dt.bfloat16
U32 = mybir.dt.uint32
ALU = mybir.AluOpType
ACT = mybir.ActivationFunctionType
AX = mybir.AxisListType

P = 128
TOK = 512
NB = TOK // P
D = 1024
KT = D // P
COLS = 512
EPS = 1e-6
NEG = -1e30

HEADS = 8
HD = 64
SPAN = 64
MAX_REL = 128
REL_W = TOK + P - 1
MEM = 256
MB = MEM // P
MEM_HEADS = 4
MEM_HD = D // MEM_HEADS
FF_T = 4 * D // P

SWA_HEADS = 8
GLA_HEADS = 4
GLA_DV = 128
GLA_RANK = 16
GLA_TAU = 16.0
GLA_HALVES = [1, 2, 4, 8, 16, 32, 64, 128, 256]

PEER_HEADS = 8
TOPK = 16
SLOTS = PEER_HEADS * TOPK
N_KEYS = 128
CAND_ROWS = [TOPK // (a + 1) for a in range(TOPK // 2)]
CAND_OFF = [sum(CAND_ROWS[:a]) for a in range(TOPK // 2)]
CAND_TAIL = sum(CAND_ROWS)
CAND = CAND_TAIL + TOPK // 2
RING = 8
TURNS = SLOTS // RING

W_SLOTS = 3
C_IN, C_OUT, C_MK, C_MV, C_MQ, C_MO, C_FF1, C_FF2, C_IN2, C_OUT2, C_WQ, C_END = (
    0, 6, 8, 10, 12, 14, 16, 24, 32, 37, 39, 43)
G_IN, G_OUT, G_MK, G_MV, G_MQ, G_MO, G_FF1, G_FF2, G_IN2, G_OUT2, G_WQ, G_END = (
    0, 24, 32, 40, 44, 52, 60, 92, 100, 122, 130, 146)

(N_MIX, N_Y, N_MEM, N_MEMPRE, N_MEMY, N_FF, N_ATT2, N_Y2, N_PEER) = range(9)
STATS = {N_MIX: 0, N_Y: 4, N_MEM: 12, N_MEMPRE: 14, N_FF: 18, N_ATT2: 22, N_PEER: 26}
BLOCKS = {N_MIX: 0, N_Y: 4, N_MEM: 8, N_MEMPRE: 10, N_FF: 14, N_ATT2: 18, N_PEER: 22}
(GC_MIX, GC_Y, GC_MEMKV, GC_MEMPRE, GC_FF, GC_ATT2, GC_PEER) = range(7)

U_FOX, U_CHK, U_MEM, U_SWA, U_END = 0, 32, 64, 80, 112


def unit(u):
    if u < U_CHK:
        return "fox", u // NB, u % NB, (u % NB + 1) * P
    if u < U_MEM:
        return "chk", (u - U_CHK) // NB, u % NB, (u % NB + 1) * P
    if u < U_SWA:
        return "mem", (u - U_MEM) // NB, u % NB, MEM
    return "swa", (u - U_SWA) // NB, u % NB, (P if u % NB == 0 else 2 * P)


def build(nc, A, out):
    ctx = ExitStack()
    with ctx:
        def sb(name, shape, dt=F32):
            return ctx.enter_context(nc.sbuf_tensor(name, shape, dt))

        def sem(name):
            return ctx.enter_context(nc.semaphore(name))

        bank = [ctx.enter_context(nc.psum_tensor(f"bank{i}", [P, COLS], F32)) for i in range(8)]

        X = sb("x_res", [P, NB, D])
        XN = sb("x_norm", [P, NB, D])
        HT = sb("h_T", [P, KT, TOK])
        W = sb("weights", [P, W_SLOTS, KT * COLS])
        AREA = sb("area", [P, 16384])
        SCR = sb("scratch", [P, 4096])
        GROW = sb("gain_rows", [P, 2, D])
        GATE = sb("gate_rows", [P, 2, D])
        NWROW = sb("gla_norm_row", [P, COLS])
        ident = sb("ident", [P, P])
        identb = sb("ident_bf", [P, P], BF16)
        ones = sb("ones", [P, P])
        epsc = sb("eps_col", [P, 1])
        onesb = sb("ones_bf", [P, COLS], BF16)
        winb = sb("window_mask", [P, 2 * P], BF16)
        levelmask = sb("level_masks", [P, 8, P])
        headsel = sb("head_select", [P, HEADS])
        gcol = sb("gain_cols", [P, 7, KT])
        bfcol = sb("forget_bias", [P, 1])
        gbcol = sb("gate_bias", [P, 2])
        bada = sb("b_ada_cols", [P, 48])
        mod = sb("mod_cols", [P, 48])
        scol = sb("scale_cols", [P, 2, KT])
        sinks = sb("sinks", [P, SWA_HEADS])
        wf = sb("w_forget", [P, KT * 72])
        up = sb("gate_up", [GLA_RANK, 2 * P])
        nmax = sb("neg_max", [P, U_END])
        rsum = sb("row_sum", [P, U_END])
        rinv = sb("row_inv", [P, U_END])
        skx = sb("sink_exp", [P, U_END])
        ssq = sb("sum_sq", [P, 40])
        rstd = sb("rstd", [P, 40])
        psq = sb("post_sum_sq", [P, 3, NB, 2])
        prstd = sb("post_rstd", [P, 3, NB])
        ssy = sb("gla_sum_sq", [P, NB, GLA_HEADS])
        rsy = sb("gla_rstd", [P, NB, GLA_HEADS])

        def area(lo, n, **dims):
            v = AREA[:, lo:lo + n]
            return v.rearrange("p (a b) -> p a b", **dims) if dims else v

        fqT, fkT, cqT, ckT = (area(2048 * i, 2048, b=TOK) for i in range(4))
        fv, cv = area(8192, 2048, b=COLS), area(10240, 2048, b=COLS)
        cpos = AREA[:, 12288:12544].bitcast(BF16)
        cneg = AREA[:, 12544:12800].bitcast(BF16)
        cposh = [AREA[:, 12800 + 256 * i:13056 + 256 * i].bitcast(BF16) for i in range(2)]
        cnegh = [AREA[:, 13312 + 256 * i:13568 + 256 * i].bitcast(BF16) for i in range(2)]
        relb = area(13824, 1024, b=COLS)
        MX, memT = area(0, 2048, b=D), area(2048, 2048, b=MEM)
        mkT, mv, mqT = area(4096, 2048, b=MEM), area(6144, 2048, b=D), area(8192, 4096, b=TOK)
        FH = area(0, 16384, b=TOK)
        aqT, akT, av = area(0, 2048, b=TOK), area(2048, 512), area(2560, 512, b=P)
        gqT, gkT = area(3072, 1024, b=TOK), area(4096, 1024, b=TOK)
        gv, gg = area(5120, 2048, b=COLS), area(7168, 2048, b=COLS)
        decay = area(9216, 1024, b=TOK)
        attd = area(10240, 2048, b=COLS)
        atto = area(12288, 3072, b=COLS)
        glrT = AREA[0:GLA_RANK, 15360:15872]
        pqT, subT = area(0, 8192, b=TOK), area(8192, 2048, b=N_KEYS)
        acc, left = area(10240, 2048, b=D), area(12288, 2048, b=N_KEYS)
        prob, probT, biased = (SCR[:, lo:lo + n].rearrange("p (a b) -> p a b", b=COLS)
                               for lo, n in ((0, 1536), (1536, 1024), (2560, 1024)))
        ada = SCR[:, 0:3072].rearrange("p (a b) -> p a b", b=D)
        crow = SCR[:, 3072:4096]
        diag = SCR[:, 0:2048].rearrange("p (a b) -> p a b", b=D)
        fade = SCR[:, 0:2048].rearrange("p (a j t) -> p a j t", a=2, j=2)
        masked = SCR[:, 2048:4096].rearrange("p (a b) -> p a b", b=COLS)
        gq2 = HT[:, 0:4, :].rearrange("p (a j) t -> p a j t", a=2)
        gk2 = HT[:, 4:8, :].rearrange("p (a j) t -> p a j t", a=2)

        def scr(lo, n, dt=None, **dims):
            v = SCR[:, lo:lo + n]
            v = v.bitcast(dt) if dt else v
            return v.rearrange("p (a b) -> p a b", **dims) if dims else v

        topv, topi = scr(0, 256, b=TOPK), scr(256, 256, U32, b=TOPK)
        topf = scr(512, 256, b=TOPK)
        cand, candl, cande = scr(768, 400, b=CAND), scr(1168, 400, b=CAND), scr(1568, 400, b=CAND)
        bestv, bestp = scr(1968, 128, b=TOPK), scr(2096, 128, U32, b=TOPK)
        bestf, eid = scr(2224, 128, b=TOPK), scr(2352, 128, b=TOPK)
        gates, expert = scr(2480, 128, b=TOPK), scr(2608, 128, U32)
        hid, wgt = scr(2736, 128), scr(2864, 128)
        hslot, gsum, ginv = scr(2992, 8), scr(3000, 8), scr(3008, 8)
        idx = scr(3016, 16, U32, b=RING)
        iota = scr(3032, CAND)
        ring = W[:, :, :].rearrange("p a (b c) -> p (a b) c", c=D)
        onehot = W[:, 2, 0:4 * TOPK * CAND].rearrange("p (h k c) -> p h k c", h=4, k=TOPK)

        x_landed, consts_landed, c_landed, rows_landed = map(sem, ("x_landed", "consts_landed", "c_landed", "rows_landed"))
        row2_landed, row3_landed, mem_landed, sub_landed = map(sem, ("row2_landed", "row3_landed", "mem_landed", "sub_landed"))
        w_landed = [sem(f"w_landed{i}") for i in range(W_SLOTS)]
        ada_landed = [sem(f"ada_landed{i}") for i in range(3)]
        rel_landed = [sem(f"rel_landed{i}") for i in range(2)]
        row_landed = [sem(f"row_landed{i}") for i in range(RING)]
        out_landed = sem("out_landed")
        w_used, ada_used, masks_ready, c_ready = map(sem, ("w_used", "ada_used", "masks_ready", "c_ready"))
        ss_ready, xn_ready, tp_done, ht_ready = map(sem, ("ss_ready", "xn_ready", "tp_done", "ht_ready"))
        proj_done, proj_out = sem("proj_done"), sem("proj_out")
        post_ready, x_ready = sem("post_ready"), sem("x_ready")
        f_done, f_log = map(sem, ("f_done", "f_log"))
        diag_ready, gate_done, gate_ready = map(sem, ("diag_ready", "gate_done", "gate_ready"))
        head_ready, sc_done, mx_ready, p_ready = map(sem, ("head_ready", "sc_done", "mx_ready", "p_ready"))
        pt_done, pt_ready, pv_done, y_done = map(sem, ("pt_done", "pt_ready", "pv_done", "y_done"))
        z_done, z_log, decay_ready = map(sem, ("z_done", "z_log", "decay_ready"))
        fade_in, fade_out, gq_ready, gk_ready = map(sem, ("fade_in", "fade_out", "gq_ready", "gk_ready"))
        ga_done, ga_masked, ga_added, ga_out = map(sem, ("ga_done", "ga_masked", "ga_added", "ga_out"))
        go_done, go_sq, go_ss, go_rms, go_ready = map(sem, ("go_done", "go_sq", "go_ss", "go_rms", "go_ready"))
        gg_ready = sem("gg_ready")
        h2_done, h2_ready, sub_done, top_done = map(sem, ("h2_done", "h2_ready", "sub_done", "top_done"))
        gate_in, gate_exp, expert_ready, staged, claimed = map(sem, ("gate_in", "gate_exp", "expert_ready", "staged", "claimed"))
        slot_free, hid_copied, hid_ready, hid_gelu, wgt_ready = map(sem, ("slot_free", "hid_copied", "hid_ready", "hid_gelu", "wgt_ready"))
        fin_x, fin_rms, fin_ready = map(sem, ("fin_x", "fin_rms", "fin_ready"))
        eps_ready = sem("eps_ready")
        act_step, dve_step, pool_step = sem("act_step"), sem("dve_step"), sem("pool_step")

        block = ctx.enter_context(nc.Block())

        chunks = [A["w_in"][i] for i in range(6)] + [A["w_out"][i] for i in range(2)]
        chunks += [A["w_mk"][i] for i in range(2)] + [A["w_mv"][i] for i in range(2)]
        chunks += [A["w_mq"][i] for i in range(2)] + [A["w_mo"][i] for i in range(2)]
        chunks += [A["w_ff1"][i] for i in range(8)] + [A["w_ff2"][i] for i in range(8)]
        chunks += [A["w_in_2"][i] for i in range(5)] + [A["w_out_2"][i] for i in range(2)]
        chunks += [A["w_pq"][i] for i in range(4)]
        assert len(chunks) == C_END

        ends = [4] * 10 + [2] * 2 + [4] * 12 + [0, 0, 0, 4] * 2 + [4, 7, 3, 4, 4] + [4] * 6
        assert len(ends) == C_END and sum(ends) == G_END

        def used(c):
            if ends[c]:
                return proj_done, sum(ends[:c + 1])
            return w_used, ends[:c + 1].count(0)

        @block.sync
        def _(sp):
            for b in range(NB):
                sp.dma_start(X[:, b, :], A["x"][b]).then_inc(x_landed, 16)
            sp.dma_start(gcol[:], A["gain_cols"]).then_inc(consts_landed, 16)
            sp.dma_start(bfcol[:], A["b_fgt"]).then_inc(consts_landed, 16)
            sp.dma_start(wf[:], A["w_fgt"]).then_inc(consts_landed, 16)
            sp.dma_start(bada[:], A["b_ada"]).then_inc(consts_landed, 16)
            sp.dma_start(gbcol[:], A["gla_gate_bias"]).then_inc(consts_landed, 16)
            sp.dma_start(up[:], A["gla_gate_up"]).then_inc(consts_landed, 16)
            sp.dma_start(sinks[:], A["sinks"].partition_broadcast(P)).then_inc(consts_landed, 16)
            for c in range(C_END):
                if c >= W_SLOTS:
                    sp.wait_ge(*used(c - W_SLOTS))
                sp.dma_start(W[:, c % W_SLOTS, :], chunks[c]).then_inc(w_landed[c % W_SLOTS], 16)
                if c == C_IN + 2:
                    for i in range(2):
                        sp.dma_start(GROW[:, i, :], A["gain_rows"][i].partition_broadcast(P)).then_inc(rows_landed, 16)
                    for i in range(4):
                        sp.dma_start(NWROW[:, i * P:(i + 1) * P], A["gla_norm"].partition_broadcast(P)).then_inc(rows_landed, 16)
                if c == C_IN + 5:
                    sp.wait_ge(y_done, U_MEM)
                    sp.dma_start(MX, A["mem"]).then_inc(mem_landed, 16)
                if c == C_MO:
                    sp.wait_ge(x_ready, NB)
                    sp.dma_start(GROW[:, 0, :], A["gain_rows"][2].partition_broadcast(P)).then_inc(row2_landed, 16)
                if c == C_FF1 + 4:
                    sp.wait_ge(x_ready, 2 * NB)
                    sp.dma_start(GROW[:, 1, :], A["gain_rows"][3].partition_broadcast(P)).then_inc(row3_landed, 16)
            sp.wait_ge(proj_out, G_OUT2 + 1)
            sp.dma_start(subT, A["subkeys"]).then_inc(sub_landed, 16)
            for b in range(NB):
                sp.wait_ge(fin_ready, b + 1)
                sp.dma_start(out[b], XN[:, b, :]).then_inc(out_landed, 16)
            sp.wait_ge(out_landed, 16 * NB)

        @block.gpsimd
        def _(pool):
            steps = [0]

            def link(ins):
                steps[0] += 1
                ins.then_inc(pool_step, 1)
                pool.wait_ge(pool_step, steps[0])

            pool.dma_start(crow, A["c"].partition_broadcast(P)).then_inc(c_landed, 16)
            for r in range(3):
                pool.dma_start(ada[:, r, :], A["w_ada"][r]).then_inc(ada_landed[r], 16)

            pool.memset(epsc[:], EPS).then_inc(eps_ready, 1)
            link(pool.memset(ident[:], 0.0))
            link(pool.affine_select(ident[:], ident[:], [[-1, P]], ALU.not_equal, 1.0, 0, 1))
            pool.memset(ones[:], 1.0)
            pool.memset(onesb[:], 1.0)
            pool.memset(levelmask[:], 1.0)
            pool.memset(headsel[:], 0.0)
            link(pool.memset(winb[:], 0.0))
            pool.tensor_copy(identb[:], ident[:])
            link(pool.affine_select(winb[:, P:2 * P], winb[:, P:2 * P], [[-1, P]], ALU.is_ge, NEG, 0, 1))
            link(pool.affine_select(winb[:, 0:P], winb[:, 0:P], [[1, P]], ALU.is_gt, NEG, 0, -1))
            for part in range(3):
                rows = headsel[32 * part:32 * part + HEADS, :]
                link(pool.affine_select(rows, rows, [[-1, HEADS]], ALU.not_equal, 1.0, 0, 1))
            link(pool.tensor_copy(levelmask[:, 0, :], ident[:]))
            for n, m in enumerate(GLA_HALVES[:7]):
                g = levelmask[:, n + 1, :].rearrange("p (g r) -> p g r", r=2 * m)
                G = P // (2 * m)
                link(pool.affine_select(g, g, [[0, G], [1, 2 * m]], ALU.is_ge, 0.0, -m, 0))
                link(pool.affine_select(g, g, [[-2 * m, G], [0, 2 * m]], ALU.is_ge, 0.0, 0, 1))
                link(pool.affine_select(g, g, [[2 * m, G], [0, 2 * m]], ALU.is_ge, 0.0, m - 1, -1))
            pool.memset(cpos, 0.0)
            link(pool.memset(cneg, 0.0))
            pool.sem_inc(masks_ready, 1)

            for r in range(3, 48):
                pool.wait_ge(ada_used, r - 2)
                pool.dma_start(ada[:, r % 3, :], A["w_ada"][r]).then_inc(ada_landed[r % 3], 16)
            for h in range(HEADS):
                if h >= 2:
                    pool.wait_ge(mx_ready, U_CHK + NB * (h - 1))
                pool.dma_start(relb[:, h % 2, :], bass.AP(A["rel"].tensor, h * REL_W, [[1, P], [1, TOK]])).then_inc(rel_landed[h % 2], 16)

            pool.wait_ge(y_done, U_END)
            def keys(l):
                pool.wait_ge(fade_out, l + 1)
                if l >= 2:
                    pool.wait_ge(ga_done, NB * l)
                pool.tensor_tensor(gk2[:, l % 2], gkT, fade[:, l % 2], ALU.mult).then_inc(gk_ready, 1)

            keys(0)
            keys(1)
            pool.wait_ge(ga_out, NB)
            for l in range(7):
                for b in range(NB):
                    n = NB * l + b
                    pool.wait_ge(ga_masked, n + 1)
                    if l > 0:
                        pool.wait_ge(ga_added, n - NB + 1)
                    pool.tensor_tensor(attd[:, b, :], attd[:, b, :], masked[:, n % 4, :], ALU.add).then_inc(ga_added, 1)
                keys(l + 2)
            pool.wait_ge(y_done, U_END)
            pool.wait_ge(go_ready, NB)
            pool.iota(iota, [[1, CAND]], 0, 0, allow_small_or_imprecise_dtypes=True).then_inc(claimed, 1)

            for b in range(NB):
                pool.wait_ge(expert_ready, b + 1)
                for table in range(2):
                    base = TURNS * (2 * b + table)
                    src = A["peer_v"] if table else A["peer_u"]
                    with pool.Fori(0, TURNS // 2) as it:
                        for half in range(2):
                            pool.tensor_copy(idx[:, half, :], expert[:, bass.ds(it * (2 * RING) + half * RING, RING)]).then_inc(staged, 1)
                            pool.wait_ge(staged, it * 2 + (base + half + 1))
                            for k in range(RING):
                                pool.wait_ge(slot_free, it * (2 * RING) + (RING * (base + half) + k + 1))
                                pool.sem_inc(claimed, 1)
                                pool.indirect_dma_start(ring[:, k, :], None, src, bass.IndirectOffsetOnAxis(ap=idx[:, half, k:k + 1], axis=0)).then_inc(row_landed[k], 16)

        @block.scalar
        def _(act):
            steps = [0]

            def link(ins):
                steps[0] += 1
                ins.then_inc(act_step, 1)
                act.wait_ge(act_step, steps[0])

            def root(i, width):
                act.activation(ssq[:, i:i + 1], ssq[:, i:i + 1], ACT.Sqrt, scale=1.0 / width, bias=epsc[:]).then_inc(ss_ready, 1)

            def squares(n):
                for b in range(NB):
                    if n == N_MIX:
                        act.wait_ge(x_landed, 16 * NB)
                    else:
                        done = {N_MEMPRE: 0, N_FF: 1, N_ATT2: 2, N_PEER: 3}[n]
                        act.wait_ge(x_ready, NB * done + b + 1)
                    i = STATS[n] + b
                    link(act.activation(XN[:, b, :], X[:, b, :], ACT.Square, accum_out=ssq[:, i:i + 1]))
                    root(i, D)

            def transposed(n, dst, width, scale, bias=None):
                for k in range(KT):
                    j = KT * n + k
                    act.wait_ge(tp_done, j + 1)
                    src = bank[4 + j % 4][:, 0:width]
                    if scale is None:
                        ins = act.copy(dst[:, k, 0:width], src)
                    elif bias is None:
                        ins = act.activation(dst[:, k, 0:width], src, ACT.Copy, scale=scale[:, k:k + 1])
                    else:
                        ins = act.activation(dst[:, k, 0:width], src, ACT.Identity, scale=scale[:, k:k + 1], bias=bias[:, k:k + 1])
                    ins.then_inc(ht_ready, 1)

            def evac(g, dst, rows=P, width=COLS, scale=1.0, at=None):
                act.wait_ge(proj_done, g + 1)
                src = bank[g % 4 if at is None else at][0:rows, 0:width]
                act.activation(dst, src, ACT.Copy, scale=scale).then_inc(proj_out, 1)

            def evac_post(s, first, banks=None):
                for half in range(2):
                    for b in range(NB):
                        g = first + NB * half + b
                        act.wait_ge(proj_done, g + 1)
                        src = bank[g % 4 if banks is None else banks[NB * half + b]]
                        link(act.copy(XN[:, b, half * COLS:(half + 1) * COLS], src[:]))
                        t = psq[:, s, b, half:half + 1]
                        act.activation(src[:], src[:], ACT.Square, accum_out=t).then_inc(proj_out, 1)
                        if half == 1:
                            act.wait_ge(proj_out, g + 1)
                            link(act.activation(t, t, ACT.Identity, bias=psq[:, s, b, 0:1]))
                            act.activation(t, t, ACT.Sqrt, scale=1.0 / D, bias=epsc[:]).then_inc(post_ready, 1)

            def attention(lo, hi):
                for u in range(lo, hi + 2):
                    if u < hi:
                        kind, h, b, n = unit(u)
                        src = biased[:, u % 2, 0:n] if kind == "chk" else bank[u % 3][:, 0:n]
                        act.wait_ge(mx_ready, u + 1)
                        if u - 3 >= lo:
                            act.wait_ge(pt_done, u - 2)
                        if kind == "swa":
                            act.activation(skx[:, u:u + 1], sinks[:, h:h + 1], ACT.Exp, bias=nmax[:, u:u + 1])
                        act.activation(prob[:, u % 3, 0:n], src, ACT.Exp, bias=nmax[:, u:u + 1],
                                       accum_out=rsum[:, u:u + 1]).then_inc(p_ready, 1)
                    v = u - 2
                    if v >= lo:
                        n = unit(v)[3]
                        act.wait_ge(pt_done, v + 1)
                        if v - 2 >= lo:
                            act.wait_ge(pv_done, v - 1)
                        act.copy(probT[:, v % 2, 0:n], bank[3 + v % 2][:, 0:n]).then_inc(pt_ready, 1)

            act.wait_ge(eps_ready, 1)
            squares(N_MIX)
            act.wait_ge(c_landed, 16)
            act.activation(crow, crow, ACT.Silu).then_inc(c_ready, 1)
            act.wait_ge(consts_landed, 112)
            transposed(N_MIX, HT, TOK, gcol[:, GC_MIX, :])
            for j in range(4):
                evac(G_IN + j, fqT[:, j, :], scale=HD ** -0.5)
            fz, fe = XN[0:72, 0, 0:512], XN[0:72, 0, 512:1024]
            act.wait_ge(f_done, 1)
            link(act.activation(fz, bank[4][0:72, :], ACT.Identity, bias=bfcol[0:72, :]))
            link(act.activation(fe, fz, ACT.Abs))
            link(act.activation(fe, fe, ACT.Exp, scale=-1.0))
            act.activation(fe, fe, ACT.Ln, bias=1.0).then_inc(f_log, 1)
            for j in range(4):
                evac(G_IN + 4 + j, fkT[:, j, :])
            for b in range(NB):
                evac(G_IN + 8 + b, fv[:, b, :])
            for j in range(4):
                evac(G_IN + 12 + j, cqT[:, j, :], scale=HD ** -0.5)
            for j in range(4):
                evac(G_IN + 16 + j, ckT[:, j, :])
            for b in range(NB):
                evac(G_IN + 20 + b, cv[:, b, :])
            for i in range(4):
                act.wait_ge(gate_done, i + 1)
                act.copy(GATE[:, i // 2, (i % 2) * COLS:(i % 2 + 1) * COLS], bank[4 + i][:]).then_inc(gate_ready, 1)
            attention(U_FOX, U_MEM)

            act.wait_ge(y_done, U_MEM)
            for b in range(NB):
                for half in range(2):
                    i = STATS[N_Y] + 2 * b + half
                    link(act.activation(HT[:, 2 * b + half, :], XN[:, b, half * COLS:(half + 1) * COLS], ACT.Square,
                                        accum_out=ssq[:, i:i + 1]))
                    root(i, D // 2)
            act.wait_ge(mem_landed, 16)
            for b in range(MB):
                i = STATS[N_MEM] + b
                link(act.activation(AREA[:, 2048 + D * b:2048 + D * (b + 1)], MX[:, b, :], ACT.Square,
                                    accum_out=ssq[:, i:i + 1]))
                root(i, D)
            transposed(N_Y, HT, TOK, gcol[:, GC_Y, :])
            evac_post(0, G_OUT)
            transposed(N_MEM, memT, MEM, gcol[:, GC_MEMKV, :])
            squares(N_MEMPRE)
            for j in range(8):
                evac(G_MK + j, mkT[:, j, :], width=MEM)
            for n in range(2):
                for b in range(MB):
                    evac(G_MV + MB * n + b, mv[:, b, n * COLS:(n + 1) * COLS])
            transposed(N_MEMPRE, HT, TOK, gcol[:, GC_MEMPRE, :])
            for j in range(8):
                evac(G_MQ + j, mqT[:, j, :], scale=MEM_HD ** -0.5)
            attention(U_MEM, U_SWA)
            transposed(N_MEMY, HT, TOK, None)
            evac_post(1, G_MO)
            squares(N_FF)
            transposed(N_FF, HT, TOK, gcol[:, GC_FF, :])
            for j in range(FF_T):
                act.wait_ge(proj_done, G_FF1 + j + 1)
                link(act.activation(FH[:, j, :], bank[(G_FF1 + j) % 4][:], ACT.Relu))
                act.activation(FH[:, j, :], FH[:, j, :], ACT.Square).then_inc(proj_out, 1)
            evac_post(2, G_FF2, banks=[0, 1, 2, 3, 4, 5, 6, 7])
            squares(N_ATT2)
            transposed(N_ATT2, HT, TOK, scol[:, 0, :], mod[:, 0:8])

            g = G_IN2
            for j in range(4):
                evac(g + j, aqT[:, j, :], scale=HD ** -0.5)
            evac(g + 4, akT)
            for b in range(NB):
                evac(g + 5 + b, av[:, b, :], width=P)
            for j in range(2):
                evac(g + 9 + j, gqT[:, j, :], scale=HD ** -0.5)
            for j in range(2):
                evac(g + 11 + j, gkT[:, j, :])
            evac(g + 13, glrT, rows=GLA_RANK)
            for j in range(2):
                act.wait_ge(z_done, j + 1)
                link(act.activation(decay[:, j, :], bank[4 + j][:], ACT.Identity, bias=gbcol[:, j:j + 1]))
            link(act.activation(fade[:, 0], decay, ACT.Abs))
            link(act.activation(fade[:, 0], fade[:, 0], ACT.Exp, scale=-1.0))
            act.activation(fade[:, 0], fade[:, 0], ACT.Ln, bias=1.0).then_inc(z_log, 1)
            for b in range(NB):
                evac(g + 14 + b, gv[:, b, :])
            for b in range(NB):
                act.wait_ge(proj_done, g + 18 + b + 1)
                act.activation(gg[:, b, :], bank[(g + 18 + b) % 4][:], ACT.Silu).then_inc(proj_out, 1)
            act.wait_ge(decay_ready, 2)
            attention(U_SWA, U_END)
            for l in range(len(GLA_HALVES)):
                act.wait_ge(fade_in, l + 1)
                act.activation(fade[:, l % 2], fade[:, l % 2], ACT.Exp, scale=-1.0 / GLA_TAU).then_inc(fade_out, 1)
            for i in range(6):
                act.wait_ge(ga_done, NB * 8 + i + 1)
                for r in range(2):
                    ins = act.copy(atto[:, i, 2 * P * r:2 * P * (r + 1)], bank[2 * (i % 4) + r][:, 0:2 * P])
                ins.then_inc(ga_out, 1)
            for b in range(NB):
                act.wait_ge(go_done, b + 1)
                act.activation(masked[:, b, :], bank[4 + b][:], ACT.Square).then_inc(go_sq, 1)
            for b in range(NB):
                act.wait_ge(go_ss, b + 1)
                act.activation(ssy[:, b, :], ssy[:, b, :], ACT.Sqrt, scale=1.0 / GLA_DV, bias=epsc[:]).then_inc(go_rms, 1)
            transposed(N_Y2, HT, TOK, None)
            for half in range(2):
                for b in range(NB):
                    evac(G_OUT2 + NB * half + b, XN[:, b, half * COLS:(half + 1) * COLS])
            squares(N_PEER)
            transposed(N_PEER, HT, TOK, scol[:, 1, :], mod[:, 24:32])
            for j in range(16):
                evac(G_WQ + j, pqT[:, j, :])
            for i in range(2 * NB):
                act.wait_ge(h2_done, i + 1)
                act.copy(XN[:, i // 2, (i % 2) * COLS:(i % 2 + 1) * COLS], bank[4 + i % 4][:]).then_inc(h2_ready, 1)
            for b in range(NB):
                act.wait_ge(gate_in, b + 1)
                act.activation(gates, gates, ACT.Exp).then_inc(gate_exp, 1)
                act.wait_ge(hid_ready, b + 1)
                act.activation(hid, hid, ACT.Gelu).then_inc(hid_gelu, 1)
                act.wait_ge(fin_x, b + 1)
                i = 30 + b
                link(act.activation(acc[:, 0, :], X[:, b, :], ACT.Square, accum_out=ssq[:, i:i + 1]))
                act.activation(ssq[:, i:i + 1], ssq[:, i:i + 1], ACT.Sqrt, scale=1.0 / D, bias=epsc[:]).then_inc(fin_rms, 1)

        @block.tensor
        def _(pe):
            def transposes(n, src, blocks):
                for k in range(KT):
                    j = KT * n + k
                    if j >= 4:
                        pe.wait_ge(ht_ready, j - 3)
                    for b in range(blocks):
                        ins = pe.transpose(bank[4 + j % 4][:, b * P:(b + 1) * P], src[:, b, k * P:(k + 1) * P], ident[:])
                    ins.then_inc(tp_done, 1)

            def begin(g, at=None):
                if g >= 4:
                    pe.wait_ge(proj_out, g - 3)
                return bank[g % 4 if at is None else at]

            def arrived(c):
                pe.wait_ge(w_landed[c % W_SLOTS], 16 * (c // W_SLOTS + 1))
                return W[:, c % W_SLOTS, :]

            def tile_T(c, g, x, lo, m, width, wait=None, last=False):
                w, ps = arrived(c), begin(g)
                for k in range(KT):
                    if wait is not None:
                        pe.wait_ge(ht_ready, wait + k + 1)
                    ins = pe.matmul(ps[0:m, 0:width], w[:, k * COLS + lo:k * COLS + lo + m], x[:, k, 0:width],
                                    start=(k == 0), stop=(k == KT - 1))
                ins.then_inc(proj_done, 1)
                return ins

            def tile_tok(c, g, x, b, lo, m, k0=0, at=None, start=True, stop=True):
                w = arrived(c)
                ps = begin(g, at) if start else bank[at]
                for k in range(KT):
                    ins = pe.matmul(ps[:, 0:m], x[:, k0 + k, b * P:(b + 1) * P], w[:, k * COLS + lo:k * COLS + lo + m],
                                    start=(start and k == 0), stop=(stop and k == KT - 1))
                if stop:
                    ins.then_inc(proj_done, 1)
                return ins

            def attention(lo, hi):
                def scores(u):
                    kind, h, b, n = unit(u)
                    ps = bank[u % 3][:, 0:n]
                    if u - 3 >= lo:
                        pe.wait_ge(p_ready, u - 2)
                    q = slice(b * P, (b + 1) * P)
                    if kind == "fox":
                        r = slice((h % 2) * HD, (h % 2 + 1) * HD)
                        pe.wait_ge(head_ready, h + 1)
                        pe.matmul(ps, fqT[r, h // 2, q], fkT[r, h // 2, 0:n], start=True, stop=False)
                        pe.matmul(ps, cposh[h % 2][0:72, q], onesb[0:72, 0:n], start=False, stop=False)
                        pe.matmul(ps, onesb[0:72, 0:P], cnegh[h % 2][0:72, 0:n], start=False, stop=False)
                        ins = pe.matmul(bank[u % 3][:, n - P:n], identb[:], winb[:, P:2 * P], start=False, stop=True)
                    elif kind == "chk":
                        r = slice((h % 2) * HD, (h % 2 + 1) * HD)
                        ins = pe.matmul(ps, cqT[r, h // 2, q], ckT[r, h // 2, 0:n], start=True, stop=True)
                    elif kind == "mem":
                        for c in range(2):
                            ins = pe.matmul(ps, mqT[:, 2 * h + c, q], mkT[:, 2 * h + c, :], start=(c == 0), stop=(c == 1))
                    else:
                        r = slice((h // 4) * HD, (h // 4 + 1) * HD)
                        pe.matmul(ps, aqT[r, h % 4, q], akT[r, (b + 1) * P - n:(b + 1) * P], start=True, stop=False)
                        ins = pe.matmul(ps, identb[:], winb[:, 2 * P - n:2 * P], start=False, stop=True)
                    ins.then_inc(sc_done, 1)

                def turn(u):
                    n = unit(u)[3]
                    pe.wait_ge(p_ready, u + 1)
                    if u - 2 >= lo:
                        pe.wait_ge(pt_ready, u - 1)
                    for j in range(n // P):
                        ins = pe.transpose(bank[3 + u % 2][:, j * P:(j + 1) * P], prob[:, u % 3, j * P:(j + 1) * P], ident[:])
                    ins.then_inc(pt_done, 1)

                def mix(u):
                    kind, h, b, n = unit(u)
                    pe.wait_ge(pt_ready, u + 1)
                    if u - 2 >= lo:
                        pe.wait_ge(y_done, u - 1)
                    for j in range(n // P):
                        if kind == "fox":
                            v = fv[:, j, h * HD:(h + 1) * HD]
                        elif kind == "chk":
                            v = cv[:, j, h * HD:(h + 1) * HD]
                        elif kind == "mem":
                            v = mv[:, j, h * MEM_HD:(h + 1) * MEM_HD]
                        else:
                            v = av[:, b + 1 - n // P + j, (h // 4) * HD:(h // 4 + 1) * HD]
                        ins = pe.matmul(bank[5 + u % 2][:, 0:v.shape[-1]], probT[:, u % 2, j * P:(j + 1) * P], v,
                                        start=(j == 0), stop=(j == n // P - 1))
                    ins.then_inc(pv_done, 1)

                for u in range(lo, hi + 3):
                    if u < hi:
                        scores(u)
                    if lo <= u - 2 < hi:
                        turn(u - 2)
                    if u - 3 >= lo:
                        mix(u - 3)

            pe.wait_ge(masks_ready, 1)
            pe.wait_ge(xn_ready, BLOCKS[N_MIX] + 4)
            transposes(N_MIX, XN, NB)
            for c in range(6):
                for j in range(4):
                    g = G_IN + 4 * c + j
                    if c in (2, 5):
                        tile_tok(C_IN + c, g, HT, j, 0, COLS)
                    else:
                        tile_T(C_IN + c, g, HT, j * P, P, TOK, wait=0 if g == 0 else None)
                if c == 0:
                    pe.wait_ge(consts_landed, 112)
                    for k in range(KT):
                        ins = pe.matmul(bank[4][0:72, :], wf[:, k * 72:(k + 1) * 72], HT[:, k, :], start=(k == 0), stop=(k == KT - 1))
                    ins.then_inc(f_done, 1)
            for i in range(4):
                pe.wait_ge(diag_ready, i // 2 + 1)
                if i == 0:
                    pe.wait_ge(f_log, 1)
                pe.matmul(bank[4 + i][:], ones[:], diag[:, i // 2, (i % 2) * COLS:(i % 2 + 1) * COLS],
                          start=True, stop=True).then_inc(gate_done, 1)
            pe.wait_ge(proj_out, G_OUT)
            pe.wait_ge(gate_ready, 4)
            attention(U_FOX, U_MEM)

            pe.wait_ge(xn_ready, BLOCKS[N_Y] + 4)
            transposes(N_Y, XN, NB)
            for n in range(2):
                for b in range(NB):
                    if n == 0 and b == 0:
                        pe.wait_ge(ht_ready, KT * (N_Y + 1))
                    tile_tok(C_OUT + n, G_OUT + NB * n + b, HT, b, 0, COLS)
            pe.wait_ge(xn_ready, BLOCKS[N_MEM] + MB)
            transposes(N_MEM, MX, MB)
            for n in range(2):
                for j in range(4):
                    tile_T(C_MK + n, G_MK + 4 * n + j, memT, j * P, P, MEM, wait=KT * N_MEM if n + j == 0 else None)
            for n in range(2):
                for b in range(MB):
                    tile_tok(C_MV + n, G_MV + MB * n + b, memT, b, 0, COLS)
            pe.wait_ge(xn_ready, BLOCKS[N_MEMPRE] + 4)
            transposes(N_MEMPRE, XN, NB)
            for n in range(2):
                for j in range(4):
                    tile_T(C_MQ + n, G_MQ + 4 * n + j, HT, j * P, P, TOK, wait=KT * N_MEMPRE if n + j == 0 else None)
            pe.wait_ge(proj_out, G_MO)
            attention(U_MEM, U_SWA)
            pe.wait_ge(y_done, U_SWA)
            transposes(N_MEMY, XN, NB)
            for n in range(2):
                for b in range(NB):
                    if n == 0 and b == 0:
                        pe.wait_ge(ht_ready, KT * (N_MEMY + 1))
                    tile_tok(C_MO + n, G_MO + NB * n + b, HT, b, 0, COLS)
            pe.wait_ge(xn_ready, BLOCKS[N_FF] + 4)
            transposes(N_FF, XN, NB)
            for c in range(8):
                for j in range(4):
                    tile_T(C_FF1 + c, G_FF1 + 4 * c + j, HT, j * P, P, TOK, wait=KT * N_FF if c + j == 0 else None)
            for n in range(2):
                for c in range(4):
                    for b in range(NB):
                        if b == 0:
                            pe.wait_ge(proj_out, G_FF1 + KT * (c + 1))
                        ins = tile_tok(C_FF2 + 4 * n + c, G_FF2 + NB * n + b, FH, b, 0, COLS, k0=KT * c, at=NB * n + b,
                                 start=(c == 0), stop=(c == 3))
                    if c < 3:
                        ins.then_inc(w_used, 1)
            pe.wait_ge(xn_ready, BLOCKS[N_ATT2] + 4)
            transposes(N_ATT2, XN, NB)
            g, c = G_IN2, C_IN2
            for j in range(4):
                tile_T(c, g + j, HT, j * P, P, TOK, wait=KT * N_ATT2 if j == 0 else None)
            tile_T(c + 1, g + 4, HT, 0, P, TOK)
            for b in range(NB):
                tile_tok(c + 1, g + 5 + b, HT, b, P, P)
            for j in range(2):
                tile_T(c + 1, g + 9 + j, HT, (2 + j) * P, P, TOK)
            for j in range(2):
                tile_T(c + 2, g + 11 + j, HT, j * P, P, TOK)
            tile_T(c + 2, g + 13, HT, 2 * P, GLA_RANK, TOK)
            pe.wait_ge(proj_out, g + 14)
            for j in range(2):
                pe.matmul(bank[4 + j][:], up[:, j * P:(j + 1) * P], glrT, start=True, stop=True).then_inc(z_done, 1)
            for n in range(2):
                for b in range(NB):
                    tile_tok(c + 3 + n, g + 14 + NB * n + b, HT, b, 0, COLS)
            pe.wait_ge(proj_out, G_OUT2)
            pe.wait_ge(z_log, 1)
            attention(U_SWA, U_END)

            def pair(k, q, ki, qi, h):
                r = slice((h % 2) * HD, (h % 2 + 1) * HD)
                return k[r, h // 2, ki * P:(ki + 1) * P], q[r, h // 2, qi * P:(qi + 1) * P]

            pe.wait_ge(y_done, U_END)
            for n in range(8 * NB):
                l, b = n // NB, n % NB
                if l == 0:
                    kk, qq = gkT, gqT
                else:
                    kk, qq = gk2[:, (l - 1) % 2], gq2[:, (l - 1) % 2]
                    if b == 0:
                        pe.wait_ge(gq_ready, l)
                        pe.wait_ge(gk_ready, l)
                    pe.wait_ge(ga_out, b + 1) if l == 1 else pe.wait_ge(ga_masked, n - 2 * NB + 1)
                for h in range(GLA_HEADS):
                    k, q = pair(kk, qq, b, b, h)
                    ins = pe.matmul(bank[2 * (n % 4) + h % 2][:, (h // 2) * P:(h // 2 + 1) * P], k, q, start=True, stop=True)
                ins.then_inc(ga_done, 1)
            for i, (ki, qi) in enumerate([(0, 1), (2, 3), (0, 2), (0, 3), (1, 2), (1, 3)]):
                l = 8 if i < 2 else 9
                pe.wait_ge(gq_ready, l)
                pe.wait_ge(gk_ready, l)
                if i < 4:
                    pe.wait_ge(ga_masked, 6 * NB + i + 1)
                else:
                    pe.wait_ge(ga_out, NB + i - 3)
                for h in range(GLA_HEADS):
                    k, q = pair(gk2[:, (l - 1) % 2], gq2[:, (l - 1) % 2], ki, qi, h)
                    ins = pe.matmul(bank[2 * (i % 4) + h % 2][:, (h // 2) * P:(h // 2 + 1) * P], k, q, start=True, stop=True)
                ins.then_inc(ga_done, 1)
            pe.wait_ge(ga_added, 7 * NB)
            pe.wait_ge(ga_out, NB + 6)
            pairs = {(0, 1): 0, (2, 3): 1, (0, 2): 2, (0, 3): 3, (1, 2): 4, (1, 3): 5}
            for b in range(NB):
                for h in range(GLA_HEADS):
                    for j in range(b + 1):
                        a = attd[:, b, :] if j == b else atto[:, pairs[j, b], :]
                        at = 2 * (h % 2) + h // 2
                        ins = pe.matmul(bank[4 + b][:, h * P:(h + 1) * P], a[:, at * P:(at + 1) * P],
                                        gv[:, j, h * GLA_DV:(h + 1) * GLA_DV], start=(j == 0), stop=(j == b))
                ins.then_inc(go_done, 1)
            pe.wait_ge(go_ready, NB)
            transposes(N_Y2, XN, NB)
            for n in range(2):
                for b in range(NB):
                    if n == 0 and b == 0:
                        pe.wait_ge(ht_ready, KT * (N_Y2 + 1))
                    tile_tok(C_OUT2 + n, G_OUT2 + NB * n + b, HT, b, 0, COLS)
            pe.wait_ge(xn_ready, BLOCKS[N_PEER] + 4)
            transposes(N_PEER, XN, NB)
            for n in range(4):
                for j in range(4):
                    tile_T(C_WQ + n, G_WQ + 4 * n + j, HT, j * P, P, TOK, wait=KT * N_PEER if n + j == 0 else None)
            pe.wait_ge(ht_ready, KT * (N_PEER + 1))
            for i in range(2 * NB):
                if i >= 4:
                    pe.wait_ge(h2_ready, i - 3)
                for j in range(4):
                    ins = pe.transpose(bank[4 + i % 4][:, j * P:(j + 1) * P],
                                       HT[:, 4 * (i % 2) + j, (i // 2) * P:(i // 2 + 1) * P], ident[:])
                ins.then_inc(h2_done, 1)
            pe.wait_ge(sub_landed, 16)
            pe.wait_ge(proj_out, G_END)
            pe.wait_ge(h2_ready, 2 * NB)
            for b in range(NB):
                if b >= 2:
                    pe.wait_ge(top_done, b - 1)
                for s in range(16):
                    ins = pe.matmul(bank[4 * (b % 2) + s // 4][:, (s % 4) * P:(s % 4 + 1) * P],
                                    pqT[:, s, b * P:(b + 1) * P], subT[:, s, :], start=True, stop=True)
                ins.then_inc(sub_done, 1)

        @block.vector
        def _(dve):
            steps = [0]

            def link(ins):
                steps[0] += 1
                ins.then_inc(dve_step, 1)
                dve.wait_ge(dve_step, steps[0])

            def normed(n):
                for b in range(NB):
                    i = STATS[n] + b
                    dve.wait_ge(ss_ready, i + 1)
                    link(dve.reciprocal(rstd[:, i:i + 1], ssq[:, i:i + 1]))
                    dve.tensor_scalar(XN[:, b, :], X[:, b, :], rstd[:, i:i + 1], None, ALU.mult).then_inc(xn_ready, 1)

            def add_post(s, row, landed, value):
                dve.wait_ge(landed, value)
                for b in range(NB):
                    dve.wait_ge(post_ready, NB * s + b + 1)
                    link(dve.reciprocal(prstd[:, s, b:b + 1], psq[:, s, b, 1:2]))
                    link(dve.scalar_tensor_tensor(out=XN[:, b, :], in0=XN[:, b, :], scalar=prstd[:, s, b:b + 1],
                                                  in1=GROW[:, row, :], op0=ALU.mult, op1=ALU.mult))
                    dve.tensor_tensor(X[:, b, :], X[:, b, :], XN[:, b, :], ALU.add).then_inc(x_ready, 1)

            def head_decays(h):
                dve.tensor_scalar(cposh[h % 2][0:72, :], cpos[0:72, :], headsel[0:72, h:h + 1], None, ALU.mult)
                dve.tensor_scalar(cnegh[h % 2][0:72, :], cneg[0:72, :], headsel[0:72, h:h + 1], None, ALU.mult).then_inc(head_ready, 1)

            def attention(lo, hi):
                for u in range(lo, hi + 3):
                    if u < hi:
                        kind, h, b, n = unit(u)
                        dve.wait_ge(sc_done, u + 1)
                        src, mx = bank[u % 3][:, 0:n], nmax[:, u:u + 1]
                        if kind == "chk":
                            if b == 0:
                                dve.wait_ge(rel_landed[h % 2], 16 * (h // 2 + 1))
                                link(dve.memset(relb[0:SPAN, h % 2, 0:SPAN], NEG))
                            if u - 2 >= lo:
                                dve.wait_ge(p_ready, u - 1)
                            link(dve.tensor_tensor_reduce(out=biased[:, u % 2, 0:n], in0=src, in1=relb[:, h % 2, n - 1::-1],
                                                          scale=1.0, scalar=-3e38, op0=ALU.add, op1=ALU.max, accum_out=mx))
                            dve.tensor_scalar(mx, mx, -1.0, None, ALU.mult).then_inc(mx_ready, 1)
                        elif kind == "swa":
                            link(dve.tensor_reduce(mx, src, AX.X, ALU.max))
                            dve.tensor_scalar(mx, mx, sinks[:, h:h + 1], -1.0, ALU.max, ALU.mult).then_inc(mx_ready, 1)
                        else:
                            dve.tensor_reduce(mx, src, AX.X, ALU.max, negate=True).then_inc(mx_ready, 1)
                        if kind == "fox" and b == 0 and 1 <= h < HEADS - 1:
                            head_decays(h + 1)
                    v = u - 3
                    if v >= lo:
                        kind, h, b, n = unit(v)
                        dve.wait_ge(p_ready, v + 1)
                        if kind == "swa":
                            link(dve.tensor_tensor(rsum[:, v:v + 1], rsum[:, v:v + 1], skx[:, v:v + 1], ALU.add))
                        link(dve.reciprocal(rinv[:, v:v + 1], rsum[:, v:v + 1]))
                        dve.wait_ge(pv_done, v + 1)
                        w = MEM_HD if kind == "mem" else HD
                        at = h * w + (COLS if kind == "chk" else 0)
                        dve.tensor_scalar(XN[:, b, at:at + w], bank[5 + v % 2][:, 0:w], rinv[:, v:v + 1], None,
                                          ALU.mult).then_inc(y_done, 1)

            normed(N_MIX)
            dve.wait_ge(c_ready, 1)
            for r in range(48):
                dve.wait_ge(ada_landed[r % 3], 16 * (r // 3 + 1))
                dve.tensor_tensor_reduce(out=ada[:, r % 3, :], in0=ada[:, r % 3, :], in1=crow, scale=1.0, scalar=0.0,
                                         op0=ALU.mult, op1=ALU.add, accum_out=mod[:, r:r + 1]).then_inc(ada_used, 1)
            dve.wait_ge(ada_used, 48)
            dve.wait_ge(consts_landed, 112)
            link(dve.tensor_tensor(mod[:], mod[:], bada[:], ALU.add))
            for i, (scale, gc) in enumerate(((8, GC_ATT2), (32, GC_PEER))):
                dve.scalar_tensor_tensor(out=scol[:, i, :], in0=mod[:, scale:scale + KT], scalar=1.0, in1=gcol[:, gc, :],
                                         op0=ALU.add, op1=ALU.mult)
            dve.wait_ge(masks_ready, 1)
            for i, gate in enumerate((16, 40)):
                for k in range(KT):
                    ins = dve.tensor_scalar(diag[:, i, k * P:(k + 1) * P], ident[:], mod[:, gate + k:gate + k + 1], None, ALU.mult)
                ins.then_inc(diag_ready, 1)
            fz, fe = XN[0:72, 0, 0:512], XN[0:72, 0, 512:1024]
            fc, fr = XN[0:72, 1, 0:512], XN[0:72, 1, 512:1024]
            dve.wait_ge(f_log, 1)
            link(dve.scalar_tensor_tensor(out=fz, in0=fz, scalar=0.0, in1=fe, op0=ALU.min, op1=ALU.subtract))
            dve.memset(fe, 1.0)
            link(dve.memset(fr, 1.0))
            link(dve.tensor_tensor_scan(fc, fe, fz, 0.0, ALU.mult, ALU.add))
            for part in range(3):
                rows = slice(32 * part, 32 * part + HEADS)
                low = cposh[0][0:72, :]
                link(dve.tensor_copy(low, fc))
                dve.tensor_copy(cpos[rows, :], low[rows, :])
                dve.tensor_scalar(cneg[rows, :], low[rows, :], -1.0, None, ALU.mult)
                link(dve.tensor_tensor(fr, fc, low, ALU.subtract))
                link(dve.tensor_copy(fc, fr))
            head_decays(0)
            head_decays(1)
            attention(U_FOX, U_MEM)

            for b in range(NB):
                for half in range(2):
                    i = STATS[N_Y] + 2 * b + half
                    y = XN[:, b, half * COLS:(half + 1) * COLS]
                    dve.wait_ge(ss_ready, i + 1)
                    link(dve.reciprocal(rstd[:, i:i + 1], ssq[:, i:i + 1]))
                    ins = dve.tensor_scalar(y, y, rstd[:, i:i + 1], None, ALU.mult)
                ins.then_inc(xn_ready, 1)
            for b in range(MB):
                i = STATS[N_MEM] + b
                dve.wait_ge(ss_ready, i + 1)
                link(dve.reciprocal(rstd[:, i:i + 1], ssq[:, i:i + 1]))
                dve.tensor_scalar(MX[:, b, :], MX[:, b, :], rstd[:, i:i + 1], None, ALU.mult).then_inc(xn_ready, 1)
            add_post(0, 0, rows_landed, 96)
            normed(N_MEMPRE)
            attention(U_MEM, U_SWA)
            add_post(1, 1, rows_landed, 96)
            normed(N_FF)
            add_post(2, 0, row2_landed, 16)
            normed(N_ATT2)
            dve.wait_ge(z_log, 1)
            link(dve.scalar_tensor_tensor(out=decay, in0=decay, scalar=0.0, in1=fade[:, 0], op0=ALU.min, op1=ALU.subtract))
            link(dve.memset(fade[:, 1, 0, :], 1.0))
            for j in range(2):
                dve.tensor_tensor_scan(fade[:, 0, j, :], fade[:, 1, 0, :], decay[:, j, :], 0.0, ALU.mult, ALU.add).then_inc(decay_ready, 1)
            dve.wait_ge(decay_ready, 2)
            link(dve.tensor_copy(decay, fade[:, 0]))
            dve.wait_ge(rows_landed, 96)
            for b in range(NB):
                dve.wait_ge(proj_out, G_IN2 + 18 + b + 1)
                dve.tensor_tensor(gg[:, b, :], gg[:, b, :], NWROW[:], ALU.mult).then_inc(gg_ready, 1)
            attention(U_SWA, U_END)

            def fading(l):
                m = GLA_HALVES[l]
                if l >= 2:
                    dve.wait_ge(gk_ready, l - 1)
                    dve.wait_ge(gq_ready, l - 1)
                src = decay.rearrange("p j t -> p (j t)").rearrange("p (g r) -> p g r", r=2 * m)
                f = fade[:, l % 2].rearrange("p j t -> p (j t)")
                dst = f.rearrange("p (g r) -> p g r", r=2 * m)
                link(dve.tensor_tensor(dst, src, src[:, :, m - 1:m].broadcast_to(src.shape), ALU.subtract))
                dve.scalar_tensor_tensor(out=f, in0=f, scalar=-1.0, in1=f, op0=ALU.mult, op1=ALU.max).then_inc(fade_in, 1)

            def queries(l):
                dve.wait_ge(fade_out, l + 1)
                if l >= 2:
                    dve.wait_ge(ga_done, NB * (l - 1) + NB)
                dve.tensor_tensor(gq2[:, l % 2], gqT, fade[:, l % 2], ALU.mult).then_inc(gq_ready, 1)

            fading(0)
            fading(1)
            for n in range(8 * NB):
                l, b = n // NB, n % NB
                if b == 0:
                    queries(l)
                    if l + 2 < len(GLA_HALVES):
                        fading(l + 2)
                    if l == 7:
                        queries(8)
                dve.wait_ge(ga_done, n + 1)
                mask = levelmask[:, l:l + 1, :].broadcast_to([P, 2, P])
                if l >= 2:
                    dve.wait_ge(ga_added, n - 2 * NB + 1)
                to, ready = (attd[:, b, :], ga_out) if l == 0 else (masked[:, n % 4, :], ga_masked)
                for r in range(2):
                    half = slice(2 * P * r, 2 * P * (r + 1))
                    ins = dve.tensor_tensor(to[:, half].rearrange("p (h t) -> p h t", h=2),
                                            bank[2 * (n % 4) + r][:, 0:2 * P].rearrange("p (h t) -> p h t", h=2), mask, ALU.mult)
                ins.then_inc(ready, 1)
            for b in range(NB):
                dve.wait_ge(go_sq, b + 1)
                dve.tensor_reduce(ssy[:, b, :], masked[:, b, :].rearrange("p (h e) -> p h e", h=GLA_HEADS), AX.X, ALU.add).then_inc(go_ss, 1)
            dve.wait_ge(gg_ready, NB)
            for b in range(NB):
                dve.wait_ge(go_rms, b + 1)
                link(dve.reciprocal(rsy[:, b, :], ssy[:, b, :]))
                for h in range(GLA_HEADS):
                    s = slice(h * GLA_DV, (h + 1) * GLA_DV)
                    ins = dve.scalar_tensor_tensor(out=XN[:, b, COLS + h * GLA_DV:COLS + (h + 1) * GLA_DV], in0=bank[4 + b][:, s],
                                                   scalar=rsy[:, b, h:h + 1], in1=gg[:, b, s], op0=ALU.mult, op1=ALU.mult)
                ins.then_inc(go_ready, 1)
            for b in range(NB):
                dve.wait_ge(proj_out, G_OUT2 + NB + b + 1)
                link(dve.tensor_tensor(XN[:, b, :], XN[:, b, :], GATE[:, 0, :], ALU.mult))
                dve.tensor_tensor(X[:, b, :], X[:, b, :], XN[:, b, :], ALU.add).then_inc(x_ready, 1)
            normed(N_PEER)

            def best(vals, pos, src, rest, n):
                for i in range(n):
                    ins = dve.max(vals[:, i, 0:8], src(i))
                link(ins)
                for i in range(n):
                    dve.max_index(pos[:, i, 0:8], vals[:, i, 0:8], src(i))
                    ins = dve.match_replace(rest[:, i, :], vals[:, i, 0:8], src(i), -3e38)
                link(ins)
                for i in range(n):
                    ins = dve.max(vals[:, i, 8:16], rest[:, i, :])
                link(ins)
                for i in range(n):
                    ins = dve.max_index(pos[:, i, 8:16], vals[:, i, 8:16], rest[:, i, :])

                return ins

            def sums(dst, first, second):
                for a, (n, off) in enumerate(zip(CAND_ROWS, CAND_OFF)):
                    dve.tensor_tensor(dst[:, :, off:off + n], second[:, :, 0:n],
                                      first[:, :, a:a + 1].broadcast_to([P, PEER_HEADS, n]), ALU.add)
                return dve.tensor_tensor(dst[:, :, CAND_TAIL:CAND], first[:, :, TOPK // 2:TOPK],
                                         second[:, :, 0:1].broadcast_to([P, PEER_HEADS, TOPK // 2]), ALU.add)

            halves_v = topv.rearrange("p (h s) k -> p s h k", s=2)
            halves_i = topf.rearrange("p (h s) k -> p s h k", s=2)
            dve.wait_ge(proj_out, G_END)
            dve.wait_ge(claimed, 1)
            for b in range(NB):
                dve.wait_ge(sub_done, b + 1)
                score = lambda i: bank[4 * (b % 2) + i // 4][:, (i % 4) * P:(i % 4 + 1) * P]
                best(topv, topi, score, left, 16).then_inc(top_done, 1)
                dve.wait_ge(top_done, b + 1)
                link(dve.tensor_copy(topf, topi))
                link(dve.tensor_scalar(halves_i[:, 0], halves_i[:, 0], float(N_KEYS), None, ALU.mult))
                sums(cand, halves_v[:, 0], halves_v[:, 1])
                link(sums(cande, halves_i[:, 0], halves_i[:, 1]))
                link(best(bestv, bestp, lambda i: cand[:, i, :], candl, PEER_HEADS))
                link(dve.tensor_copy(bestf, bestp))
                dve.tensor_tensor(gates, bestv, bestv[:, :, 0:1].broadcast_to([P, PEER_HEADS, TOPK]), ALU.subtract).then_inc(gate_in, 1)
                for q in range(2):
                    hs = slice(4 * q, 4 * q + 4)
                    shape = [P, 4, TOPK, CAND]
                    link(dve.tensor_tensor(onehot, iota[:, None, None, :].broadcast_to(shape),
                                           bestf[:, hs, :, None].broadcast_to(shape), ALU.is_equal))
                    link(dve.tensor_tensor(onehot, onehot, cande[:, hs, None, :].broadcast_to(shape), ALU.mult))
                    link(dve.tensor_reduce(eid[:, hs, :], onehot, AX.X, ALU.add))
                ins = dve.tensor_copy(expert.rearrange("p (h k) -> p h k", k=TOPK), eid).then_inc(expert_ready, 1)
                if b == 0:
                    dve.sem_inc(slot_free, RING)
                dve.wait_ge(gate_exp, b + 1)
                link(dve.tensor_reduce(gsum, gates, AX.X, ALU.add))
                link(dve.reciprocal(ginv, gsum))
                link(dve.tensor_tensor(gates, gates, ginv[:, :, None].broadcast_to([P, PEER_HEADS, TOPK]), ALU.mult))
                dve.wait_ge(h2_ready, 2 * NB)
                base = TURNS * 2 * b
                with dve.Fori(0, TURNS) as it:
                    for k in range(RING):
                        dve.wait_ge(row_landed[k], it * 16 + 16 * (base + 1))
                        dve.tensor_tensor_reduce(out=ring[:, k, :], in0=ring[:, k, :], in1=XN[:, b, :], scale=1.0, scalar=0.0,
                                                 op0=ALU.mult, op1=ALU.add, accum_out=hslot[:, k:k + 1]).then_inc(slot_free, 1)
                    dve.wait_ge(slot_free, it * RING + RING * (base + 2))
                    dve.tensor_copy(hid[:, bass.ds(it * RING, RING)], hslot).then_inc(hid_copied, 1)
                    dve.wait_ge(hid_copied, it + (TURNS * b + 1))
                dve.sem_inc(hid_ready, 1)
                dve.memset(acc[:, :, :], 0.0).then_inc(dve_step, 1)
                steps[0] += 1
                dve.wait_ge(dve_step, steps[0])
                dve.wait_ge(hid_gelu, b + 1)
                link(dve.tensor_tensor(wgt, hid, gates.rearrange("p h k -> p (h k)"), ALU.mult))
                base = TURNS * (2 * b + 1)
                with dve.Fori(0, TURNS) as it:
                    for k in range(RING):
                        dve.wait_ge(row_landed[k], it * 16 + 16 * (base + 1))
                        dve.wait_ge(slot_free, it * RING + (RING * (base + 1) + k - 1))
                        dve.scalar_tensor_tensor(out=acc[:, k % 2, :], in0=ring[:, k, :], scalar=wgt[:, bass.ds(it * RING + k, 1)],
                                                 in1=acc[:, k % 2, :], op0=ALU.mult, op1=ALU.add).then_inc(slot_free, 1)
                dve.wait_ge(slot_free, RING * (base + TURNS + 1))
                link(dve.tensor_tensor(acc[:, 1, :], acc[:, 0, :], acc[:, 1, :], ALU.add))
                link(dve.tensor_tensor(acc[:, 1, :], acc[:, 1, :], GATE[:, 1, :], ALU.mult))
                dve.tensor_tensor(X[:, b, :], X[:, b, :], acc[:, 1, :], ALU.add).then_inc(fin_x, 1)
                dve.wait_ge(row3_landed, 16)
                dve.wait_ge(fin_rms, b + 1)
                link(dve.reciprocal(rstd[:, 30 + b:31 + b], ssq[:, 30 + b:31 + b]))
                dve.scalar_tensor_tensor(out=XN[:, b, :], in0=X[:, b, :], scalar=rstd[:, 30 + b:31 + b], in1=GROW[:, 1, :],
                                         op0=ALU.mult, op1=ALU.mult).then_inc(fin_ready, 1)


def pack(w):
    k, n = w.shape
    return w.reshape(k // D, KT, P, n // COLS, COLS).transpose(3, 0, 2, 1, 4).reshape(-1, P, KT * COLS)


def column(v, width=P):
    return v.reshape(-1, width).T


def layouts(i):
    w_in, w_in_2 = i["w_in"][0], i["w_in_2"][0]
    nf = HEADS * HD
    a = {}
    a["x"] = i["x"][0].reshape(NB, P, D)
    a["mem"] = i["mem"][0].reshape(MB, P, D).transpose(1, 0, 2)
    a["c"] = i["c_2"]
    main = np.concatenate([w_in[:, :3 * nf], w_in[:, 3 * nf + HEADS:]], axis=1)
    a["w_in"] = pack(main)
    f = np.zeros((D, 72), np.float32)
    bf = np.zeros((P, 1), np.float32)
    for part in range(3):
        f[:, 32 * part:32 * part + HEADS] = w_in[:, 3 * nf:3 * nf + HEADS]
        bf[32 * part:32 * part + HEADS, 0] = i["b_fgt"][0]
    a["w_fgt"] = f.reshape(KT, P, 72).transpose(1, 0, 2).reshape(P, -1)
    a["b_fgt"] = bf
    for n in ("w_out", "w_mk", "w_mv", "w_mq", "w_mo", "w_ff1", "w_ff2", "w_out_2"):
        a[n] = pack(i[n][0])
    a["w_pq"] = pack(i["peer_wq_2"][0])
    aq = w_in_2[:, :512].reshape(D, 2, 4, HD).transpose(0, 2, 1, 3).reshape(D, 512)
    ak, av, gq, gk, gv, gg, glr = np.split(w_in_2[:, 512:], np.cumsum([128, 128, 256, 256, 512, 512]), axis=1)
    third = np.concatenate([gk, glr, np.zeros((D, 512 - 256 - GLA_RANK), np.float32)], axis=1)
    a["w_in_2"] = pack(np.concatenate([aq, ak, av, gq, third, gv, gg], axis=1))
    rel = np.clip(np.arange(REL_W) - (P - 1), -MAX_REL, MAX_REL) + MAX_REL
    a["rel"] = i["rel_bias"][0][:, rel]
    a["gain_cols"] = np.stack([column(v) for v in (
        i["g_mix_pre"][0], np.concatenate([i["g_fox_out"][0], i["g_chk_out"][0]]), i["g_mem_kv"][0],
        i["g_mem_pre"][0], i["g_ff_pre"][0], i["norm1_w_2"][0], i["norm2_w_2"][0])], axis=1)
    a["gain_rows"] = np.stack([i["g_mix_post"][0], i["g_mem_post"][0], i["g_ff_post"][0], i["final_norm_w_2"]])[:, None, :]
    a["gla_norm"] = i["gla_norm_w_2"]
    a["gla_gate_up"] = i["gla_gate_up_2"][0]
    a["gla_gate_bias"] = column(i["gla_gate_bias_2"][0])
    a["sinks"] = i["attn_sinks_2"]
    a["w_ada"] = i["w_ada_2"][0].T.reshape(48, P, D)
    a["b_ada"] = column(i["b_ada_2"][0])
    a["subkeys"] = i["peer_subkeys_2"][0].reshape(16, N_KEYS, P).transpose(2, 0, 1)
    a["peer_u"] = i["peer_u_2"][0]
    a["peer_v"] = i["peer_v_2"][0]
    return a


def kernel(**inputs):
    import concourse.bacc as bacc
    from concourse.bass_utils import run_bass_kernel_spmd

    nc = bacc.Bacc("TRN2", target_bir_lowering=False, num_devices=1)
    arrays, args = {}, {}
    for name, a in layouts({k: np.asarray(v) for k, v in inputs.items()}).items():
        a = np.ascontiguousarray(a)
        arrays[f"in_{name}"] = a
        args[name] = nc.dram_tensor(f"in_{name}", a.shape, mybir.dt.from_np(a.dtype), kind="ExternalInput").ap()
    out = nc.dram_tensor("out", (NB, P, D), F32, kind="ExternalOutput").ap()
    build(nc, args, out)
    r = run_bass_kernel_spmd(nc, [arrays], core_ids=[0])
    return r.results[0]["out"].reshape(1, TOK, D)
```

```python
from contextlib import ExitStack

import numpy as np

import concourse.bass as bass
from concourse import mybir

F32 = mybir.dt.float32
BF16 = mybir.dt.bfloat16
U32 = mybir.dt.uint32
ALU = mybir.AluOpType
ACT = mybir.ActivationFunctionType
AX = mybir.AxisListType

P = 128
TOK = 512
NB = TOK // P
D = 1024
KT = D // P
COLS = 512
EPS = 1e-6
NEG = -1e30

HEADS = 8
HD = 64
SPAN = 64
MAX_REL = 128
REL_W = TOK + P - 1
MEM = 256
MB = MEM // P
MEM_HEADS = 4
MEM_HD = D // MEM_HEADS
FF_T = 4 * D // P

SWA_HEADS = 8
GLA_HEADS = 4
GLA_DV = 128
GLA_RANK = 16
GLA_TAU = 16.0
GLA_HALVES = [1, 2, 4, 8, 16, 32, 64, 128, 256]

PEER_HEADS = 8
TOPK = 16
SLOTS = PEER_HEADS * TOPK
N_KEYS = 128
CAND_PARTS = [(0, 1, 16), (1, 1, 8), (2, 2, 5), (4, 4, 3), (8, 8, 1)]
CAND = sum(na * nb for _, na, nb in CAND_PARTS)
assert all(any(a0 <= a < a0 + na and TOPK // (a + 1) <= nb for a0, na, nb in CAND_PARTS) for a in range(TOPK))
RING = 8
TURNS = SLOTS // RING
QUARTERS = 4
CHUNKS = 2 * QUARTERS
SHARED = range(1, RING, 2)

W_SLOTS = 3
C_IN, C_OUT, C_MK, C_MV, C_MQ, C_MO, C_FF1, C_FF2, C_IN2, C_OUT2, C_END = (
    0, 6, 8, 10, 12, 14, 16, 24, 32, 37, 39)
G_IN, G_OUT, G_MK, G_MV, G_MQ, G_MO, G_FF1, G_FF2, G_IN2, G_OUT2 = (
    0, 24, 32, 40, 44, 52, 60, 92, 100, 122)
LATE = [("out", 0, i) for i in range(2)] + [("out", 1, i) for i in range(2)]
for _b in range(NB):
    LATE += [("turn", _b, i) for i in range(2)] + [("query", _b, i) for i in range(16)] + [("token", _b, i) for i in range(2)]
    if _b == 0:
        LATE += [("out", b, i) for b in (2, 3) for i in range(2)]


def late(*event):
    return G_OUT2 + LATE.index(event)


(N_MIX, N_Y, N_MEM, N_MEMPRE, N_MEMY, N_FF, N_ATT2, N_Y2, N_PEER) = range(9)
STATS = {N_MIX: 0, N_Y: 4, N_MEM: 12, N_MEMPRE: 14, N_FF: 18, N_ATT2: 22, N_PEER: 26}
BLOCKS = {N_MIX: 0, N_Y: 4, N_MEM: 8, N_MEMPRE: 10, N_FF: 14, N_ATT2: 18, N_PEER: 22}
(GC_MIX, GC_Y, GC_MEMKV, GC_MEMPRE, GC_FF, GC_ATT2, GC_PEER) = range(7)

U_FOX, U_CHK, U_MEM, U_SWA, U_END = 0, 32, 64, 80, 112


def unit(u):
    if u < U_CHK:
        return "fox", u // NB, u % NB, (u % NB + 1) * P
    if u < U_MEM:
        return "chk", (u - U_CHK) // NB, u % NB, (u % NB + 1) * P
    if u < U_SWA:
        return "mem", (u - U_MEM) // NB, u % NB, MEM
    return "swa", (u - U_SWA) // NB, u % NB, (P if u % NB == 0 else 2 * P)


def build(nc, A, out):
    ctx = ExitStack()
    with ctx:
        def sb(name, shape, dt=F32):
            return ctx.enter_context(nc.sbuf_tensor(name, shape, dt))

        def sem(name):
            return ctx.enter_context(nc.semaphore(name))

        bank = [ctx.enter_context(nc.psum_tensor(f"bank{i}", [P, COLS], F32)) for i in range(8)]

        X = sb("x_res", [P, NB, D])
        XN = sb("x_norm", [P, NB, D])
        HT = sb("h_T", [P, KT, TOK])
        W = sb("weights", [P, W_SLOTS, KT * COLS])
        AREA = sb("area", [P, 16384])
        SCR = sb("scratch", [P, 4096])
        GROW = sb("gain_rows", [P, 2, D])
        GATE = sb("gate_rows", [P, 2, D])
        NWROW = sb("gla_norm_row", [P, COLS])
        ident = sb("ident", [P, P])
        identb = sb("ident_bf", [P, P], BF16)
        ones = sb("ones", [P, P])
        epsc = sb("eps_col", [P, 1])
        onesb = sb("ones_bf", [P, COLS], BF16)
        winb = sb("window_mask", [P, 2 * P], BF16)
        levelmask = sb("level_masks", [P, 8, P])
        headsel = sb("head_select", [P, HEADS])
        gcol = sb("gain_cols", [P, 7, KT])
        bfcol = sb("forget_bias", [P, 1])
        gbcol = sb("gate_bias", [P, 2])
        bada = sb("b_ada_cols", [P, 48])
        mod = sb("mod_cols", [P, 48])
        scol = sb("scale_cols", [P, 2, KT])
        sinks = sb("sinks", [P, SWA_HEADS])
        wf = sb("w_forget", [P, KT * 72])
        up = sb("gate_up", [GLA_RANK, 2 * P])
        nmax = sb("neg_max", [P, U_END])
        rsum = sb("row_sum", [P, U_END])
        rinv = sb("row_inv", [P, U_END])
        skx = sb("sink_exp", [P, U_END])
        ssq = sb("sum_sq", [P, 40])
        rstd = sb("rstd", [P, 40])
        psq = sb("post_sum_sq", [P, 3, NB, 2])
        prstd = sb("post_rstd", [P, 3, NB])
        ssy = sb("gla_sum_sq", [P, NB, GLA_HEADS])
        rsy = sb("gla_rstd", [P, NB, GLA_HEADS])

        def area(lo, n, **dims):
            v = AREA[:, lo:lo + n]
            return v.rearrange("p (a b) -> p a b", **dims) if dims else v

        fqT, fkT, cqT, ckT = (area(2048 * i, 2048, b=TOK) for i in range(4))
        fv, cv = area(8192, 2048, b=COLS), area(10240, 2048, b=COLS)
        cpos = AREA[:, 12288:12544].bitcast(BF16)
        cneg = AREA[:, 12544:12800].bitcast(BF16)
        cposh = [AREA[:, 12800 + 256 * i:13056 + 256 * i].bitcast(BF16) for i in range(2)]
        cnegh = [AREA[:, 13312 + 256 * i:13568 + 256 * i].bitcast(BF16) for i in range(2)]
        relb = area(13824, 1024, b=COLS)
        MX, memT = area(0, 2048, b=D), area(2048, 2048, b=MEM)
        mkT, mv, mqT = area(4096, 2048, b=MEM), area(6144, 2048, b=D), area(8192, 4096, b=TOK)
        FH = area(0, 16384, b=TOK)
        aqT, akT, av = area(0, 2048, b=TOK), area(2048, 512), area(2560, 512, b=P)
        gqT, gkT = area(3072, 1024, b=TOK), area(4096, 1024, b=TOK)
        gv, gg = area(5120, 2048, b=COLS), area(7168, 2048, b=COLS)
        decay = area(9216, 1024, b=TOK)
        attd = area(10240, 2048, b=COLS)
        atto = area(12288, 3072, b=COLS)
        glrT = AREA[0:GLA_RANK, 15360:15872]
        wq = area(0, 16384, b=KT * COLS)
        pqT = W[:, 0, 0:2048].rearrange("p (a b) -> p a b", b=P)
        subT = W[:, 0, 2048:4096].rearrange("p (a b) -> p a b", b=N_KEYS)
        left = NWROW[:].rearrange("p (a b) -> p a b", b=N_KEYS)
        prob, probT, biased = (SCR[:, lo:lo + n].rearrange("p (a b) -> p a b", b=COLS)
                               for lo, n in ((0, 1536), (1536, 1024), (2560, 1024)))
        ada = SCR[:, 0:3072].rearrange("p (a b) -> p a b", b=D)
        crow = SCR[:, 3072:4096]
        diag = SCR[:, 0:2048].rearrange("p (a b) -> p a b", b=D)
        fade = SCR[:, 0:2048].rearrange("p (a j t) -> p a j t", a=2, j=2)
        masked = SCR[:, 2048:4096].rearrange("p (a b) -> p a b", b=COLS)
        gq2 = HT[:, 0:4, :].rearrange("p (a j) t -> p a j t", a=2)
        gk2 = HT[:, 4:8, :].rearrange("p (a j) t -> p a j t", a=2)

        def scr(lo, n, dt=None, **dims):
            v = SCR[:, lo:lo + n]
            v = v.bitcast(dt) if dt else v
            return v.rearrange("p (a b) -> p a b", **dims) if dims else v

        topv, topi = scr(0, 256, b=TOPK), scr(256, 256, U32, b=TOPK)
        topf, bestv = scr(512, 64, b=TOPK), scr(576, 128, b=TOPK)
        bestp, bestf, eid = scr(704, 32, U32, b=TOPK), scr(736, 32, b=TOPK), scr(768, 32, b=TOPK)
        gates, expert = scr(800, 128, b=TOPK), scr(928, 256, U32, b=SLOTS)
        hid, wgt = scr(1184, 128), scr(1312, 128)
        hslot, gsum, ginv = scr(1440, 8), scr(1448, 8), scr(1456, 8)
        idx = scr(1464, 16, U32, b=RING)
        iota = scr(1480, CAND)
        cand, candl, cande = (scr(1536 + 2 * CAND * i, 2 * CAND, b=CAND) for i in range(3))
        ring = W[:, 1:3, :].rearrange("p a (b c) -> p (a b) c", c=D)
        onehot = [t[:, 0:TOPK * CAND].rearrange("p (k c) -> p k c", c=CAND)
                  for t in (levelmask[:].rearrange("p a b -> p (a b)"), SCR[:, 2048:3072])]
        acc = SCR[:, 3072:4096]
        wdiag = GROW[:, 0, 0:P * len(SHARED)].rearrange("p (a b) -> p a b", b=P)

        x_landed, consts_landed, c_landed, rows_landed = map(sem, ("x_landed", "consts_landed", "c_landed", "rows_landed"))
        row2_landed, row3_landed, mem_landed, sub_landed = map(sem, ("row2_landed", "row3_landed", "mem_landed", "sub_landed"))
        w_landed = [sem(f"w_landed{i}") for i in range(W_SLOTS)]
        ada_landed = [sem(f"ada_landed{i}") for i in range(3)]
        rel_landed = [sem(f"rel_landed{i}") for i in range(2)]
        row_landed = [sem(f"row_landed{i}") for i in range(RING)]
        out_landed = sem("out_landed")
        w_used, ada_used, masks_ready, c_ready = map(sem, ("w_used", "ada_used", "masks_ready", "c_ready"))
        ss_ready, xn_ready, tp_done, ht_ready = map(sem, ("ss_ready", "xn_ready", "tp_done", "ht_ready"))
        proj_done, proj_out = sem("proj_done"), sem("proj_out")
        post_ready, x_ready = sem("post_ready"), sem("x_ready")
        f_done, f_log = map(sem, ("f_done", "f_log"))
        diag_ready, gate_done, gate_ready = map(sem, ("diag_ready", "gate_done", "gate_ready"))
        head_ready, sc_done, mx_ready, p_ready = map(sem, ("head_ready", "sc_done", "mx_ready", "p_ready"))
        pt_done, pt_ready, pv_done, y_done = map(sem, ("pt_done", "pt_ready", "pv_done", "y_done"))
        z_done, z_log, decay_ready = map(sem, ("z_done", "z_log", "decay_ready"))
        fade_in, fade_out, gq_ready, gk_ready = map(sem, ("fade_in", "fade_out", "gq_ready", "gk_ready"))
        ga_done, ga_masked, ga_added, ga_out = map(sem, ("ga_done", "ga_masked", "ga_added", "ga_out"))
        go_done, go_sq, go_ss, go_rms, go_ready = map(sem, ("go_done", "go_sq", "go_ss", "go_rms", "go_ready"))
        gg_ready = sem("gg_ready")
        wq_landed, sub_done, top_done = map(sem, ("wq_landed", "sub_done", "top_done"))
        gate_in, gate_exp, expert_ready, staged, claimed = map(sem, ("gate_in", "gate_exp", "expert_ready", "staged", "claimed"))
        slot_free = [sem(f"slot_free{i}") for i in range(RING)]
        hid_copied, hid_ready, hid_gelu, wgt_ready = map(sem, ("hid_copied", "hid_ready", "hid_gelu", "wgt_ready"))
        wdiag_ready = sem("wdiag_ready")
        fin_x, fin_rms, fin_ready = map(sem, ("fin_x", "fin_rms", "fin_ready"))
        eps_ready = sem("eps_ready")
        act_step, dve_step, pool_step = sem("act_step"), sem("dve_step"), sem("pool_step")

        block = ctx.enter_context(nc.Block())

        chunks = [A["w_in"][i] for i in range(6)] + [A["w_out"][i] for i in range(2)]
        chunks += [A["w_mk"][i] for i in range(2)] + [A["w_mv"][i] for i in range(2)]
        chunks += [A["w_mq"][i] for i in range(2)] + [A["w_mo"][i] for i in range(2)]
        chunks += [A["w_ff1"][i] for i in range(8)] + [A["w_ff2"][i] for i in range(8)]
        chunks += [A["w_in_2"][i] for i in range(5)] + [A["w_out_2"][i] for i in range(2)]
        assert len(chunks) == C_END

        ends = [4] * 10 + [2] * 2 + [4] * 12 + [0, 0, 0, 4] * 2 + [4, 7, 3, 4, 4] + [4] * 2
        assert len(ends) == C_END and sum(ends[:C_OUT2]) == G_OUT2

        def used(c):
            if ends[c]:
                return proj_done, sum(ends[:c + 1])
            return w_used, ends[:c + 1].count(0)

        @block.sync
        def _(sp):
            for b in range(NB):
                sp.dma_start(X[:, b, :], A["x"][b]).then_inc(x_landed, 16)
            sp.dma_start(gcol[:], A["gain_cols"]).then_inc(consts_landed, 16)
            sp.dma_start(bfcol[:], A["b_fgt"]).then_inc(consts_landed, 16)
            sp.dma_start(wf[:], A["w_fgt"]).then_inc(consts_landed, 16)
            sp.dma_start(bada[:], A["b_ada"]).then_inc(consts_landed, 16)
            sp.dma_start(gbcol[:], A["gla_gate_bias"]).then_inc(consts_landed, 16)
            sp.dma_start(up[:], A["gla_gate_up"]).then_inc(consts_landed, 16)
            sp.dma_start(sinks[:], A["sinks"].partition_broadcast(P)).then_inc(consts_landed, 16)
            for c in range(C_END):
                if c >= W_SLOTS:
                    sp.wait_ge(*used(c - W_SLOTS))
                sp.dma_start(W[:, c % W_SLOTS, :], chunks[c]).then_inc(w_landed[c % W_SLOTS], 16)
                if c == C_IN + 2:
                    for i in range(2):
                        sp.dma_start(GROW[:, i, :], A["gain_rows"][i].partition_broadcast(P)).then_inc(rows_landed, 16)
                    for i in range(4):
                        sp.dma_start(NWROW[:, i * P:(i + 1) * P], A["gla_norm"].partition_broadcast(P)).then_inc(rows_landed, 16)
                if c == C_IN + 5:
                    sp.wait_ge(y_done, U_MEM)
                    sp.dma_start(MX, A["mem"]).then_inc(mem_landed, 16)
                if c == C_MO:
                    sp.wait_ge(x_ready, NB)
                    sp.dma_start(GROW[:, 0, :], A["gain_rows"][2].partition_broadcast(P)).then_inc(row2_landed, 16)
                if c == C_FF1 + 4:
                    sp.wait_ge(x_ready, 2 * NB)
                    sp.dma_start(GROW[:, 1, :], A["gain_rows"][3].partition_broadcast(P)).then_inc(row3_landed, 16)
            sp.wait_ge(proj_done, G_OUT2)
            sp.dma_start(subT, A["subkeys"]).then_inc(sub_landed, 16)
            sp.wait_ge(go_ready, NB)
            for i in range(4):
                sp.dma_start(wq[:, i, :], A["w_pq"][i]).then_inc(wq_landed, 16)
            for b in range(NB):
                sp.wait_ge(fin_ready, b + 1)
                sp.dma_start(out[b], XN[:, b, :]).then_inc(out_landed, 16)
            sp.wait_ge(out_landed, 16 * NB)

        @block.gpsimd
        def _(pool):
            steps = [0]

            def link(ins):
                steps[0] += 1
                ins.then_inc(pool_step, 1)
                pool.wait_ge(pool_step, steps[0])

            pool.dma_start(crow, A["c"].partition_broadcast(P)).then_inc(c_landed, 16)
            for r in range(3):
                pool.dma_start(ada[:, r, :], A["w_ada"][r]).then_inc(ada_landed[r], 16)

            pool.memset(epsc[:], EPS).then_inc(eps_ready, 1)
            link(pool.memset(ident[:], 0.0))
            link(pool.affine_select(ident[:], ident[:], [[-1, P]], ALU.not_equal, 1.0, 0, 1))
            pool.memset(ones[:], 1.0)
            pool.memset(onesb[:], 1.0)
            pool.memset(levelmask[:], 1.0)
            pool.memset(headsel[:], 0.0)
            link(pool.memset(winb[:], 0.0))
            pool.tensor_copy(identb[:], ident[:])
            link(pool.affine_select(winb[:, P:2 * P], winb[:, P:2 * P], [[-1, P]], ALU.is_ge, NEG, 0, 1))
            link(pool.affine_select(winb[:, 0:P], winb[:, 0:P], [[1, P]], ALU.is_gt, NEG, 0, -1))
            for part in range(3):
                rows = headsel[32 * part:32 * part + HEADS, :]
                link(pool.affine_select(rows, rows, [[-1, HEADS]], ALU.not_equal, 1.0, 0, 1))
            link(pool.tensor_copy(levelmask[:, 0, :], ident[:]))
            for n, m in enumerate(GLA_HALVES[:7]):
                g = levelmask[:, n + 1, :].rearrange("p (g r) -> p g r", r=2 * m)
                G = P // (2 * m)
                link(pool.affine_select(g, g, [[0, G], [1, 2 * m]], ALU.is_ge, 0.0, -m, 0))
                link(pool.affine_select(g, g, [[-2 * m, G], [0, 2 * m]], ALU.is_ge, 0.0, 0, 1))
                link(pool.affine_select(g, g, [[2 * m, G], [0, 2 * m]], ALU.is_ge, 0.0, m - 1, -1))
            pool.memset(cpos, 0.0)
            link(pool.memset(cneg, 0.0))
            pool.sem_inc(masks_ready, 1)

            for r in range(3, 48):
                pool.wait_ge(ada_used, r - 2)
                pool.dma_start(ada[:, r % 3, :], A["w_ada"][r]).then_inc(ada_landed[r % 3], 16)
            for h in range(HEADS):
                if h >= 2:
                    pool.wait_ge(mx_ready, U_CHK + NB * (h - 1))
                pool.dma_start(relb[:, h % 2, :], bass.AP(A["rel"].tensor, h * REL_W, [[1, P], [1, TOK]])).then_inc(rel_landed[h % 2], 16)

            pool.wait_ge(y_done, U_END)
            def keys(l):
                pool.wait_ge(fade_out, l + 1)
                if l >= 2:
                    pool.wait_ge(ga_done, NB * l)
                pool.tensor_tensor(gk2[:, l % 2], gkT, fade[:, l % 2], ALU.mult).then_inc(gk_ready, 1)

            keys(0)
            keys(1)
            pool.wait_ge(ga_out, NB)
            for l in range(7):
                for b in range(NB):
                    n = NB * l + b
                    pool.wait_ge(ga_masked, n + 1)
                    if l > 0:
                        pool.wait_ge(ga_added, n - NB + 1)
                    pool.tensor_tensor(attd[:, b, :], attd[:, b, :], masked[:, n % 4, :], ALU.add).then_inc(ga_added, 1)
                keys(l + 2)
            pool.wait_ge(y_done, U_END)
            pool.wait_ge(go_ready, NB)
            pool.iota(iota, [[1, CAND]], 0, 0, allow_small_or_imprecise_dtypes=True).then_inc(claimed, 1)

            pool.wait_ge(proj_done, late("out", NB - 1, 1) + 1)
            for b in range(NB):
                for table in range(2):
                    base = TURNS * (2 * b + table)
                    src = A["peer_v"] if table else A["peer_u"]
                    with pool.Fori(0, QUARTERS) as it:
                        pool.wait_ge(expert_ready, it + (QUARTERS * b + 1))
                        for turn in range(4):
                            pool.tensor_copy(idx[:, turn % 2, :], expert[:, b % 2, bass.ds(it * (4 * RING) + turn * RING, RING)]).then_inc(staged, 1)
                            pool.wait_ge(staged, it * 4 + (base + turn + 1))
                            for k in range(RING):
                                pool.wait_ge(slot_free[k], it * 4 + (base + turn + 1))
                                pool.sem_inc(claimed, 1)
                                pool.indirect_dma_start(ring[:, k, :], None, src, bass.IndirectOffsetOnAxis(ap=idx[:, turn % 2, k:k + 1], axis=0)).then_inc(row_landed[k], 16)

        @block.scalar
        def _(act):
            steps = [0]

            def link(ins):
                steps[0] += 1
                ins.then_inc(act_step, 1)
                act.wait_ge(act_step, steps[0])

            def root(i, width):
                act.activation(ssq[:, i:i + 1], ssq[:, i:i + 1], ACT.Sqrt, scale=1.0 / width, bias=epsc[:]).then_inc(ss_ready, 1)

            def squares(n, blocks=None):
                for b in range(NB) if blocks is None else blocks:
                    if n == N_MIX:
                        act.wait_ge(x_landed, 16 * NB)
                    else:
                        done = {N_MEMPRE: 0, N_FF: 1, N_ATT2: 2, N_PEER: 3}[n]
                        act.wait_ge(x_ready, NB * done + b + 1)
                    i = STATS[n] + b
                    link(act.activation(XN[:, b, :], X[:, b, :], ACT.Square, accum_out=ssq[:, i:i + 1]))
                    root(i, D)

            def transposed(n, dst, width, scale, bias=None):
                for k in range(KT):
                    j = KT * n + k
                    act.wait_ge(tp_done, j + 1)
                    src = bank[4 + j % 4][:, 0:width]
                    if scale is None:
                        ins = act.copy(dst[:, k, 0:width], src)
                    elif bias is None:
                        ins = act.activation(dst[:, k, 0:width], src, ACT.Copy, scale=scale[:, k:k + 1])
                    else:
                        ins = act.activation(dst[:, k, 0:width], src, ACT.Identity, scale=scale[:, k:k + 1], bias=bias[:, k:k + 1])
                    ins.then_inc(ht_ready, 1)

            def evac(g, dst, rows=P, width=COLS, scale=1.0, at=None):
                act.wait_ge(proj_done, g + 1)
                src = bank[g % 4 if at is None else at][0:rows, 0:width]
                act.activation(dst, src, ACT.Copy, scale=scale).then_inc(proj_out, 1)

            def evac_post(s, first, banks=None):
                for half in range(2):
                    for b in range(NB):
                        g = first + NB * half + b
                        act.wait_ge(proj_done, g + 1)
                        src = bank[g % 4 if banks is None else banks[NB * half + b]]
                        link(act.copy(XN[:, b, half * COLS:(half + 1) * COLS], src[:]))
                        t = psq[:, s, b, half:half + 1]
                        act.activation(src[:], src[:], ACT.Square, accum_out=t).then_inc(proj_out, 1)
                        if half == 1:
                            act.wait_ge(proj_out, g + 1)
                            link(act.activation(t, t, ACT.Identity, bias=psq[:, s, b, 0:1]))
                            act.activation(t, t, ACT.Sqrt, scale=1.0 / D, bias=epsc[:]).then_inc(post_ready, 1)

            def attention(lo, hi):
                for u in range(lo, hi + 2):
                    if u < hi:
                        kind, h, b, n = unit(u)
                        src = biased[:, u % 2, 0:n] if kind == "chk" else bank[u % 3][:, 0:n]
                        act.wait_ge(mx_ready, u + 1)
                        if u - 3 >= lo:
                            act.wait_ge(pt_done, u - 2)
                        if kind == "swa":
                            act.activation(skx[:, u:u + 1], sinks[:, h:h + 1], ACT.Exp, bias=nmax[:, u:u + 1])
                        act.activation(prob[:, u % 3, 0:n], src, ACT.Exp, bias=nmax[:, u:u + 1],
                                       accum_out=rsum[:, u:u + 1]).then_inc(p_ready, 1)
                    v = u - 2
                    if v >= lo:
                        n = unit(v)[3]
                        act.wait_ge(pt_done, v + 1)
                        if v - 2 >= lo:
                            act.wait_ge(pv_done, v - 1)
                        act.copy(probT[:, v % 2, 0:n], bank[3 + v % 2][:, 0:n]).then_inc(pt_ready, 1)

            act.wait_ge(eps_ready, 1)
            squares(N_MIX)
            act.wait_ge(c_landed, 16)
            act.activation(crow, crow, ACT.Silu).then_inc(c_ready, 1)
            act.wait_ge(consts_landed, 112)
            transposed(N_MIX, HT, TOK, gcol[:, GC_MIX, :])
            for j in range(4):
                evac(G_IN + j, fqT[:, j, :], scale=HD ** -0.5)
            fz, fe = XN[0:72, 0, 0:512], XN[0:72, 0, 512:1024]
            act.wait_ge(f_done, 1)
            link(act.activation(fz, bank[4][0:72, :], ACT.Identity, bias=bfcol[0:72, :]))
            link(act.activation(fe, fz, ACT.Abs))
            link(act.activation(fe, fe, ACT.Exp, scale=-1.0))
            act.activation(fe, fe, ACT.Ln, bias=1.0).then_inc(f_log, 1)
            for j in range(4):
                evac(G_IN + 4 + j, fkT[:, j, :])
            for b in range(NB):
                evac(G_IN + 8 + b, fv[:, b, :])
            for j in range(4):
                evac(G_IN + 12 + j, cqT[:, j, :], scale=HD ** -0.5)
            for j in range(4):
                evac(G_IN + 16 + j, ckT[:, j, :])
            for b in range(NB):
                evac(G_IN + 20 + b, cv[:, b, :])
            for i in range(4):
                act.wait_ge(gate_done, i + 1)
                act.copy(GATE[:, i // 2, (i % 2) * COLS:(i % 2 + 1) * COLS], bank[4 + i][:]).then_inc(gate_ready, 1)
            attention(U_FOX, U_MEM)

            act.wait_ge(y_done, U_MEM)
            for b in range(NB):
                for half in range(2):
                    i = STATS[N_Y] + 2 * b + half
                    link(act.activation(HT[:, 2 * b + half, :], XN[:, b, half * COLS:(half + 1) * COLS], ACT.Square,
                                        accum_out=ssq[:, i:i + 1]))
                    root(i, D // 2)
            act.wait_ge(mem_landed, 16)
            for b in range(MB):
                i = STATS[N_MEM] + b
                link(act.activation(AREA[:, 2048 + D * b:2048 + D * (b + 1)], MX[:, b, :], ACT.Square,
                                    accum_out=ssq[:, i:i + 1]))
                root(i, D)
            transposed(N_Y, HT, TOK, gcol[:, GC_Y, :])
            evac_post(0, G_OUT)
            transposed(N_MEM, memT, MEM, gcol[:, GC_MEMKV, :])
            squares(N_MEMPRE)
            for j in range(8):
                evac(G_MK + j, mkT[:, j, :], width=MEM)
            for n in range(2):
                for b in range(MB):
                    evac(G_MV + MB * n + b, mv[:, b, n * COLS:(n + 1) * COLS])
            transposed(N_MEMPRE, HT, TOK, gcol[:, GC_MEMPRE, :])
            for j in range(8):
                evac(G_MQ + j, mqT[:, j, :], scale=MEM_HD ** -0.5)
            attention(U_MEM, U_SWA)
            transposed(N_MEMY, HT, TOK, None)
            evac_post(1, G_MO)
            squares(N_FF)
            transposed(N_FF, HT, TOK, gcol[:, GC_FF, :])
            for j in range(FF_T):
                act.wait_ge(proj_done, G_FF1 + j + 1)
                link(act.activation(FH[:, j, :], bank[(G_FF1 + j) % 4][:], ACT.Relu))
                act.activation(FH[:, j, :], FH[:, j, :], ACT.Square).then_inc(proj_out, 1)
            evac_post(2, G_FF2, banks=[0, 1, 2, 3, 4, 5, 6, 7])
            squares(N_ATT2)
            transposed(N_ATT2, HT, TOK, scol[:, 0, :], mod[:, 0:8])

            g = G_IN2
            for j in range(4):
                evac(g + j, aqT[:, j, :], scale=HD ** -0.5)
            evac(g + 4, akT)
            for b in range(NB):
                evac(g + 5 + b, av[:, b, :], width=P)
            for j in range(2):
                evac(g + 9 + j, gqT[:, j, :], scale=HD ** -0.5)
            for j in range(2):
                evac(g + 11 + j, gkT[:, j, :])
            evac(g + 13, glrT, rows=GLA_RANK)
            for j in range(2):
                act.wait_ge(z_done, j + 1)
                link(act.activation(decay[:, j, :], bank[4 + j][:], ACT.Identity, bias=gbcol[:, j:j + 1]))
            link(act.activation(fade[:, 0], decay, ACT.Abs))
            link(act.activation(fade[:, 0], fade[:, 0], ACT.Exp, scale=-1.0))
            act.activation(fade[:, 0], fade[:, 0], ACT.Ln, bias=1.0).then_inc(z_log, 1)
            for b in range(NB):
                evac(g + 14 + b, gv[:, b, :])
            for b in range(NB):
                act.wait_ge(proj_done, g + 18 + b + 1)
                act.activation(gg[:, b, :], bank[(g + 18 + b) % 4][:], ACT.Silu).then_inc(proj_out, 1)
            act.wait_ge(decay_ready, 2)
            attention(U_SWA, U_END)
            for l in range(len(GLA_HALVES)):
                act.wait_ge(fade_in, l + 1)
                act.activation(fade[:, l % 2], fade[:, l % 2], ACT.Exp, scale=-1.0 / GLA_TAU).then_inc(fade_out, 1)
            for i in range(6):
                act.wait_ge(ga_done, NB * 8 + i + 1)
                for r in range(2):
                    ins = act.copy(atto[:, i, 2 * P * r:2 * P * (r + 1)], bank[2 * (i % 4) + r][:, 0:2 * P])
                ins.then_inc(ga_out, 1)
            for b in range(NB):
                act.wait_ge(go_done, b + 1)
                act.activation(masked[:, b, :], bank[4 + b][:], ACT.Square).then_inc(go_sq, 1)
            for b in range(NB):
                act.wait_ge(go_ss, b + 1)
                act.activation(ssy[:, b, :], ssy[:, b, :], ACT.Sqrt, scale=1.0 / GLA_DV, bias=epsc[:]).then_inc(go_rms, 1)
            transposed(N_Y2, HT, TOK, None)
            def evac_late(kind, b):
                for i in range(16 if kind == "query" else 2):
                    g = late(kind, b, i)
                    half = slice(i * COLS, (i + 1) * COLS)
                    if kind in ("out", "token"):
                        evac(g, XN[:, b, half])
                    elif kind == "query":
                        if b > 0 and i % 4 == 0:
                            act.wait_ge(sub_done, QUARTERS * (b - 1) + i // 4 + 1)
                        evac(g, pqT[:, i, :], width=P)
                    else:
                        act.wait_ge(proj_done, g + 1)
                        for j in range(4):
                            k = 4 * i + j
                            ins = act.activation(HT[:, k, b * P:(b + 1) * P], bank[g % 4][:, j * P:(j + 1) * P], ACT.Identity,
                                                 scale=scol[:, 1, k:k + 1], bias=mod[:, 24 + k:25 + k])
                        ins.then_inc(proj_out, 1)

            def evac_queries(b):
                evac_late("turn", b)
                evac_late("query", b)
                evac_late("token", b)

            def exponentials(b):
                act.wait_ge(gate_in, b + 1)
                act.activation(gates, gates, ACT.Exp).then_inc(gate_exp, 1)

            def gelus(b):
                act.wait_ge(hid_ready, b + 1)
                act.activation(hid, hid, ACT.Gelu).then_inc(hid_gelu, 1)

            def final_squares(b):
                act.wait_ge(fin_x, b + 1)
                i = 30 + b
                link(act.activation(XN[:, b, :], X[:, b, :], ACT.Square, accum_out=ssq[:, i:i + 1]))
                act.activation(ssq[:, i:i + 1], ssq[:, i:i + 1], ACT.Sqrt, scale=1.0 / D, bias=epsc[:]).then_inc(fin_rms, 1)

            for b in range(2):
                evac_late("out", b)
                squares(N_PEER, [b])
            evac_queries(0)
            evac_late("out", 2)
            evac_late("out", 3)
            evac_queries(1)
            squares(N_PEER, [2, 3])
            exponentials(0)
            for b in range(NB):
                if b == 0:
                    evac_queries(2)
                gelus(b)
                act.wait_ge(wgt_ready, b + 1)
                base = TURNS * (2 * b + 1)
                with act.Fori(0, TURNS) as it:
                    for i, k in enumerate(SHARED):
                        act.wait_ge(slot_free[k], it + (base + 1))
                        act.activation(wdiag[:, i, :], ident[:], ACT.Copy,
                                       scale=wgt[:, bass.ds(it * RING + k, 1)]).then_inc(wdiag_ready, 1)
                if b + 1 < NB:
                    exponentials(b + 1)
                final_squares(b)
                if b == 0:
                    evac_queries(3)

        @block.tensor
        def _(pe):
            def transposes(n, src, blocks):
                for k in range(KT):
                    j = KT * n + k
                    if j >= 4:
                        pe.wait_ge(ht_ready, j - 3)
                    for b in range(blocks):
                        ins = pe.transpose(bank[4 + j % 4][:, b * P:(b + 1) * P], src[:, b, k * P:(k + 1) * P], ident[:])
                    ins.then_inc(tp_done, 1)

            def begin(g, at=None):
                if g >= 4:
                    pe.wait_ge(proj_out, g - 3)
                return bank[g % 4 if at is None else at]

            def arrived(c):
                pe.wait_ge(w_landed[c % W_SLOTS], 16 * (c // W_SLOTS + 1))
                return W[:, c % W_SLOTS, :]

            def tile_T(c, g, x, lo, m, width, wait=None, last=False):
                w, ps = arrived(c), begin(g)
                for k in range(KT):
                    if wait is not None:
                        pe.wait_ge(ht_ready, wait + k + 1)
                    ins = pe.matmul(ps[0:m, 0:width], w[:, k * COLS + lo:k * COLS + lo + m], x[:, k, 0:width],
                                    start=(k == 0), stop=(k == KT - 1))
                ins.then_inc(proj_done, 1)
                return ins

            def tile_tok(c, g, x, b, lo, m, k0=0, at=None, start=True, stop=True):
                w = arrived(c)
                ps = begin(g, at) if start else bank[at]
                for k in range(KT):
                    ins = pe.matmul(ps[:, 0:m], x[:, k0 + k, b * P:(b + 1) * P], w[:, k * COLS + lo:k * COLS + lo + m],
                                    start=(start and k == 0), stop=(stop and k == KT - 1))
                if stop:
                    ins.then_inc(proj_done, 1)
                return ins

            def attention(lo, hi):
                def scores(u):
                    kind, h, b, n = unit(u)
                    ps = bank[u % 3][:, 0:n]
                    if u - 3 >= lo:
                        pe.wait_ge(p_ready, u - 2)
                    q = slice(b * P, (b + 1) * P)
                    if kind == "fox":
                        r = slice((h % 2) * HD, (h % 2 + 1) * HD)
                        pe.wait_ge(head_ready, h + 1)
                        pe.matmul(ps, fqT[r, h // 2, q], fkT[r, h // 2, 0:n], start=True, stop=False)
                        pe.matmul(ps, cposh[h % 2][0:72, q], onesb[0:72, 0:n], start=False, stop=False)
                        pe.matmul(ps, onesb[0:72, 0:P], cnegh[h % 2][0:72, 0:n], start=False, stop=False)
                        ins = pe.matmul(bank[u % 3][:, n - P:n], identb[:], winb[:, P:2 * P], start=False, stop=True)
                    elif kind == "chk":
                        r = slice((h % 2) * HD, (h % 2 + 1) * HD)
                        ins = pe.matmul(ps, cqT[r, h // 2, q], ckT[r, h // 2, 0:n], start=True, stop=True)
                    elif kind == "mem":
                        for c in range(2):
                            ins = pe.matmul(ps, mqT[:, 2 * h + c, q], mkT[:, 2 * h + c, :], start=(c == 0), stop=(c == 1))
                    else:
                        r = slice((h // 4) * HD, (h // 4 + 1) * HD)
                        pe.matmul(ps, aqT[r, h % 4, q], akT[r, (b + 1) * P - n:(b + 1) * P], start=True, stop=False)
                        ins = pe.matmul(ps, identb[:], winb[:, 2 * P - n:2 * P], start=False, stop=True)
                    ins.then_inc(sc_done, 1)

                def turn(u):
                    n = unit(u)[3]
                    pe.wait_ge(p_ready, u + 1)
                    if u - 2 >= lo:
                        pe.wait_ge(pt_ready, u - 1)
                    for j in range(n // P):
                        ins = pe.transpose(bank[3 + u % 2][:, j * P:(j + 1) * P], prob[:, u % 3, j * P:(j + 1) * P], ident[:])
                    ins.then_inc(pt_done, 1)

                def mix(u):
                    kind, h, b, n = unit(u)
                    pe.wait_ge(pt_ready, u + 1)
                    if u - 2 >= lo:
                        pe.wait_ge(y_done, u - 1)
                    for j in range(n // P):
                        if kind == "fox":
                            v = fv[:, j, h * HD:(h + 1) * HD]
                        elif kind == "chk":
                            v = cv[:, j, h * HD:(h + 1) * HD]
                        elif kind == "mem":
                            v = mv[:, j, h * MEM_HD:(h + 1) * MEM_HD]
                        else:
                            v = av[:, b + 1 - n // P + j, (h // 4) * HD:(h // 4 + 1) * HD]
                        ins = pe.matmul(bank[5 + u % 2][:, 0:v.shape[-1]], probT[:, u % 2, j * P:(j + 1) * P], v,
                                        start=(j == 0), stop=(j == n // P - 1))
                    ins.then_inc(pv_done, 1)

                for u in range(lo, hi + 3):
                    if u < hi:
                        scores(u)
                    if lo <= u - 2 < hi:
                        turn(u - 2)
                    if u - 3 >= lo:
                        mix(u - 3)

            pe.wait_ge(masks_ready, 1)
            pe.wait_ge(xn_ready, BLOCKS[N_MIX] + 4)
            transposes(N_MIX, XN, NB)
            for c in range(6):
                for j in range(4):
                    g = G_IN + 4 * c + j
                    if c in (2, 5):
                        tile_tok(C_IN + c, g, HT, j, 0, COLS)
                    else:
                        tile_T(C_IN + c, g, HT, j * P, P, TOK, wait=0 if g == 0 else None)
                if c == 0:
                    pe.wait_ge(consts_landed, 112)
                    for k in range(KT):
                        ins = pe.matmul(bank[4][0:72, :], wf[:, k * 72:(k + 1) * 72], HT[:, k, :], start=(k == 0), stop=(k == KT - 1))
                    ins.then_inc(f_done, 1)
            for i in range(4):
                pe.wait_ge(diag_ready, i // 2 + 1)
                if i == 0:
                    pe.wait_ge(f_log, 1)
                pe.matmul(bank[4 + i][:], ones[:], diag[:, i // 2, (i % 2) * COLS:(i % 2 + 1) * COLS],
                          start=True, stop=True).then_inc(gate_done, 1)
            pe.wait_ge(proj_out, G_OUT)
            pe.wait_ge(gate_ready, 4)
            attention(U_FOX, U_MEM)

            pe.wait_ge(xn_ready, BLOCKS[N_Y] + 4)
            transposes(N_Y, XN, NB)
            for n in range(2):
                for b in range(NB):
                    if n == 0 and b == 0:
                        pe.wait_ge(ht_ready, KT * (N_Y + 1))
                    tile_tok(C_OUT + n, G_OUT + NB * n + b, HT, b, 0, COLS)
            pe.wait_ge(xn_ready, BLOCKS[N_MEM] + MB)
            transposes(N_MEM, MX, MB)
            for n in range(2):
                for j in range(4):
                    tile_T(C_MK + n, G_MK + 4 * n + j, memT, j * P, P, MEM, wait=KT * N_MEM if n + j == 0 else None)
            for n in range(2):
                for b in range(MB):
                    tile_tok(C_MV + n, G_MV + MB * n + b, memT, b, 0, COLS)
            pe.wait_ge(xn_ready, BLOCKS[N_MEMPRE] + 4)
            transposes(N_MEMPRE, XN, NB)
            for n in range(2):
                for j in range(4):
                    tile_T(C_MQ + n, G_MQ + 4 * n + j, HT, j * P, P, TOK, wait=KT * N_MEMPRE if n + j == 0 else None)
            pe.wait_ge(proj_out, G_MO)
            attention(U_MEM, U_SWA)
            pe.wait_ge(y_done, U_SWA)
            transposes(N_MEMY, XN, NB)
            for n in range(2):
                for b in range(NB):
                    if n == 0 and b == 0:
                        pe.wait_ge(ht_ready, KT * (N_MEMY + 1))
                    tile_tok(C_MO + n, G_MO + NB * n + b, HT, b, 0, COLS)
            pe.wait_ge(xn_ready, BLOCKS[N_FF] + 4)
            transposes(N_FF, XN, NB)
            for c in range(8):
                for j in range(4):
                    tile_T(C_FF1 + c, G_FF1 + 4 * c + j, HT, j * P, P, TOK, wait=KT * N_FF if c + j == 0 else None)
            for n in range(2):
                for c in range(4):
                    for b in range(NB):
                        if b == 0:
                            pe.wait_ge(proj_out, G_FF1 + KT * (c + 1))
                        ins = tile_tok(C_FF2 + 4 * n + c, G_FF2 + NB * n + b, FH, b, 0, COLS, k0=KT * c, at=NB * n + b,
                                 start=(c == 0), stop=(c == 3))
                    if c < 3:
                        ins.then_inc(w_used, 1)
            pe.wait_ge(xn_ready, BLOCKS[N_ATT2] + 4)
            transposes(N_ATT2, XN, NB)
            g, c = G_IN2, C_IN2
            for j in range(4):
                tile_T(c, g + j, HT, j * P, P, TOK, wait=KT * N_ATT2 if j == 0 else None)
            tile_T(c + 1, g + 4, HT, 0, P, TOK)
            for b in range(NB):
                tile_tok(c + 1, g + 5 + b, HT, b, P, P)
            for j in range(2):
                tile_T(c + 1, g + 9 + j, HT, (2 + j) * P, P, TOK)
            for j in range(2):
                tile_T(c + 2, g + 11 + j, HT, j * P, P, TOK)
            tile_T(c + 2, g + 13, HT, 2 * P, GLA_RANK, TOK)
            pe.wait_ge(proj_out, g + 14)
            for j in range(2):
                pe.matmul(bank[4 + j][:], up[:, j * P:(j + 1) * P], glrT, start=True, stop=True).then_inc(z_done, 1)
            for n in range(2):
                for b in range(NB):
                    tile_tok(c + 3 + n, g + 14 + NB * n + b, HT, b, 0, COLS)
            pe.wait_ge(proj_out, G_OUT2)
            pe.wait_ge(z_log, 1)
            attention(U_SWA, U_END)

            def pair(k, q, ki, qi, h):
                r = slice((h % 2) * HD, (h % 2 + 1) * HD)
                return k[r, h // 2, ki * P:(ki + 1) * P], q[r, h // 2, qi * P:(qi + 1) * P]

            pe.wait_ge(y_done, U_END)
            for n in range(8 * NB):
                l, b = n // NB, n % NB
                if l == 0:
                    kk, qq = gkT, gqT
                else:
                    kk, qq = gk2[:, (l - 1) % 2], gq2[:, (l - 1) % 2]
                    if b == 0:
                        pe.wait_ge(gq_ready, l)
                        pe.wait_ge(gk_ready, l)
                    pe.wait_ge(ga_out, b + 1) if l == 1 else pe.wait_ge(ga_masked, n - 2 * NB + 1)
                for h in range(GLA_HEADS):
                    k, q = pair(kk, qq, b, b, h)
                    ins = pe.matmul(bank[2 * (n % 4) + h % 2][:, (h // 2) * P:(h // 2 + 1) * P], k, q, start=True, stop=True)
                ins.then_inc(ga_done, 1)
            for i, (ki, qi) in enumerate([(0, 1), (2, 3), (0, 2), (0, 3), (1, 2), (1, 3)]):
                l = 8 if i < 2 else 9
                pe.wait_ge(gq_ready, l)
                pe.wait_ge(gk_ready, l)
                if i < 4:
                    pe.wait_ge(ga_masked, 6 * NB + i + 1)
                else:
                    pe.wait_ge(ga_out, NB + i - 3)
                for h in range(GLA_HEADS):
                    k, q = pair(gk2[:, (l - 1) % 2], gq2[:, (l - 1) % 2], ki, qi, h)
                    ins = pe.matmul(bank[2 * (i % 4) + h % 2][:, (h // 2) * P:(h // 2 + 1) * P], k, q, start=True, stop=True)
                ins.then_inc(ga_done, 1)
            pe.wait_ge(ga_added, 7 * NB)
            pe.wait_ge(ga_out, NB + 6)
            pairs = {(0, 1): 0, (2, 3): 1, (0, 2): 2, (0, 3): 3, (1, 2): 4, (1, 3): 5}
            for b in range(NB):
                for h in range(GLA_HEADS):
                    for j in range(b + 1):
                        a = attd[:, b, :] if j == b else atto[:, pairs[j, b], :]
                        at = 2 * (h % 2) + h // 2
                        ins = pe.matmul(bank[4 + b][:, h * P:(h + 1) * P], a[:, at * P:(at + 1) * P],
                                        gv[:, j, h * GLA_DV:(h + 1) * GLA_DV], start=(j == 0), stop=(j == b))
                ins.then_inc(go_done, 1)
            pe.wait_ge(go_ready, NB)
            transposes(N_Y2, XN, NB)
            pe.wait_ge(ht_ready, KT * (N_Y2 + 1))
            def key_scores(b):
                pe.wait_ge(sub_landed, 16)
                for q in range(QUARTERS):
                    pe.wait_ge(proj_out, late("query", b, 4 * q + 3) + 1)
                    if b > 0:
                        pe.wait_ge(top_done, QUARTERS * (b - 1) + q + 1)
                    for s in range(4):
                        ins = pe.matmul(bank[4 + q][:, s * P:(s + 1) * P], pqT[:, 4 * q + s, :], subT[:, 4 * q + s, :],
                                        start=True, stop=True)
                    ins.then_inc(sub_done, 1)

            def add_rows(b):
                base = TURNS * (2 * b + 1)

                def turn(n, first, last):
                    for i, k in enumerate(SHARED):
                        pe.wait_ge(wdiag_ready, n * len(SHARED) + (len(SHARED) * TURNS * b + i + 1))
                        pe.wait_ge(row_landed[k], n * 16 + 16 * (base + 1))
                        for half in range(2):
                            ins = pe.matmul(bank[half][:], wdiag[:, i, :], ring[:, k, half * COLS:(half + 1) * COLS],
                                            start=(first and i == 0), stop=(last and i == len(SHARED) - 1))
                        ins.then_inc(slot_free[k], 1)

                if b > 0:
                    pe.wait_ge(fin_x, b)
                turn(0, True, False)
                with pe.Fori(1, TURNS - 1) as it:
                    turn(it, False, False)
                turn(TURNS - 1, False, True)

            for kind, b, i in LATE:
                g = late(kind, b, i)
                if (kind, b, i) == ("turn", NB - 1, 0):
                    pe.wait_ge(proj_out, g)
                    add_rows(0)
                    key_scores(2)
                    pe.wait_ge(fin_x, 1)
                if kind == "out":
                    tile_tok(C_OUT2 + i, g, HT, b, 0, COLS)
                elif kind == "turn":
                    pe.wait_ge(xn_ready, BLOCKS[N_PEER] + b + 1)
                    ps = begin(g)
                    for j in range(4):
                        ins = pe.transpose(ps[:, j * P:(j + 1) * P], XN[:, b, (4 * i + j) * P:(4 * i + j + 1) * P], ident[:])
                    ins.then_inc(proj_done, 1)
                elif kind == "query":
                    pe.wait_ge(wq_landed, 64)
                    pe.wait_ge(proj_out, late("turn", b, 1) + 1)
                    ps = begin(g)
                    for k in range(KT):
                        at = k * COLS + (i % 4) * P
                        ins = pe.matmul(ps[:, 0:P], wq[:, i // 4, at:at + P], HT[:, k, b * P:(b + 1) * P], start=(k == 0), stop=(k == KT - 1))
                    ins.then_inc(proj_done, 1)
                else:
                    ps = begin(g)
                    for j in range(4):
                        ins = pe.transpose(ps[:, j * P:(j + 1) * P], HT[:, 4 * i + j, b * P:(b + 1) * P], ident[:])
                    ins.then_inc(proj_done, 1)
                    if i == 1 and b < 2:
                        key_scores(b)
            pe.wait_ge(proj_out, G_OUT2 + len(LATE))
            for b in range(1, NB):
                add_rows(b)
                if b == 1:
                    key_scores(3)

        @block.vector
        def _(dve):
            steps = [0]

            def link(ins):
                steps[0] += 1
                ins.then_inc(dve_step, 1)
                dve.wait_ge(dve_step, steps[0])

            def normed(n, blocks=range(NB)):
                for b in blocks:
                    i = STATS[n] + b
                    dve.wait_ge(ss_ready, i + 1)
                    link(dve.reciprocal(rstd[:, i:i + 1], ssq[:, i:i + 1]))
                    dve.tensor_scalar(XN[:, b, :], X[:, b, :], rstd[:, i:i + 1], None, ALU.mult).then_inc(xn_ready, 1)

            def add_post(s, row, landed, value):
                dve.wait_ge(landed, value)
                for b in range(NB):
                    dve.wait_ge(post_ready, NB * s + b + 1)
                    link(dve.reciprocal(prstd[:, s, b:b + 1], psq[:, s, b, 1:2]))
                    link(dve.scalar_tensor_tensor(out=XN[:, b, :], in0=XN[:, b, :], scalar=prstd[:, s, b:b + 1],
                                                  in1=GROW[:, row, :], op0=ALU.mult, op1=ALU.mult))
                    dve.tensor_tensor(X[:, b, :], X[:, b, :], XN[:, b, :], ALU.add).then_inc(x_ready, 1)

            def head_decays(h):
                dve.tensor_scalar(cposh[h % 2][0:72, :], cpos[0:72, :], headsel[0:72, h:h + 1], None, ALU.mult)
                dve.tensor_scalar(cnegh[h % 2][0:72, :], cneg[0:72, :], headsel[0:72, h:h + 1], None, ALU.mult).then_inc(head_ready, 1)

            def attention(lo, hi):
                for u in range(lo, hi + 3):
                    if u < hi:
                        kind, h, b, n = unit(u)
                        dve.wait_ge(sc_done, u + 1)
                        src, mx = bank[u % 3][:, 0:n], nmax[:, u:u + 1]
                        if kind == "chk":
                            if b == 0:
                                dve.wait_ge(rel_landed[h % 2], 16 * (h // 2 + 1))
                                link(dve.memset(relb[0:SPAN, h % 2, 0:SPAN], NEG))
                            if u - 2 >= lo:
                                dve.wait_ge(p_ready, u - 1)
                            link(dve.tensor_tensor_reduce(out=biased[:, u % 2, 0:n], in0=src, in1=relb[:, h % 2, n - 1::-1],
                                                          scale=1.0, scalar=-3e38, op0=ALU.add, op1=ALU.max, accum_out=mx))
                            dve.tensor_scalar(mx, mx, -1.0, None, ALU.mult).then_inc(mx_ready, 1)
                        elif kind == "swa":
                            link(dve.tensor_reduce(mx, src, AX.X, ALU.max))
                            dve.tensor_scalar(mx, mx, sinks[:, h:h + 1], -1.0, ALU.max, ALU.mult).then_inc(mx_ready, 1)
                        else:
                            dve.tensor_reduce(mx, src, AX.X, ALU.max, negate=True).then_inc(mx_ready, 1)
                        if kind == "fox" and b == 0 and 1 <= h < HEADS - 1:
                            head_decays(h + 1)
                    v = u - 3
                    if v >= lo:
                        kind, h, b, n = unit(v)
                        dve.wait_ge(p_ready, v + 1)
                        if kind == "swa":
                            link(dve.tensor_tensor(rsum[:, v:v + 1], rsum[:, v:v + 1], skx[:, v:v + 1], ALU.add))
                        link(dve.reciprocal(rinv[:, v:v + 1], rsum[:, v:v + 1]))
                        dve.wait_ge(pv_done, v + 1)
                        w = MEM_HD if kind == "mem" else HD
                        at = h * w + (COLS if kind == "chk" else 0)
                        dve.tensor_scalar(XN[:, b, at:at + w], bank[5 + v % 2][:, 0:w], rinv[:, v:v + 1], None,
                                          ALU.mult).then_inc(y_done, 1)

            normed(N_MIX)
            dve.wait_ge(c_ready, 1)
            for r in range(48):
                dve.wait_ge(ada_landed[r % 3], 16 * (r // 3 + 1))
                dve.tensor_tensor_reduce(out=ada[:, r % 3, :], in0=ada[:, r % 3, :], in1=crow, scale=1.0, scalar=0.0,
                                         op0=ALU.mult, op1=ALU.add, accum_out=mod[:, r:r + 1]).then_inc(ada_used, 1)
            dve.wait_ge(ada_used, 48)
            dve.wait_ge(consts_landed, 112)
            link(dve.tensor_tensor(mod[:], mod[:], bada[:], ALU.add))
            for i, (scale, gc) in enumerate(((8, GC_ATT2), (32, GC_PEER))):
                dve.scalar_tensor_tensor(out=scol[:, i, :], in0=mod[:, scale:scale + KT], scalar=1.0, in1=gcol[:, gc, :],
                                         op0=ALU.add, op1=ALU.mult)
            dve.wait_ge(masks_ready, 1)
            for i, gate in enumerate((16, 40)):
                for k in range(KT):
                    ins = dve.tensor_scalar(diag[:, i, k * P:(k + 1) * P], ident[:], mod[:, gate + k:gate + k + 1], None, ALU.mult)
                ins.then_inc(diag_ready, 1)
            fz, fe = XN[0:72, 0, 0:512], XN[0:72, 0, 512:1024]
            fc, fr = XN[0:72, 1, 0:512], XN[0:72, 1, 512:1024]
            dve.wait_ge(f_log, 1)
            link(dve.scalar_tensor_tensor(out=fz, in0=fz, scalar=0.0, in1=fe, op0=ALU.min, op1=ALU.subtract))
            dve.memset(fe, 1.0)
            link(dve.memset(fr, 1.0))
            link(dve.tensor_tensor_scan(fc, fe, fz, 0.0, ALU.mult, ALU.add))
            for part in range(3):
                rows = slice(32 * part, 32 * part + HEADS)
                low = cposh[0][0:72, :]
                link(dve.tensor_copy(low, fc))
                dve.tensor_copy(cpos[rows, :], low[rows, :])
                dve.tensor_scalar(cneg[rows, :], low[rows, :], -1.0, None, ALU.mult)
                link(dve.tensor_tensor(fr, fc, low, ALU.subtract))
                link(dve.tensor_copy(fc, fr))
            head_decays(0)
            head_decays(1)
            attention(U_FOX, U_MEM)

            for b in range(NB):
                for half in range(2):
                    i = STATS[N_Y] + 2 * b + half
                    y = XN[:, b, half * COLS:(half + 1) * COLS]
                    dve.wait_ge(ss_ready, i + 1)
                    link(dve.reciprocal(rstd[:, i:i + 1], ssq[:, i:i + 1]))
                    ins = dve.tensor_scalar(y, y, rstd[:, i:i + 1], None, ALU.mult)
                ins.then_inc(xn_ready, 1)
            for b in range(MB):
                i = STATS[N_MEM] + b
                dve.wait_ge(ss_ready, i + 1)
                link(dve.reciprocal(rstd[:, i:i + 1], ssq[:, i:i + 1]))
                dve.tensor_scalar(MX[:, b, :], MX[:, b, :], rstd[:, i:i + 1], None, ALU.mult).then_inc(xn_ready, 1)
            add_post(0, 0, rows_landed, 96)
            normed(N_MEMPRE)
            attention(U_MEM, U_SWA)
            add_post(1, 1, rows_landed, 96)
            normed(N_FF)
            add_post(2, 0, row2_landed, 16)
            normed(N_ATT2)
            dve.wait_ge(z_log, 1)
            link(dve.scalar_tensor_tensor(out=decay, in0=decay, scalar=0.0, in1=fade[:, 0], op0=ALU.min, op1=ALU.subtract))
            link(dve.memset(fade[:, 1, 0, :], 1.0))
            for j in range(2):
                dve.tensor_tensor_scan(fade[:, 0, j, :], fade[:, 1, 0, :], decay[:, j, :], 0.0, ALU.mult, ALU.add).then_inc(decay_ready, 1)
            dve.wait_ge(decay_ready, 2)
            link(dve.tensor_copy(decay, fade[:, 0]))
            dve.wait_ge(rows_landed, 96)
            for b in range(NB):
                dve.wait_ge(proj_out, G_IN2 + 18 + b + 1)
                dve.tensor_tensor(gg[:, b, :], gg[:, b, :], NWROW[:], ALU.mult).then_inc(gg_ready, 1)
            attention(U_SWA, U_END)

            def fading(l):
                m = GLA_HALVES[l]
                if l >= 2:
                    dve.wait_ge(gk_ready, l - 1)
                    dve.wait_ge(gq_ready, l - 1)
                src = decay.rearrange("p j t -> p (j t)").rearrange("p (g r) -> p g r", r=2 * m)
                f = fade[:, l % 2].rearrange("p j t -> p (j t)")
                dst = f.rearrange("p (g r) -> p g r", r=2 * m)
                link(dve.tensor_tensor(dst, src, src[:, :, m - 1:m].broadcast_to(src.shape), ALU.subtract))
                dve.scalar_tensor_tensor(out=f, in0=f, scalar=-1.0, in1=f, op0=ALU.mult, op1=ALU.max).then_inc(fade_in, 1)

            def queries(l):
                dve.wait_ge(fade_out, l + 1)
                if l >= 2:
                    dve.wait_ge(ga_done, NB * (l - 1) + NB)
                dve.tensor_tensor(gq2[:, l % 2], gqT, fade[:, l % 2], ALU.mult).then_inc(gq_ready, 1)

            fading(0)
            fading(1)
            for n in range(8 * NB):
                l, b = n // NB, n % NB
                if b == 0:
                    queries(l)
                    if l + 2 < len(GLA_HALVES):
                        fading(l + 2)
                    if l == 7:
                        queries(8)
                dve.wait_ge(ga_done, n + 1)
                mask = levelmask[:, l:l + 1, :].broadcast_to([P, 2, P])
                if l >= 2:
                    dve.wait_ge(ga_added, n - 2 * NB + 1)
                to, ready = (attd[:, b, :], ga_out) if l == 0 else (masked[:, n % 4, :], ga_masked)
                for r in range(2):
                    half = slice(2 * P * r, 2 * P * (r + 1))
                    ins = dve.tensor_tensor(to[:, half].rearrange("p (h t) -> p h t", h=2),
                                            bank[2 * (n % 4) + r][:, 0:2 * P].rearrange("p (h t) -> p h t", h=2), mask, ALU.mult)
                ins.then_inc(ready, 1)
            for b in range(NB):
                dve.wait_ge(go_sq, b + 1)
                dve.tensor_reduce(ssy[:, b, :], masked[:, b, :].rearrange("p (h e) -> p h e", h=GLA_HEADS), AX.X, ALU.add).then_inc(go_ss, 1)
            dve.wait_ge(gg_ready, NB)
            for b in range(NB):
                dve.wait_ge(go_rms, b + 1)
                link(dve.reciprocal(rsy[:, b, :], ssy[:, b, :]))
                for h in range(GLA_HEADS):
                    s = slice(h * GLA_DV, (h + 1) * GLA_DV)
                    ins = dve.scalar_tensor_tensor(out=XN[:, b, COLS + h * GLA_DV:COLS + (h + 1) * GLA_DV], in0=bank[4 + b][:, s],
                                                   scalar=rsy[:, b, h:h + 1], in1=gg[:, b, s], op0=ALU.mult, op1=ALU.mult)
                ins.then_inc(go_ready, 1)
            def add_mixed(b):
                dve.wait_ge(proj_out, late("out", b, 1) + 1)
                link(dve.tensor_tensor(XN[:, b, :], XN[:, b, :], GATE[:, 0, :], ALU.mult))
                dve.tensor_tensor(X[:, b, :], X[:, b, :], XN[:, b, :], ALU.add).then_inc(x_ready, 1)

            for b in range(2):
                add_mixed(b)
                normed(N_PEER, [b])

            def best_half(vals, pos, src, rest, n):
                for i in range(n):
                    ins = dve.max(vals[:, i, 0:8], src(i))
                link(ins)
                for i in range(n):
                    dve.max_index(pos[:, i, 0:8], vals[:, i, 0:8], src(i))
                    ins = dve.match_replace(rest[:, i, :], vals[:, i, 0:8], src(i), -3e38)
                return ins

            def other_half(vals, pos, rest, n):
                for i in range(n):
                    ins = dve.max(vals[:, i, 8:16], rest[:, i, :])
                link(ins)
                for i in range(n):
                    ins = dve.max_index(pos[:, i, 8:16], vals[:, i, 8:16], rest[:, i, :])
                return ins

            def sums(dst, first, second):
                off = 0
                for a0, na, nb in CAND_PARTS:
                    for h in range(2) if na > 1 else (slice(0, 2),):
                        if na > 1:
                            shape = [P, na, nb]
                            to = dst[:, h, off:off + na * nb].rearrange("p (a b) -> p a b", b=nb)
                            ins = dve.tensor_tensor(to, first[:, h, a0:a0 + na, None].broadcast_to(shape),
                                                    second[:, h, None, 0:nb].broadcast_to(shape), ALU.add)
                        else:
                            ins = dve.tensor_tensor(dst[:, :, off:off + nb], second[:, :, 0:nb],
                                                    first[:, :, a0:a0 + 1].broadcast_to([P, 2, nb]), ALU.add)
                    off += na * nb
                return ins

            halves_v = topv.rearrange("p (h s) k -> p s h k", s=2)
            halves_i = topf.rearrange("p (h s) k -> p s h k", s=2)

            def pick(b, q, step):
                ls, hs = slice(4 * q, 4 * q + 4), slice(2 * q, 2 * q + 2)
                if step == 0:
                    dve.wait_ge(sub_done, QUARTERS * b + q + 1)
                    link(best_half(topv[:, ls, :], topi[:, ls, :], lambda i: bank[4 + q][:, i * P:(i + 1) * P], left, 4))
                elif step == 1:
                    other_half(topv[:, ls, :], topi[:, ls, :], left, 4).then_inc(top_done, 1)
                    dve.wait_ge(top_done, QUARTERS * b + q + 1)
                elif step == 2:
                    sums(cand, halves_v[:, 0, hs], halves_v[:, 1, hs])
                    link(dve.tensor_copy(topf, topi[:, ls, :]))
                    link(dve.tensor_scalar(halves_i[:, 0], halves_i[:, 0], float(N_KEYS), None, ALU.mult))
                    link(sums(cande, halves_i[:, 0], halves_i[:, 1]))
                    link(best_half(bestv[:, hs, :], bestp, lambda i: cand[:, i, :], candl, 2))
                    link(other_half(bestv[:, hs, :], bestp, candl, 2))
                    link(dve.tensor_copy(bestf, bestp))
                else:
                    shape = [P, TOPK, CAND]
                    for i in range(2):
                        ins = dve.tensor_tensor(onehot[i], iota[:, None, :].broadcast_to(shape),
                                                bestf[:, i, :, None].broadcast_to(shape), ALU.is_equal)
                    link(ins)
                    for i in range(2):
                        ins = dve.tensor_tensor(onehot[i], onehot[i], cande[:, i, None, :].broadcast_to(shape), ALU.mult)
                    link(ins)
                    for i in range(2):
                        ins = dve.tensor_reduce(eid[:, i, :], onehot[i], AX.X, ALU.add)
                    link(ins)
                    dve.tensor_copy(expert[:, b % 2, 2 * TOPK * q:2 * TOPK * (q + 1)].rearrange("p (h k) -> p h k", k=TOPK),
                                    eid).then_inc(expert_ready, 1)
                    if q == QUARTERS - 1:
                        dve.tensor_tensor(gates, bestv, bestv[:, :, 0:1].broadcast_to([P, PEER_HEADS, TOPK]), ALU.subtract).then_inc(gate_in, 1)

            def hidden(b, c):
                base = TURNS * 2 * b + 2 * c
                with dve.Fori(0, 2) as it:
                    for k in range(RING):
                        dve.wait_ge(row_landed[k], it * 16 + 16 * (base + 1))
                        dve.tensor_tensor_reduce(out=ring[:, k, :], in0=ring[:, k, :], in1=XN[:, b, :], scale=1.0, scalar=0.0,
                                                 op0=ALU.mult, op1=ALU.add, accum_out=hslot[:, k:k + 1]).then_inc(slot_free[k], 1)
                    dve.wait_ge(slot_free[RING - 1], it + (base + 2))
                    dve.tensor_copy(hid[:, bass.ds(it * RING + 2 * RING * c, RING)], hslot).then_inc(hid_copied, 1)
                    dve.wait_ge(hid_copied, it + (TURNS * b + 2 * c + 1))

            def prepare(b):
                dve.wait_ge(gate_exp, b + 1)
                link(dve.tensor_reduce(gsum, gates, AX.X, ALU.add))
                link(dve.reciprocal(ginv, gsum))
                dve.tensor_tensor(gates, gates, ginv[:, :, None].broadcast_to([P, PEER_HEADS, TOPK]), ALU.mult)
                if b > 0:
                    dve.wait_ge(fin_x, b)
                link(dve.memset(acc, 0.0))

            def weights(b):
                dve.wait_ge(hid_gelu, b + 1)
                dve.tensor_tensor(wgt, hid, gates.rearrange("p h k -> p (h k)"), ALU.mult).then_inc(wgt_ready, 1)
                dve.wait_ge(wgt_ready, b + 1)

            def weighted(b, t):
                base = TURNS * (2 * b + 1)
                mine = [k for k in range(RING) if k not in SHARED]
                for i, k in enumerate(mine):
                    dve.wait_ge(row_landed[k], t * 16 + 16 * (base + 1))
                    dve.wait_ge(slot_free[mine[i - 1]], t + (base + (2 if i else 1)))
                    dve.scalar_tensor_tensor(out=acc, in0=ring[:, k, :], scalar=wgt[:, bass.ds(t * RING + k, 1)],
                                             in1=acc, op0=ALU.mult, op1=ALU.add).then_inc(slot_free[k], 1)

            def add_experts(b):
                for k in (RING - 1, RING - 2):
                    dve.wait_ge(slot_free[k], TURNS * 2 * (b + 1) + 1)
                for half in range(2):
                    s = slice(half * COLS, (half + 1) * COLS)
                    ins = dve.tensor_tensor(acc[:, s], acc[:, s], bank[half][:], ALU.add)
                link(ins)
                link(dve.tensor_tensor(acc, acc, GATE[:, 1, :], ALU.mult))
                dve.tensor_tensor(X[:, b, :], X[:, b, :], acc, ALU.add).then_inc(fin_x, 1)

            def final_norm(b):
                dve.wait_ge(row3_landed, 16)
                dve.wait_ge(fin_rms, b + 1)
                link(dve.reciprocal(rstd[:, 30 + b:31 + b], ssq[:, 30 + b:31 + b]))
                dve.scalar_tensor_tensor(out=XN[:, b, :], in0=X[:, b, :], scalar=rstd[:, 30 + b:31 + b], in1=GROW[:, 1, :],
                                         op0=ALU.mult, op1=ALU.mult).then_inc(fin_ready, 1)

            dve.wait_ge(claimed, 1)
            for k in range(RING):
                dve.sem_inc(slot_free[k], 1)
            for step in range(4):
                pick(0, 0, step)
            for b in range(NB):
                dve.wait_ge(proj_out, late("token", b, 1) + 1)
                for c in range(CHUNKS):
                    if b == 0 and c < CHUNKS - 2:
                        for step in range(2):
                            pick(0, c // 2 + 1, 2 * (c % 2) + step)
                    if c == CHUNKS - 1:
                        prepare(b)
                    hidden(b, c)
                    if b == 0 and c in (1, 2):
                        add_mixed(c + 1)
                    if b == 0 and c in (3, 4):
                        normed(N_PEER, [c - 1])
                    if b > 0 and c == 0:
                        final_norm(b - 1)
                dve.sem_inc(hid_ready, 1)
                weights(b)
                if b + 1 < NB:
                    for t in range(TURNS):
                        weighted(b, t)
                        pick(b + 1, t // 4, t % 4)
                else:
                    with dve.Fori(0, TURNS) as it:
                        weighted(b, it)
                add_experts(b)
            final_norm(NB - 1)


def pack(w):
    k, n = w.shape
    return w.reshape(k // D, KT, P, n // COLS, COLS).transpose(3, 0, 2, 1, 4).reshape(-1, P, KT * COLS)


def column(v, width=P):
    return v.reshape(-1, width).T


def layouts(i):
    w_in, w_in_2 = i["w_in"][0], i["w_in_2"][0]
    nf = HEADS * HD
    a = {}
    a["x"] = i["x"][0].reshape(NB, P, D)
    a["mem"] = i["mem"][0].reshape(MB, P, D).transpose(1, 0, 2)
    a["c"] = i["c_2"]
    main = np.concatenate([w_in[:, :3 * nf], w_in[:, 3 * nf + HEADS:]], axis=1)
    a["w_in"] = pack(main)
    f = np.zeros((D, 72), np.float32)
    bf = np.zeros((P, 1), np.float32)
    for part in range(3):
        f[:, 32 * part:32 * part + HEADS] = w_in[:, 3 * nf:3 * nf + HEADS]
        bf[32 * part:32 * part + HEADS, 0] = i["b_fgt"][0]
    a["w_fgt"] = f.reshape(KT, P, 72).transpose(1, 0, 2).reshape(P, -1)
    a["b_fgt"] = bf
    for n in ("w_out", "w_mk", "w_mv", "w_mq", "w_mo", "w_ff1", "w_ff2", "w_out_2"):
        a[n] = pack(i[n][0])
    a["w_pq"] = pack(i["peer_wq_2"][0])
    aq = w_in_2[:, :512].reshape(D, 2, 4, HD).transpose(0, 2, 1, 3).reshape(D, 512)
    ak, av, gq, gk, gv, gg, glr = np.split(w_in_2[:, 512:], np.cumsum([128, 128, 256, 256, 512, 512]), axis=1)
    third = np.concatenate([gk, glr, np.zeros((D, 512 - 256 - GLA_RANK), np.float32)], axis=1)
    a["w_in_2"] = pack(np.concatenate([aq, ak, av, gq, third, gv, gg], axis=1))
    rel = np.clip(np.arange(REL_W) - (P - 1), -MAX_REL, MAX_REL) + MAX_REL
    a["rel"] = i["rel_bias"][0][:, rel]
    a["gain_cols"] = np.stack([column(v) for v in (
        i["g_mix_pre"][0], np.concatenate([i["g_fox_out"][0], i["g_chk_out"][0]]), i["g_mem_kv"][0],
        i["g_mem_pre"][0], i["g_ff_pre"][0], i["norm1_w_2"][0], i["norm2_w_2"][0])], axis=1)
    a["gain_rows"] = np.stack([i["g_mix_post"][0], i["g_mem_post"][0], i["g_ff_post"][0], i["final_norm_w_2"]])[:, None, :]
    a["gla_norm"] = i["gla_norm_w_2"]
    a["gla_gate_up"] = i["gla_gate_up_2"][0]
    a["gla_gate_bias"] = column(i["gla_gate_bias_2"][0])
    a["sinks"] = i["attn_sinks_2"]
    a["w_ada"] = i["w_ada_2"][0].T.reshape(48, P, D)
    a["b_ada"] = column(i["b_ada_2"][0])
    a["subkeys"] = i["peer_subkeys_2"][0].reshape(16, N_KEYS, P).transpose(2, 0, 1)
    a["peer_u"] = i["peer_u_2"][0]
    a["peer_v"] = i["peer_v_2"][0]
    return a


def kernel(**inputs):
    import concourse.bacc as bacc
    from concourse.bass_utils import run_bass_kernel_spmd

    nc = bacc.Bacc("TRN2", target_bir_lowering=False, num_devices=1)
    arrays, args = {}, {}
    for name, a in layouts({k: np.asarray(v) for k, v in inputs.items()}).items():
        a = np.ascontiguousarray(a)
        arrays[f"in_{name}"] = a
        args[name] = nc.dram_tensor(f"in_{name}", a.shape, mybir.dt.from_np(a.dtype), kind="ExternalInput").ap()
    out = nc.dram_tensor("out", (NB, P, D), F32, kind="ExternalOutput").ap()
    build(nc, args, out)
    r = run_bass_kernel_spmd(nc, [arrays], core_ids=[0])
    return r.results[0]["out"].reshape(1, TOK, D)
```

```python
from contextlib import ExitStack

import numpy as np

import concourse.bass as bass
from concourse import mybir

F32 = mybir.dt.float32
F32R = mybir.dt.float32r
BF16 = mybir.dt.bfloat16
U32 = mybir.dt.uint32
ALU = mybir.AluOpType
ACT = mybir.ActivationFunctionType
AX = mybir.AxisListType

P = 128
TOK = 512
NB = TOK // P
D = 1024
KT = D // P
COLS = 512
HALF = 256
EPS = 1e-6
NEG = -1e30

HEADS = 8
HD = 64
SPAN = 64
MAX_REL = 128
REL_W = TOK + P - 1
MEM = 256
MB = MEM // P
MEM_HEADS = 4
MEM_HD = D // MEM_HEADS
FF_T = 4 * D // P // 2

SWA_HEADS = 8
GLA_HEADS = 4
GLA_DV = 128
GLA_RANK = 16
GLA_TAU = 16.0
GLA_HALVES = [1, 2, 4, 8, 16, 32, 64, 128, 256]

PEER_HEADS = 8
TOPK = 16
SLOTS = PEER_HEADS * TOPK
N_KEYS = 128
CAND_PARTS = [(0, 1, 16), (1, 1, 8), (2, 2, 5), (4, 4, 3), (8, 8, 1)]
CAND = sum(na * nb for _, na, nb in CAND_PARTS)
assert all(any(a0 <= a < a0 + na and TOPK // (a + 1) <= nb for a0, na, nb in CAND_PARTS) for a in range(TOPK))
RING = 8
TURNS = SLOTS // RING
QUARTERS = 4
CHUNKS = 2 * QUARTERS
SHARED = range(1, RING, 2)

W_SLOTS = 3
C_IN, C_OUT, C_MK, C_MV, C_MQ, C_MO, C_FF1, C_FF2, C_IN2, C_OUT2, C_END = (
    0, 12, 16, 20, 24, 28, 32, 40, 64, 74, 76)
G_IN, G_OUT, G_MK, G_MV, G_MQ, G_MO, G_FF1, G_FF2, G_IN2, G_OUT2 = (
    0, 24, 32, 40, 44, 52, 60, 76, 108, 130)
C_ROUND, G_ROUND = 16, FF_T + 2 * NB
LATE = [(kind, b, i) for kind, b in (("mixed", 0), ("mixed", 1), ("out", 0), ("mixed", 2), ("mixed", 3), ("out", 1)) for i in range(2)]
for _b in range(NB):
    LATE += [("turn", _b, i) for i in range(2)] + [("query", _b, i) for i in range(16)] + [("token", _b, i) for i in range(2)]
    if _b == 0:
        LATE += [("out", b, i) for i in range(2) for b in (2, 3)]


def late(*event):
    return G_OUT2 + LATE.index(event)


(N_MIX, N_Y, N_MEM, N_MEMPRE, N_MEMY, N_FF, N_ATT2, N_PEER) = range(8)
NORMED = [N_MEMPRE, N_FF, N_ATT2, N_PEER]
SCALED = [N_MIX, N_Y, N_MEMPRE, N_MEMY, N_FF, N_ATT2]
STATS = {N_MIX: 0, N_Y: 4, N_MEM: 12, N_MEMPRE: 14, N_FF: 18, N_ATT2: 22, N_PEER: 26}
BLOCKS = {N_MIX: 0, N_Y: 4, N_MEM: 8, N_MEMPRE: 10, N_FF: 14, N_ATT2: 18, N_PEER: 22}
(GC_MIX, GC_Y, GC_MEMKV, GC_MEMPRE, GC_FF, GC_ATT2, GC_PEER) = range(7)

U_FOX, U_CHK, U_MEM, U_SWA, U_END = 0, 32, 64, 80, 112


def unit(u):
    if u < U_CHK:
        return "fox", u // NB, u % NB, (u % NB + 1) * P
    if u < U_MEM:
        return "chk", (u - U_CHK) // NB, u % NB, (u % NB + 1) * P
    if u < U_SWA:
        return "mem", (u - U_MEM) // NB, u % NB, MEM
    return "swa", (u - U_SWA) // NB, u % NB, (P if u % NB == 0 else 2 * P)


def build(nc, A, out):
    ctx = ExitStack()
    with ctx:
        def sb(name, shape, dt=F32):
            return ctx.enter_context(nc.sbuf_tensor(name, shape, dt))

        def sem(name):
            return ctx.enter_context(nc.semaphore(name))

        bank = [ctx.enter_context(nc.psum_tensor(f"bank{i}", [P, COLS], F32)) for i in range(8)]

        X = sb("x_res", [P, NB, D])
        XN = sb("x_norm", [P, NB, D])
        def below(*shapes):
            with ExitStack() as inner:
                return [inner.enter_context(nc.sbuf_tensor(name, shape, dt)) for name, shape, dt in shapes]

        HTH, = below(("h_T_high", [P, KT, TOK], F32R))
        HT = sb("h_T", [P, KT, TOK])
        HTL, = below(("h_T_low", [P, KT, TOK], F32R))
        GATE = sb("gate_rows", [P, 2, D])
        levelmask = sb("level_masks", [P, 8, P])
        FINROW = sb("final_gain_row", [P, D])
        WS, = below(("weights_split", [P, W_SLOTS, KT * COLS], F32R))
        W = sb("weights", [P, W_SLOTS, KT * COLS])
        _, WFL, WFH = below(("mixer_parts", [P, 14848], F32), ("w_forget_low", [P, KT * 72], F32R),
                            ("w_forget_high", [P, KT * 72], F32R))
        FHH, FHL = below(("hidden_high", [P, FF_T, TOK], F32R), ("hidden_low", [P, FF_T, TOK], F32R))
        AREA = sb("area", [P, 16384])
        SCR = sb("scratch", [P, 4096])
        GROW = sb("gain_row", [P, D])
        NWROW = sb("gla_norm_row", [P, COLS])
        ident = sb("ident", [P, P])
        identb = sb("ident_bf", [P, P], BF16)
        ones = sb("ones", [P, P])
        epsc = sb("eps_col", [P, 1])
        onesb = sb("ones_bf", [P, COLS], BF16)
        winb = sb("window_mask", [P, 2 * P], BF16)
        headsel = sb("head_select", [P, HEADS])
        gcol = sb("gain_cols", [P, 7, KT])
        bfcol = sb("forget_bias", [P, 1])
        gbcol = sb("gate_bias", [P, 2])
        bada = sb("b_ada_cols", [P, 48])
        mod = sb("mod_cols", [P, 48])
        scol = sb("scale_cols", [P, 2, KT])
        sinks = sb("sinks", [P, SWA_HEADS])
        up = sb("gate_up", [GLA_RANK, 2 * P])
        nmax = sb("neg_max", [P, U_END])
        rsum = sb("row_sum", [P, U_END])
        rinv = sb("row_inv", [P, U_END])
        skx = sb("sink_exp", [P, U_END])
        ssq = sb("sum_sq", [P, 40])
        rstd = sb("rstd", [P, 40])
        psq = sb("post_sum_sq", [P, 3, NB, 2])
        prstd = sb("post_rstd", [P, 3, NB])
        ssy = sb("gla_sum_sq", [P, NB, GLA_HEADS])
        rsy = sb("gla_rstd", [P, NB, GLA_HEADS])

        def area(lo, n, **dims):
            v = AREA[:, lo:lo + n]
            return v.rearrange("p (a b) -> p a b", **dims) if dims else v

        fqT, fkT, cqT, ckT = (area(2048 * i, 2048, b=TOK) for i in range(4))
        wf = area(14848, KT * 72)
        fv, cv = area(8192, 2048, b=COLS), area(10240, 2048, b=COLS)
        cpos = AREA[:, 12288:12544].bitcast(BF16)
        cneg = AREA[:, 12544:12800].bitcast(BF16)
        cposh = [AREA[:, 12800 + 256 * i:13056 + 256 * i].bitcast(BF16) for i in range(2)]
        cnegh = [AREA[:, 13312 + 256 * i:13568 + 256 * i].bitcast(BF16) for i in range(2)]
        relb = area(13824, 2048, b=COLS)
        MX, memT = area(0, 2048, b=D), area(2048, 2048, b=MEM)
        mkT, mv, mqT = area(4096, 2048, b=MEM), area(6144, 2048, b=D), area(8192, 4096, b=TOK)
        aqT, akT, av = area(0, 2048, b=TOK), area(2048, 512), area(2560, 512, b=P)
        gqT, gkT = area(3072, 1024, b=TOK), area(4096, 1024, b=TOK)
        gv, gg = area(5120, 2048, b=COLS), area(7168, 2048, b=COLS)
        decay = area(9216, 1024, b=TOK)
        attd = area(10240, 2048, b=COLS)
        atto = area(12288, 3072, b=COLS)
        glrT = AREA[0:GLA_RANK, 15360:15872]
        wq = area(0, 16384, b=KT * COLS)
        pqT = W[:, 1, 0:2048].rearrange("p (a b) -> p a b", b=P)
        subT = W[:, 1, 2048:4096].rearrange("p (a b) -> p a b", b=N_KEYS)
        left = NWROW[:].rearrange("p (a b) -> p a b", b=N_KEYS)
        prob, probT, biased = (SCR[:, lo:lo + n].rearrange("p (a b) -> p a b", b=COLS)
                               for lo, n in ((0, 2048), (2048, 1024), (3072, 1024)))
        score_bank = [bank[i] for i in (0, 1, 2, 7)]
        ada = SCR[:, 0:3072].rearrange("p (a b) -> p a b", b=D)
        crow = SCR[:, 3072:4096]
        diag = SCR[:, 0:2048].rearrange("p (a b) -> p a b", b=D)
        fade = SCR[:, 0:2048].rearrange("p (a j t) -> p a j t", a=2, j=2)
        masked = SCR[:, 2048:4096].rearrange("p (a b) -> p a b", b=COLS)
        gq2 = HT[:, 0:4, :].rearrange("p (a j) t -> p a j t", a=2)
        gk2 = HT[:, 4:8, :].rearrange("p (a j) t -> p a j t", a=2)

        def scr(lo, n, dt=None, **dims):
            v = SCR[:, lo:lo + n]
            v = v.bitcast(dt) if dt else v
            return v.rearrange("p (a b) -> p a b", **dims) if dims else v

        topv, topi = scr(0, 256, b=TOPK), scr(256, 256, U32, b=TOPK)
        topf, bestv = scr(512, 64, b=TOPK), scr(576, 128, b=TOPK)
        bestp, bestf, eid = scr(704, 32, U32, b=TOPK), scr(736, 32, b=TOPK), scr(768, 32, b=TOPK)
        gates, expert = scr(800, 128, b=TOPK), scr(928, 256, U32, b=SLOTS)
        hid, wgt = scr(1184, 128), scr(1312, 128)
        hslot, gsum, ginv = scr(1440, 8), scr(1448, 8), scr(1456, 8)
        idx = scr(1464, 16, U32, b=RING)
        iota = scr(1480, CAND)
        cand, candl, cande = (scr(1536 + 2 * CAND * i, 2 * CAND, b=CAND) for i in range(3))
        ring = [W[:, 2 - 2 * (k // 4), D * (k % 4):D * (k % 4 + 1)] for k in range(RING)]
        onehot = [t[:, 0:TOPK * CAND].rearrange("p (k c) -> p k c", c=CAND)
                  for t in (levelmask[:].rearrange("p a b -> p (a b)"), SCR[:, 2048:3072])]
        acc = SCR[:, 3072:4096]
        wdiag = GROW[:, 0:P * len(SHARED)].rearrange("p (a b) -> p a b", b=P)

        x_landed = [sem(f"x_landed{b}") for b in range(NB)]
        consts_landed, c_landed, rows_landed = map(sem, ("consts_landed", "c_landed", "rows_landed"))
        row1_landed, row2_landed, row3_landed, mem_landed, sub_landed = map(sem, ("row1_landed", "row2_landed", "row3_landed", "mem_landed", "sub_landed"))
        w_landed = [sem(f"w_landed{i}") for i in range(W_SLOTS)]
        ada_landed = [sem(f"ada_landed{i}") for i in range(3)]
        rel_landed = [sem(f"rel_landed{i}") for i in range(4)]
        row_landed = [sem(f"row_landed{i}") for i in range(RING)]
        out_landed = sem("out_landed")
        w_used, ada_used, masks_ready, c_ready = map(sem, ("w_used", "ada_used", "masks_ready", "c_ready"))
        w_split_v, w_split, f_split, ident_ready, level_ready = map(sem, ("w_split_v", "w_split", "f_split", "ident_ready", "level_ready"))
        rstd_ready = sem("rstd_ready")
        scaled, squared, ff_added = map(sem, ("scaled", "squared", "ff_added"))
        ss_ready, xn_ready, tp_done, ht_ready = map(sem, ("ss_ready", "xn_ready", "tp_done", "ht_ready"))
        proj_done, proj_out = sem("proj_done"), sem("proj_out")
        post_ready, x_ready = sem("post_ready"), sem("x_ready")
        f_done, f_log = map(sem, ("f_done", "f_log"))
        diag_ready, gate_done, gate_ready = map(sem, ("diag_ready", "gate_done", "gate_ready"))
        head_ready, sc_done, mx_ready, p_ready = map(sem, ("head_ready", "sc_done", "mx_ready", "p_ready"))
        pt_done, pt_ready, pv_done, y_done = map(sem, ("pt_done", "pt_ready", "pv_done", "y_done"))
        z_done, z_log, decay_ready = map(sem, ("z_done", "z_log", "decay_ready"))
        fade_in, fade_out, gq_ready, gk_ready = map(sem, ("fade_in", "fade_out", "gq_ready", "gk_ready"))
        ga_done, ga_masked, ga_added, ga_out = map(sem, ("ga_done", "ga_masked", "ga_added", "ga_out"))
        go_done, go_sq, go_ss, go_rms, go_ready = map(sem, ("go_done", "go_sq", "go_ss", "go_rms", "go_ready"))
        gg_ready = sem("gg_ready")
        wq_landed, sub_done, top_done = map(sem, ("wq_landed", "sub_done", "top_done"))
        gate_in, gate_exp, expert_ready, staged, claimed = map(sem, ("gate_in", "gate_exp", "expert_ready", "staged", "claimed"))
        slot_free = [sem(f"slot_free{i}") for i in range(RING)]
        hid_copied, hid_ready, hid_gelu, wgt_ready = map(sem, ("hid_copied", "hid_ready", "hid_gelu", "wgt_ready"))
        wdiag_ready = sem("wdiag_ready")
        fin_x, fin_rms, fin_ready = map(sem, ("fin_x", "fin_rms", "fin_ready"))
        eps_ready = sem("eps_ready")
        act_step, dve_step, pool_step = sem("act_step"), sem("dve_step"), sem("pool_step")

        block = ctx.enter_context(nc.Block())

        chunks = [A["w_in"][i] for i in range(12)]
        for name in ("w_out", "w_mk", "w_mv", "w_mq", "w_mo"):
            chunks += [A[name][i] for i in range(4)]
        for r in range(2):
            chunks += [A["w_ff1"][8 * r + i] for i in range(8)]
            chunks += [A["w_ff2"][4 * q + 2 * r + k] for q in range(4) for k in range(2)]
        chunks += [A["w_in_2"][i] for i in range(10)] + [A["w_out_2"][i] for i in range(2)]
        assert len(chunks) == C_END
        splits = [c for c in range(C_OUT2) if not C_MK <= c < C_MQ]

        by_vector = [C_IN + i for i in (3, 5, 7, 9, 11)] + [C_MQ + 1, C_MQ + 3, C_MO + 3] + list(range(C_FF1 + 3, C_IN2))
        by_vector += [C_IN2 + i for i in (3, 4, 5, 8)]
        by_pool = [c for c in splits if c not in by_vector]

        def split_parts(c):
            s = c % W_SLOTS
            return W[:, s, 0:KT * HALF], WS[:, s, KT * HALF:2 * KT * HALF], WS[:, s, 0:KT * HALF]

        by_feature, by_token = [2, 2], [0, 4]
        ends = (by_feature * 2 + by_token) * 2 + by_token * 2 + by_feature * 2 + [0, 2] * 2 + by_feature * 2
        ends += by_token * 2 + (by_feature * 4 + [0, 0, 0, 4] * 2) * 2 + by_feature + [5, 2] + [2, 1] + by_token * 2
        assert len(ends) == C_OUT2 and sum(ends) == G_OUT2

        def used(c):
            if ends[c]:
                return proj_done, sum(ends[:c + 1])
            return w_used, ends[:c + 1].count(0)

        @block.sync
        def _(sp):
            for b in range(NB):
                sp.dma_start(X[:, b, :], A["x"][b]).then_inc(x_landed[b], 16)
            sp.dma_start(gcol[:], A["gain_cols"]).then_inc(consts_landed, 16)
            sp.dma_start(bfcol[:], A["b_fgt"]).then_inc(consts_landed, 16)
            sp.dma_start(wf, A["w_fgt"]).then_inc(consts_landed, 16)
            sp.dma_start(bada[:], A["b_ada"]).then_inc(consts_landed, 16)
            sp.dma_start(gbcol[:], A["gla_gate_bias"]).then_inc(consts_landed, 16)
            sp.dma_start(up[:], A["gla_gate_up"]).then_inc(consts_landed, 16)
            sp.dma_start(sinks[:], A["sinks"].partition_broadcast(P)).then_inc(consts_landed, 16)
            rows = 0
            for c in range(C_END):
                if c >= W_SLOTS:
                    sp.wait_ge(*used(c - W_SLOTS))
                width = chunks[c].shape[-1]
                sp.dma_start(W[:, c % W_SLOTS, 0:width], chunks[c]).then_inc(w_landed[c % W_SLOTS], 16)
                if c == 2:
                    sp.dma_start(crow, A["c"].partition_broadcast(P)).then_inc(c_landed, 16)
                for r in range(rows, {2: 3}.get(c, min(48, rows + 5) if c > 2 else 0)):
                    if r >= 3:
                        sp.wait_ge(ada_used, r - 2)
                    sp.dma_start(ada[:, r % 3, :], A["w_ada"][r]).then_inc(ada_landed[r % 3], 16)
                    rows = r + 1
                if c == C_IN + 5:
                    sp.dma_start(GROW[:], A["gain_rows"][0].partition_broadcast(P)).then_inc(rows_landed, 16)
                    for i in range(4):
                        sp.dma_start(NWROW[:, i * P:(i + 1) * P], A["gla_norm"].partition_broadcast(P)).then_inc(rows_landed, 16)
                if c == C_OUT + 2:
                    for h in range(HEADS):
                        if h == 2:
                            sp.wait_ge(f_done, 1)
                        if h >= 4:
                            sp.wait_ge(mx_ready, U_CHK + NB * (h - 3))
                        sp.dma_start(relb[:, h % 4, :], bass.AP(A["rel"].tensor, h * REL_W, [[1, P], [1, TOK]])).then_inc(rel_landed[h % 4], 16)
                    sp.wait_ge(y_done, U_MEM)
                    sp.dma_start(MX, A["mem"]).then_inc(mem_landed, 16)
                if c == C_MO:
                    sp.wait_ge(x_ready, NB)
                    sp.dma_start(GROW[:], A["gain_rows"][1].partition_broadcast(P)).then_inc(row1_landed, 16)
                if c == C_FF1 + 8:
                    sp.wait_ge(x_ready, 2 * NB)
                    sp.dma_start(GROW[:], A["gain_rows"][2].partition_broadcast(P)).then_inc(row2_landed, 16)
            sp.wait_ge(proj_done, G_OUT2)
            sp.dma_start(subT, A["subkeys"]).then_inc(sub_landed, 16)
            sp.dma_start(FINROW[:], A["gain_rows"][3].partition_broadcast(P)).then_inc(row3_landed, 16)
            sp.wait_ge(gq_ready, len(GLA_HALVES))
            sp.wait_ge(ga_done, NB * 8)
            sp.dma_start(wq[:, 0, :], A["w_pq"][0]).then_inc(wq_landed, 16)
            sp.wait_ge(go_ready, NB)
            for i in range(1, 4):
                sp.dma_start(wq[:, i, :], A["w_pq"][i]).then_inc(wq_landed, 16)
            for b in range(NB):
                sp.wait_ge(fin_ready, b + 1)
                sp.dma_start(out[b], XN[:, b, :]).then_inc(out_landed, 16)
            sp.wait_ge(out_landed, 16 * NB)

        @block.gpsimd
        def _(pool):
            steps = [0]

            def link(ins):
                steps[0] += 1
                ins.then_inc(pool_step, 1)
                pool.wait_ge(pool_step, steps[0])

            def split(c):
                raw, high, low = split_parts(c)
                pool.wait_ge(w_landed[c % W_SLOTS], 16 * (c // W_SLOTS + 1))
                link(pool.tensor_copy(high, raw))
                pool.tensor_tensor(low, raw, high.bitcast(F32), ALU.subtract).then_inc(w_split, 1)

            pool.memset(epsc[:], EPS).then_inc(eps_ready, 1)
            link(pool.memset(ident[:], 0.0))
            pool.affine_select(ident[:], ident[:], [[-1, P]], ALU.not_equal, 1.0, 0, 1).then_inc(ident_ready, 1)
            split(0)
            split(1)
            pool.wait_ge(consts_landed, 112)
            link(pool.tensor_copy(WFH[:], wf))
            pool.tensor_tensor(WFL[:], wf, WFH[:].bitcast(F32), ALU.subtract).then_inc(f_split, 1)
            split(2)
            pool.memset(ones[:], 1.0)
            pool.memset(onesb[:], 1.0)
            pool.memset(headsel[:], 0.0)
            link(pool.memset(winb[:], 0.0))
            pool.wait_ge(ident_ready, 1)
            pool.tensor_copy(identb[:], ident[:])
            link(pool.affine_select(winb[:, P:2 * P], winb[:, P:2 * P], [[-1, P]], ALU.is_ge, NEG, 0, 1))
            link(pool.affine_select(winb[:, 0:P], winb[:, 0:P], [[1, P]], ALU.is_gt, NEG, 0, -1))
            for part in range(3):
                rows = headsel[32 * part:32 * part + HEADS, :]
                link(pool.affine_select(rows, rows, [[-1, HEADS]], ALU.not_equal, 1.0, 0, 1))
            pool.memset(cpos, 0.0)
            link(pool.memset(cneg, 0.0))
            pool.sem_inc(masks_ready, 1)
            for c in by_pool[3:]:
                split(c)

            pool.wait_ge(proj_done, G_OUT2)
            link(pool.memset(levelmask[:], 1.0))
            link(pool.tensor_copy(levelmask[:, 0, :], ident[:]))
            for n, m in enumerate(GLA_HALVES[:7]):
                g = levelmask[:, n + 1, :].rearrange("p (g r) -> p g r", r=2 * m)
                G = P // (2 * m)
                link(pool.affine_select(g, g, [[0, G], [1, 2 * m]], ALU.is_ge, 0.0, -m, 0))
                link(pool.affine_select(g, g, [[-2 * m, G], [0, 2 * m]], ALU.is_ge, 0.0, 0, 1))
                link(pool.affine_select(g, g, [[2 * m, G], [0, 2 * m]], ALU.is_ge, 0.0, m - 1, -1))
            pool.sem_inc(level_ready, 1)

            pool.wait_ge(y_done, U_END)
            def keys(l):
                pool.wait_ge(fade_out, l + 1)
                if l >= 2:
                    pool.wait_ge(ga_done, NB * l)
                pool.tensor_tensor(gk2[:, l % 2], gkT, fade[:, l % 2], ALU.mult).then_inc(gk_ready, 1)

            keys(0)
            keys(1)
            pool.wait_ge(ga_out, NB)
            for l in range(7):
                for b in range(NB):
                    n = NB * l + b
                    pool.wait_ge(ga_masked, n + 1)
                    if l > 0:
                        pool.wait_ge(ga_added, n - NB + 1)
                    pool.tensor_tensor(attd[:, b, :], attd[:, b, :], masked[:, n % 4, :], ALU.add).then_inc(ga_added, 1)
                keys(l + 2)
            pool.wait_ge(y_done, U_END)
            pool.wait_ge(go_ready, NB)
            pool.iota(iota, [[1, CAND]], 0, 0, allow_small_or_imprecise_dtypes=True).then_inc(claimed, 1)

            for b in range(NB):
                for table in range(2):
                    base = TURNS * (2 * b + table)
                    src = A["peer_v"] if table else A["peer_u"]

                    def gather(it, weights_below=False):
                        pool.wait_ge(expert_ready, it + (QUARTERS * b + 1))
                        for turn in range(4):
                            pool.tensor_copy(idx[:, turn % 2, :], expert[:, b % 2, bass.ds(it * (4 * RING) + turn * RING, RING)]).then_inc(staged, 1)
                            pool.wait_ge(staged, it * 4 + (base + turn + 1))
                            for k in range(RING):
                                pool.wait_ge(slot_free[k], it * 4 + (base + turn + 1))
                                if weights_below and turn == 0 and k % 4 == 0:
                                    pool.wait_ge(proj_done, late("out", NB - 1, k // 4) + 1)
                                pool.sem_inc(claimed, 1)
                                pool.indirect_dma_start(ring[k], None, src, bass.IndirectOffsetOnAxis(ap=idx[:, turn % 2, k:k + 1], axis=0)).then_inc(row_landed[k], 16)

                    if b == 0 and table == 0:
                        gather(0, weights_below=True)
                        with pool.Fori(1, QUARTERS) as it:
                            gather(it)
                    else:
                        with pool.Fori(0, QUARTERS) as it:
                            gather(it)

        @block.scalar
        def _(act):
            steps = [0]

            def link(ins):
                steps[0] += 1
                ins.then_inc(act_step, 1)
                act.wait_ge(act_step, steps[0])

            def root(i, width):
                act.activation(ssq[:, i:i + 1], ssq[:, i:i + 1], ACT.Sqrt, scale=1.0 / width, bias=epsc[:]).then_inc(ss_ready, 1)

            def normed(n, b):
                i = STATS[n] + b
                act.wait_ge(rstd_ready, NB * NORMED.index(n) + b + 1)
                act.activation(XN[:, b, :], X[:, b, :], ACT.Copy, scale=rstd[:, i:i + 1]).then_inc(xn_ready, 1)

            def squares(n, b):
                if n == N_MIX:
                    act.wait_ge(x_landed[b], 16)
                else:
                    done = {N_MEMPRE: 0, N_FF: 1, N_ATT2: 2, N_PEER: 3}[n]
                    act.wait_ge(x_ready, NB * done + b + 1)
                i = STATS[n] + b
                link(act.activation(XN[:, b, :], X[:, b, :], ACT.Square, accum_out=ssq[:, i:i + 1]))
                root(i, D)

            def transposed(n, scale, bias=None):
                for k in range(KT):
                    j = KT * n + k
                    act.wait_ge(tp_done, j + 1)
                    src, high = bank[4 + j % 4][:], HTH[:, k, :]
                    if bias is not None:
                        ins = act.activation(src, src, ACT.Identity, scale=scale[:, k:k + 1], bias=bias[:, k:k + 1])
                    elif scale is not None:
                        ins = act.activation(high, src, ACT.Copy, scale=scale[:, k:k + 1])
                    else:
                        ins = act.copy(high, src)
                    ins.then_inc(scaled, 1)

            def evac(g, dst, rows=P, width=COLS, scale=1.0, lo=0):
                act.wait_ge(proj_done, g + 1)
                src = bank[g % 4][0:rows, lo:lo + width]
                act.activation(dst, src, ACT.Copy, scale=scale).then_inc(proj_out, 1)

            def evac_post(s, first, following):
                for half in range(2):
                    for b in range(NB):
                        g = first + NB * half + b
                        to, t = XN[:, b, half * COLS:(half + 1) * COLS], psq[:, s, b, half:half + 1]
                        if s == 2:
                            act.wait_ge(ff_added, NB * half + b + 1)
                            act.activation(bank[NB * half + b][:], to, ACT.Square, accum_out=t).then_inc(proj_out, 1)
                        else:
                            src = bank[g % 4][:]
                            act.wait_ge(proj_done, g + 1)
                            link(act.copy(to, src))
                            act.activation(src, src, ACT.Square, accum_out=t).then_inc(proj_out, 1)
                        if half == 1:
                            act.wait_ge(proj_out, g + 1)
                            link(act.activation(t, t, ACT.Identity, bias=psq[:, s, b, 0:1]))
                            act.activation(t, t, ACT.Sqrt, scale=1.0 / D, bias=epsc[:]).then_inc(post_ready, 1)
                            if following is not None:
                                if b >= 1:
                                    squares(following, b - 1)
                                if b >= 2:
                                    normed(following, b - 2)
                if following is not None:
                    squares(following, NB - 1)
                    normed(following, NB - 2)
                    normed(following, NB - 1)

            def attention(lo, hi):
                for u in range(lo, hi + 4):
                    v = u - 4
                    if v >= lo:
                        n = unit(v)[3]
                        act.wait_ge(pt_done, v + 1)
                        if v - 2 >= lo:
                            act.wait_ge(pv_done, v - 1)
                        act.copy(probT[:, v % 2, 0:n], bank[3 + v % 2][:, 0:n]).then_inc(pt_ready, 1)
                    if u < hi:
                        kind, h, b, n = unit(u)
                        src = biased[:, u % 2, 0:n] if kind == "chk" else score_bank[u % 4][:, 0:n]
                        act.wait_ge(mx_ready, u + 1)
                        if u - 4 >= lo:
                            act.wait_ge(pt_done, u - 3)
                        if kind == "swa":
                            act.activation(skx[:, u:u + 1], sinks[:, h:h + 1], ACT.Exp, bias=nmax[:, u:u + 1])
                        act.activation(prob[:, u % 4, 0:n], src, ACT.Exp, bias=nmax[:, u:u + 1],
                                       accum_out=rsum[:, u:u + 1]).then_inc(p_ready, 1)

            act.wait_ge(eps_ready, 1)
            for b in range(NB):
                squares(N_MIX, b)
            act.wait_ge(c_landed, 16)
            act.activation(crow, crow, ACT.Silu).then_inc(c_ready, 1)
            act.wait_ge(consts_landed, 112)
            transposed(N_MIX, gcol[:, GC_MIX, :])
            for j in range(4):
                evac(G_IN + j, fqT[:, j, :], scale=HD ** -0.5)
            fz, fe = XN[0:72, 0, 0:512], XN[0:72, 0, 512:1024]
            act.wait_ge(f_done, 1)
            link(act.activation(fz, bank[4][0:72, :], ACT.Identity, bias=bfcol[0:72, :]))
            link(act.activation(fe, fz, ACT.Abs))
            link(act.activation(fe, fe, ACT.Exp, scale=-1.0))
            act.activation(fe, fe, ACT.Ln, bias=1.0).then_inc(f_log, 1)
            for j in range(4):
                evac(G_IN + 4 + j, fkT[:, j, :])
            for b in range(NB):
                evac(G_IN + 8 + b, fv[:, b, :])
            for j in range(4):
                evac(G_IN + 12 + j, cqT[:, j, :], scale=HD ** -0.5)
            for j in range(4):
                evac(G_IN + 16 + j, ckT[:, j, :])
            for b in range(NB):
                evac(G_IN + 20 + b, cv[:, b, :])
            attention(U_FOX, U_MEM)

            act.wait_ge(y_done, U_MEM)
            for b in range(NB):
                for half in range(2):
                    i = STATS[N_Y] + 2 * b + half
                    link(act.activation(HT[:, 2 * b + half, :], XN[:, b, half * COLS:(half + 1) * COLS], ACT.Square,
                                        accum_out=ssq[:, i:i + 1]))
                    root(i, D // 2)
            act.wait_ge(mem_landed, 16)
            for b in range(MB):
                i = STATS[N_MEM] + b
                link(act.activation(AREA[:, 2048 + D * b:2048 + D * (b + 1)], MX[:, b, :], ACT.Square,
                                    accum_out=ssq[:, i:i + 1]))
                root(i, D)
            transposed(N_Y, gcol[:, GC_Y, :])
            evac_post(0, G_OUT, None)
            for k in range(KT):
                act.wait_ge(tp_done, KT * N_MEM + k + 1)
                act.activation(memT[:, k, :], bank[4 + k % 4][:, 0:MEM], ACT.Copy,
                               scale=gcol[:, GC_MEMKV, k:k + 1]).then_inc(ht_ready, 1)
            for b in range(NB):
                squares(N_MEMPRE, b)
                if b > 0:
                    normed(N_MEMPRE, b - 1)
            normed(N_MEMPRE, NB - 1)
            for j in range(8):
                evac(G_MK + j, mkT[:, j, :], width=MEM)
            for n in range(2):
                for b in range(MB):
                    evac(G_MV + MB * n + b, mv[:, b, n * COLS:(n + 1) * COLS])
            transposed(N_MEMPRE, gcol[:, GC_MEMPRE, :])
            for j in range(8):
                evac(G_MQ + j, mqT[:, j, :], scale=MEM_HD ** -0.5)
            attention(U_MEM, U_SWA)
            transposed(N_MEMY, None)
            evac_post(1, G_MO, N_FF)
            transposed(N_FF, gcol[:, GC_FF, :])
            for r in range(2):
                for j in range(FF_T):
                    g = G_FF1 + G_ROUND * r + j
                    act.wait_ge(proj_done, g + 1)
                    link(act.activation(bank[g % 4][:], bank[g % 4][:], ACT.Relu))
                    act.activation(bank[g % 4][:], bank[g % 4][:], ACT.Square).then_inc(squared, 1)
                if r == 0:
                    for i in range(2 * NB):
                        act.wait_ge(proj_done, G_FF2 + i + 1)
                        act.copy(XN[:, i % NB, (i // NB) * COLS:(i // NB + 1) * COLS], bank[i][:]).then_inc(proj_out, 1)
            evac_post(2, G_FF2 + G_ROUND, N_ATT2)
            transposed(N_ATT2, scol[:, 0, :], mod[:, 0:8])

            g = G_IN2
            for j in range(4):
                evac(g + j, aqT[:, j, :], scale=HD ** -0.5)
            evac(g + 4, akT)
            for b in range(NB):
                evac(g + 5 + b, av[:, b, :], width=P, lo=P)
            for j in range(2):
                evac(g + 9 + j, gqT[:, j, :], scale=HD ** -0.5)
            for j in range(2):
                evac(g + 11 + j, gkT[:, j, :])
            evac(g + 13, glrT, rows=GLA_RANK)
            for j in range(2):
                act.wait_ge(z_done, j + 1)
                link(act.activation(decay[:, j, :], bank[4 + j][:], ACT.Identity, bias=gbcol[:, j:j + 1]))
            link(act.activation(fade[:, 0], decay, ACT.Abs))
            link(act.activation(fade[:, 0], fade[:, 0], ACT.Exp, scale=-1.0))
            act.activation(fade[:, 0], fade[:, 0], ACT.Ln, bias=1.0).then_inc(z_log, 1)
            for b in range(NB):
                evac(g + 14 + b, gv[:, b, :])
            for b in range(NB):
                act.wait_ge(proj_done, g + 18 + b + 1)
                act.activation(gg[:, b, :], bank[(g + 18 + b) % 4][:], ACT.Silu).then_inc(proj_out, 1)
            for i in range(4):
                act.wait_ge(gate_done, i + 1)
                act.copy(GATE[:, i // 2, (i % 2) * COLS:(i % 2 + 1) * COLS], bank[4 + i][:]).then_inc(gate_ready, 1)
            attention(U_SWA, U_END)
            for l in range(len(GLA_HALVES)):
                act.wait_ge(fade_in, l + 1)
                act.activation(fade[:, l % 2], fade[:, l % 2], ACT.Exp, scale=-1.0 / GLA_TAU).then_inc(fade_out, 1)
            for i in range(6):
                act.wait_ge(ga_done, NB * 8 + i + 1)
                for r in range(2):
                    ins = act.copy(atto[:, i, 2 * P * r:2 * P * (r + 1)], bank[2 * (i % 4) + r][:, 0:2 * P])
                ins.then_inc(ga_out, 1)
            for b in range(NB):
                act.wait_ge(go_done, b + 1)
                act.activation(masked[:, b, :], bank[4 + b][:], ACT.Square).then_inc(go_sq, 1)
                act.wait_ge(go_ss, b + 1)
                act.activation(ssy[:, b, :], ssy[:, b, :], ACT.Sqrt, scale=1.0 / GLA_DV, bias=epsc[:]).then_inc(go_rms, 1)
            def evac_late(kind, b):
                for i in range(16 if kind == "query" else 2):
                    g = late(kind, b, i)
                    half = slice(i * COLS, (i + 1) * COLS)
                    if kind == "mixed":
                        evac(g, HT[:, 4 * i:4 * i + 4, b * P:(b + 1) * P])
                    elif kind in ("out", "token"):
                        evac(g, XN[:, b, half])
                    elif kind == "query":
                        if b > 0 and i % 4 == 0:
                            act.wait_ge(sub_done, QUARTERS * (b - 1) + i // 4 + 1)
                        evac(g, pqT[:, i, :], width=P)
                    else:
                        act.wait_ge(proj_done, g + 1)
                        for j in range(4):
                            k = 4 * i + j
                            ins = act.activation(HT[:, k, b * P:(b + 1) * P], bank[g % 4][:, j * P:(j + 1) * P], ACT.Identity,
                                                 scale=scol[:, 1, k:k + 1], bias=mod[:, 24 + k:25 + k])
                        ins.then_inc(proj_out, 1)

            def evac_queries(b):
                evac_late("turn", b)
                evac_late("query", b)
                evac_late("token", b)

            def exponentials(b):
                act.wait_ge(gate_in, b + 1)
                act.activation(gates, gates, ACT.Exp).then_inc(gate_exp, 1)

            def gelus(b):
                act.wait_ge(hid_ready, b + 1)
                act.activation(hid, hid, ACT.Gelu).then_inc(hid_gelu, 1)

            def final_squares(b):
                act.wait_ge(fin_x, b + 1)
                i = 30 + b
                link(act.activation(XN[:, b, :], X[:, b, :], ACT.Square, accum_out=ssq[:, i:i + 1]))
                act.activation(ssq[:, i:i + 1], ssq[:, i:i + 1], ACT.Sqrt, scale=1.0 / D, bias=epsc[:]).then_inc(fin_rms, 1)

            for kind, b in (("mixed", 0), ("mixed", 1), ("out", 0), ("mixed", 2), ("mixed", 3)):
                evac_late(kind, b)
            squares(N_PEER, 0)
            normed(N_PEER, 0)
            evac_late("out", 1)
            evac_late("turn", 0)
            squares(N_PEER, 1)
            normed(N_PEER, 1)
            evac_late("query", 0)
            evac_late("token", 0)
            for i in range(2):
                for b in (2, 3):
                    evac(late("out", b, i), XN[:, b, i * COLS:(i + 1) * COLS])
            evac_queries(1)
            exponentials(0)
            for b in range(NB):
                gelus(b)
                act.wait_ge(wgt_ready, b + 1)
                base = TURNS * (2 * b + 1)
                with act.Fori(0, TURNS) as it:
                    for i, k in enumerate(SHARED):
                        act.wait_ge(slot_free[k], it + (base + 1))
                        act.activation(wdiag[:, i, :], ident[:], ACT.Copy,
                                       scale=wgt[:, bass.ds(it * RING + k, 1)]).then_inc(wdiag_ready, 1)
                if b + 1 < NB:
                    exponentials(b + 1)
                final_squares(b)
                if b == 0:
                    for i in (2, 3):
                        squares(N_PEER, i)
                        normed(N_PEER, i)
                    evac_queries(2)
                    evac_queries(3)

        @block.tensor
        def _(pe):
            def transposes(n, src, blocks):
                for k in range(KT):
                    j = KT * n + k
                    if j >= 4:
                        pe.wait_ge(ht_ready, j - 3)
                    for b in range(blocks):
                        ins = pe.transpose(bank[4 + j % 4][:, b * P:(b + 1) * P], src[:, b, k * P:(k + 1) * P], ident[:])
                    ins.then_inc(tp_done, 1)

            def begin(g, at=None):
                if g >= 4:
                    pe.wait_ge(proj_out, g - 3)
                return bank[g % 4 if at is None else at]

            def arrived(c):
                if c in by_vector:
                    pe.wait_ge(w_split_v, by_vector.index(c) + 1)
                else:
                    pe.wait_ge(w_split, by_pool.index(c) + 1)
                return split_parts(c)[1:]

            def three(ps, lhs, rhs, start, stop):
                pe.matmul(ps, lhs[0], rhs[0], start=start, stop=False)
                pe.matmul(ps, lhs[0], rhs[1], start=False, stop=False)
                return pe.matmul(ps, lhs[1], rhs[0], start=False, stop=stop)

            def tile_T(c, g, x, lo, m, width, wait=None):
                w, ps = arrived(c), begin(g)
                for k in range(KT):
                    if wait is not None:
                        pe.wait_ge(ht_ready, wait + k + 1)
                    ins = three(ps[0:m, 0:width], [t[:, k * HALF + lo:k * HALF + lo + m] for t in w],
                                [t[:, k, 0:width] for t in x], k == 0, k == KT - 1)
                ins.then_inc(proj_done, 1)

            def tiles_T(c, g, x, n, width, wait=None):
                for j in range(n):
                    tile_T(c + j // 2, g + j, x, j % 2 * P, P, width, wait if j == 0 else None)

            def tiles_tok(c, g, x, blocks, by_block=False):
                order = [(half, b) for half in range(2) for b in range(blocks)]
                for half, b in sorted(order, key=lambda hb: hb[1]) if by_block else order:
                    w = arrived(c + half)
                    ps = begin(g + b) if half == 0 else bank[(g + b) % 4]
                    for k in range(KT):
                        ins = three(ps[:, half * HALF:(half + 1) * HALF], [t[:, k, b * P:(b + 1) * P] for t in x],
                                    [t[:, k * HALF:(k + 1) * HALF] for t in w], k == 0, k == KT - 1)
                    if half == 1:
                        ins.then_inc(proj_done, 1)
                    elif b == blocks - 1:
                        ins.then_inc(w_used, 1)

            def plain_tok(c, x, b, ps):
                pe.wait_ge(w_landed[c % W_SLOTS], 16 * (c // W_SLOTS + 1))
                for k in range(KT):
                    ins = pe.matmul(ps, x[:, k, b * P:(b + 1) * P], W[:, c % W_SLOTS, k * COLS:(k + 1) * COLS],
                                    start=(k == 0), stop=(k == KT - 1))
                return ins

            def attention(lo, hi):
                def scores(u):
                    kind, h, b, n = unit(u)
                    ps = score_bank[u % 4][:, 0:n]
                    if u - 4 >= lo:
                        pe.wait_ge(p_ready, u - 3)
                    q = slice(b * P, (b + 1) * P)
                    if kind == "fox":
                        r = slice((h % 2) * HD, (h % 2 + 1) * HD)
                        pe.wait_ge(head_ready, h + 1)
                        pe.matmul(ps, fqT[r, h // 2, q], fkT[r, h // 2, 0:n], start=True, stop=False)
                        pe.matmul(ps, cposh[h % 2][0:72, q], onesb[0:72, 0:n], start=False, stop=False)
                        pe.matmul(ps, onesb[0:72, 0:P], cnegh[h % 2][0:72, 0:n], start=False, stop=False)
                        ins = pe.matmul(score_bank[u % 4][:, n - P:n], identb[:], winb[:, P:2 * P], start=False, stop=True)
                    elif kind == "chk":
                        r = slice((h % 2) * HD, (h % 2 + 1) * HD)
                        ins = pe.matmul(ps, cqT[r, h // 2, q], ckT[r, h // 2, 0:n], start=True, stop=True)
                    elif kind == "mem":
                        for c in range(2):
                            ins = pe.matmul(ps, mqT[:, 2 * h + c, q], mkT[:, 2 * h + c, :], start=(c == 0), stop=(c == 1))
                    else:
                        r = slice((h // 4) * HD, (h // 4 + 1) * HD)
                        pe.matmul(ps, aqT[r, h % 4, q], akT[r, (b + 1) * P - n:(b + 1) * P], start=True, stop=False)
                        ins = pe.matmul(ps, identb[:], winb[:, 2 * P - n:2 * P], start=False, stop=True)
                    ins.then_inc(sc_done, 1)

                def turn(u):
                    n = unit(u)[3]
                    pe.wait_ge(p_ready, u + 1)
                    if u - 2 >= lo:
                        pe.wait_ge(pt_ready, u - 1)
                    for j in range(n // P):
                        ins = pe.transpose(bank[3 + u % 2][:, j * P:(j + 1) * P], prob[:, u % 4, j * P:(j + 1) * P], ident[:])
                    ins.then_inc(pt_done, 1)

                def mix(u):
                    kind, h, b, n = unit(u)
                    pe.wait_ge(pt_ready, u + 1)
                    if u - 2 >= lo:
                        pe.wait_ge(y_done, u - 1)
                    for j in range(n // P):
                        if kind == "fox":
                            v = fv[:, j, h * HD:(h + 1) * HD]
                        elif kind == "chk":
                            v = cv[:, j, h * HD:(h + 1) * HD]
                        elif kind == "mem":
                            v = mv[:, j, h * MEM_HD:(h + 1) * MEM_HD]
                        else:
                            v = av[:, b + 1 - n // P + j, (h // 4) * HD:(h // 4 + 1) * HD]
                        ins = pe.matmul(bank[5 + u % 2][:, 0:v.shape[-1]], probT[:, u % 2, j * P:(j + 1) * P], v,
                                        start=(j == 0), stop=(j == n // P - 1))
                    ins.then_inc(pv_done, 1)

                for u in range(lo, hi + 4):
                    if u < hi:
                        scores(u)
                    if lo <= u - 3 < hi:
                        turn(u - 3)
                    if u - 4 >= lo:
                        mix(u - 4)

            h = (HTH, HTL)
            pe.wait_ge(ident_ready, 1)
            pe.wait_ge(xn_ready, BLOCKS[N_MIX] + 4)
            transposes(N_MIX, XN, NB)
            tiles_T(C_IN, G_IN, h, 4, TOK, wait=0)
            pe.wait_ge(f_split, 1)
            for k in range(KT):
                ins = three(bank[4][0:72, :], [t[:, k * 72:(k + 1) * 72] for t in (WFH, WFL)], [t[:, k, :] for t in h],
                            k == 0, k == KT - 1)
            ins.then_inc(f_done, 1)
            tiles_T(C_IN + 2, G_IN + 4, h, 4, TOK)
            tiles_tok(C_IN + 4, G_IN + 8, h, NB)
            tiles_T(C_IN + 6, G_IN + 12, h, 8, TOK)
            tiles_tok(C_IN + 10, G_IN + 20, h, NB)
            pe.wait_ge(proj_out, G_OUT)
            pe.wait_ge(f_log, 1)
            pe.wait_ge(masks_ready, 1)
            attention(U_FOX, U_MEM)

            pe.wait_ge(xn_ready, BLOCKS[N_Y] + 4)
            transposes(N_Y, XN, NB)
            pe.wait_ge(ht_ready, KT * (N_Y + 1))
            for n in range(2):
                tiles_tok(C_OUT + 2 * n, G_OUT + NB * n, h, NB)
            pe.wait_ge(xn_ready, BLOCKS[N_MEM] + MB)
            transposes(N_MEM, MX, MB)
            def plain_half(c):
                pe.wait_ge(w_landed[c % W_SLOTS], 16 * (c // W_SLOTS + 1))
                return W[:, c % W_SLOTS, 0:KT * HALF]

            for j in range(8):
                w, ps = plain_half(C_MK + j // 2), begin(G_MK + j)[:, 0:MEM]
                for k in range(KT):
                    if j == 0:
                        pe.wait_ge(ht_ready, KT * N_MEM + k + 1)
                    at = k * HALF + j % 2 * P
                    ins = pe.matmul(ps, w[:, at:at + P], memT[:, k, :], start=(k == 0), stop=(k == KT - 1))
                ins.then_inc(proj_done, 1)
            for i in range(4):
                w, half = plain_half(C_MV + i), i % 2
                for b in range(MB):
                    g = G_MV + MB * (i // 2) + b
                    ps = begin(g) if half == 0 else bank[g % 4]
                    for k in range(KT):
                        ins = pe.matmul(ps[:, half * HALF:(half + 1) * HALF], memT[:, k, b * P:(b + 1) * P], w[:, k * HALF:(k + 1) * HALF],
                                        start=(k == 0), stop=(k == KT - 1))
                    if half == 1:
                        ins.then_inc(proj_done, 1)
                if half == 0:
                    ins.then_inc(w_used, 1)
            pe.wait_ge(xn_ready, BLOCKS[N_MEMPRE] + 4)
            transposes(N_MEMPRE, XN, NB)
            tiles_T(C_MQ, G_MQ, h, 8, TOK, wait=KT * N_MEMPRE)
            pe.wait_ge(proj_out, G_MO)
            attention(U_MEM, U_SWA)
            pe.wait_ge(y_done, U_SWA)
            transposes(N_MEMY, XN, NB)
            pe.wait_ge(ht_ready, KT * (N_MEMY + 1))
            for n in range(2):
                tiles_tok(C_MO + 2 * n, G_MO + NB * n, h, NB, by_block=(n == 1))
            pe.wait_ge(xn_ready, BLOCKS[N_FF] + 4)
            transposes(N_FF, XN, NB)
            for r in range(2):
                tiles_T(C_FF1 + C_ROUND * r, G_FF1 + G_ROUND * r, h, FF_T, TOK, wait=None if r else KT * N_FF)
                first = G_FF2 + G_ROUND * r
                pe.wait_ge(proj_out, first)
                for n in range(2):
                    order = [(i, b) for i in range(4) for b in range(NB)]
                    if r == n == 1:
                        order = order[:2 * NB] + [(i, b) for b in range(NB) for i in (2, 3)]
                    for i, b in order:
                        q, k0 = i // 2, KT * (i % 2)
                        w = arrived(C_FF2 + C_ROUND * r + 4 * n + i)
                        at = NB * n + b
                        if i == 0:
                            begin(first + at)
                        for k in range(KT):
                            ins = three(bank[at][:, q * HALF:(q + 1) * HALF], [t[:, k0 + k, b * P:(b + 1) * P] for t in (FHH, FHL)],
                                        [t[:, k * HALF:(k + 1) * HALF] for t in w], k0 + k == 0, k0 + k == FF_T - 1)
                        if i == 3:
                            ins.then_inc(proj_done, 1)
                        elif b == NB - 1:
                            ins.then_inc(w_used, 1)
            pe.wait_ge(xn_ready, BLOCKS[N_ATT2] + 4)
            transposes(N_ATT2, XN, NB)
            g, c = G_IN2, C_IN2
            tiles_T(c, g, h, 4, TOK, wait=KT * N_ATT2)
            tile_T(c + 2, g + 4, h, 0, P, TOK)
            for b in range(NB):
                w, ps = arrived(c + 2), begin(g + 5 + b)
                for k in range(KT):
                    ins = three(ps[:, 0:HALF], [t[:, k, b * P:(b + 1) * P] for t in h], [t[:, k * HALF:(k + 1) * HALF] for t in w],
                                k == 0, k == KT - 1)
                ins.then_inc(proj_done, 1)
            tiles_T(c + 3, g + 9, h, 4, TOK)
            tile_T(c + 5, g + 13, h, 0, GLA_RANK, TOK)
            pe.wait_ge(proj_out, g + 14)
            for j in range(2):
                pe.matmul(bank[4 + j][:], up[:, j * P:(j + 1) * P], glrT, start=True, stop=True).then_inc(z_done, 1)
            for n in range(2):
                tiles_tok(c + 6 + 2 * n, g + 14 + NB * n, h, NB)
            pe.wait_ge(proj_out, G_OUT2)
            pe.wait_ge(z_log, 1)
            for i in range(4):
                pe.wait_ge(diag_ready, i // 2 + 1)
                pe.matmul(bank[4 + i][:], ones[:], diag[:, i // 2, (i % 2) * COLS:(i % 2 + 1) * COLS],
                          start=True, stop=True).then_inc(gate_done, 1)
            pe.wait_ge(gate_ready, 4)
            attention(U_SWA, U_END)

            def pair(k, q, ki, qi, h):
                r = slice((h % 2) * HD, (h % 2 + 1) * HD)
                return k[r, h // 2, ki * P:(ki + 1) * P], q[r, h // 2, qi * P:(qi + 1) * P]

            pe.wait_ge(y_done, U_END)
            for n in range(8 * NB):
                l, b = n // NB, n % NB
                if l == 0:
                    kk, qq = gkT, gqT
                else:
                    kk, qq = gk2[:, (l - 1) % 2], gq2[:, (l - 1) % 2]
                    if b == 0:
                        pe.wait_ge(gq_ready, l)
                        pe.wait_ge(gk_ready, l)
                    pe.wait_ge(ga_out, b + 1) if l == 1 else pe.wait_ge(ga_masked, n - 2 * NB + 1)
                for h in range(GLA_HEADS):
                    k, q = pair(kk, qq, b, b, h)
                    ins = pe.matmul(bank[2 * (n % 4) + h % 2][:, (h // 2) * P:(h // 2 + 1) * P], k, q, start=True, stop=True)
                ins.then_inc(ga_done, 1)
            for i, (ki, qi) in enumerate([(0, 1), (2, 3), (0, 2), (0, 3), (1, 2), (1, 3)]):
                l = 8 if i < 2 else 9
                pe.wait_ge(gq_ready, l)
                pe.wait_ge(gk_ready, l)
                if i < 4:
                    pe.wait_ge(ga_masked, 6 * NB + i + 1)
                else:
                    pe.wait_ge(ga_out, NB + i - 3)
                for h in range(GLA_HEADS):
                    k, q = pair(gk2[:, (l - 1) % 2], gq2[:, (l - 1) % 2], ki, qi, h)
                    ins = pe.matmul(bank[2 * (i % 4) + h % 2][:, (h // 2) * P:(h // 2 + 1) * P], k, q, start=True, stop=True)
                ins.then_inc(ga_done, 1)
            pe.wait_ge(ga_added, 7 * NB)
            pe.wait_ge(ga_out, NB + 6)
            pairs = {(0, 1): 0, (2, 3): 1, (0, 2): 2, (0, 3): 3, (1, 2): 4, (1, 3): 5}
            for b in range(NB):
                for h in range(GLA_HEADS):
                    for j in range(b + 1):
                        a = attd[:, b, :] if j == b else atto[:, pairs[j, b], :]
                        at = 2 * (h % 2) + h // 2
                        ins = pe.matmul(bank[4 + b][:, h * P:(h + 1) * P], a[:, at * P:(at + 1) * P],
                                        gv[:, j, h * GLA_DV:(h + 1) * GLA_DV], start=(j == 0), stop=(j == b))
                ins.then_inc(go_done, 1)
            def key_scores(b):
                pe.wait_ge(sub_landed, 16)
                for q in range(QUARTERS):
                    pe.wait_ge(proj_out, late("query", b, 4 * q + 3) + 1)
                    if b > 0:
                        pe.wait_ge(top_done, QUARTERS * (b - 1) + q + 1)
                    for s in range(4):
                        ins = pe.matmul(bank[4 + q][:, s * P:(s + 1) * P], pqT[:, 4 * q + s, :], subT[:, 4 * q + s, :],
                                        start=True, stop=True)
                    ins.then_inc(sub_done, 1)

            def add_rows(b):
                base = TURNS * (2 * b + 1)

                def turn(n, first, last):
                    for i, k in enumerate(SHARED):
                        pe.wait_ge(wdiag_ready, n * len(SHARED) + (len(SHARED) * TURNS * b + i + 1))
                        pe.wait_ge(row_landed[k], n * 16 + 16 * (base + 1))
                        for half in range(2):
                            ins = pe.matmul(bank[half][:], wdiag[:, i, :], ring[k][:, half * COLS:(half + 1) * COLS],
                                            start=(first and i == 0), stop=(last and i == len(SHARED) - 1))
                        ins.then_inc(slot_free[k], 1)

                if b > 0:
                    pe.wait_ge(fin_x, b)
                turn(0, True, False)
                with pe.Fori(1, TURNS - 1) as it:
                    turn(it, False, False)
                turn(TURNS - 1, False, True)

            for kind, b, i in LATE:
                g = late(kind, b, i)
                if (kind, b, i) == ("turn", 2, 0):
                    pe.wait_ge(proj_out, g)
                    add_rows(0)
                    pe.wait_ge(fin_x, 1)
                if kind == "mixed":
                    pe.wait_ge(go_ready, b + 1)
                    ps = begin(g)
                    for j in range(4):
                        ins = pe.transpose(ps[:, j * P:(j + 1) * P], XN[:, b, (4 * i + j) * P:(4 * i + j + 1) * P], ident[:])
                    ins.then_inc(proj_done, 1)
                elif kind == "out":
                    pe.wait_ge(proj_out, late("mixed", b, 1) + 1)
                    plain_tok(C_OUT2 + i, HT, b, begin(g)[:]).then_inc(proj_done, 1)
                elif kind == "turn":
                    pe.wait_ge(xn_ready, BLOCKS[N_PEER] + b + 1)
                    ps = begin(g)
                    for j in range(4):
                        ins = pe.transpose(ps[:, j * P:(j + 1) * P], XN[:, b, (4 * i + j) * P:(4 * i + j + 1) * P], ident[:])
                    ins.then_inc(proj_done, 1)
                elif kind == "query":
                    pe.wait_ge(wq_landed, 64)
                    pe.wait_ge(proj_out, late("turn", b, 1) + 1)
                    ps = begin(g)
                    for k in range(KT):
                        at = k * COLS + (i % 4) * P
                        ins = pe.matmul(ps[:, 0:P], wq[:, i // 4, at:at + P], HT[:, k, b * P:(b + 1) * P], start=(k == 0), stop=(k == KT - 1))
                    ins.then_inc(proj_done, 1)
                else:
                    ps = begin(g)
                    for j in range(4):
                        ins = pe.transpose(ps[:, j * P:(j + 1) * P], HT[:, 4 * i + j, b * P:(b + 1) * P], ident[:])
                    ins.then_inc(proj_done, 1)
                    if i == 1 and b < 3:
                        key_scores(b)
            pe.wait_ge(proj_out, G_OUT2 + len(LATE))
            for b in range(1, NB):
                add_rows(b)
                if b == 1:
                    key_scores(3)

        @block.vector
        def _(dve):
            steps = [0]

            def link(ins):
                steps[0] += 1
                ins.then_inc(dve_step, 1)
                dve.wait_ge(dve_step, steps[0])

            def reciprocal_root(n, b):
                i = STATS[n] + b
                dve.wait_ge(ss_ready, i + 1)
                dve.reciprocal(rstd[:, i:i + 1], ssq[:, i:i + 1]).then_inc(rstd_ready, 1)

            def normed(n):
                for b in range(NB):
                    i = STATS[n] + b
                    dve.wait_ge(ss_ready, i + 1)
                    link(dve.reciprocal(rstd[:, i:i + 1], ssq[:, i:i + 1]))
                    dve.tensor_scalar(XN[:, b, :], X[:, b, :], rstd[:, i:i + 1], None, ALU.mult).then_inc(xn_ready, 1)

            def split(*cs):
                for c in cs:
                    raw, high, low = split_parts(c)
                    dve.wait_ge(w_landed[c % W_SLOTS], 16 * (c // W_SLOTS + 1))
                    link(dve.tensor_copy(high, raw))
                    dve.tensor_tensor(low, raw, high.bitcast(F32), ALU.subtract).then_inc(w_split_v, 1)

            def split_T(n, scale=None):
                for k in range(KT):
                    dve.wait_ge(scaled, KT * SCALED.index(n) + k + 1)
                    src, high, low = bank[4 + k % 4][:], HTH[:, k, :], HTL[:, k, :]
                    if n == N_ATT2:
                        link(dve.tensor_copy(high, src))
                    if scale is None:
                        ins = dve.tensor_tensor(low, src, high.bitcast(F32), ALU.subtract)
                    else:
                        ins = dve.scalar_tensor_tensor(out=low, in0=src, scalar=scale[:, k:k + 1], in1=high.bitcast(F32),
                                                       op0=ALU.mult, op1=ALU.subtract)
                    ins.then_inc(ht_ready, 1)

            def add_rounds(n, b):
                to = XN[:, b, n * COLS:(n + 1) * COLS]
                dve.wait_ge(proj_done, G_FF2 + G_ROUND + NB * n + b + 1)
                dve.tensor_tensor(to, to, bank[NB * n + b][:], ALU.add).then_inc(ff_added, 1)

            def add_post(s, landed, value, following):
                dve.wait_ge(landed, value)
                for b in range(NB):
                    if s == 2:
                        add_rounds(1, b)
                    dve.wait_ge(post_ready, NB * s + b + 1)
                    link(dve.reciprocal(prstd[:, s, b:b + 1], psq[:, s, b, 1:2]))
                    link(dve.scalar_tensor_tensor(out=XN[:, b, :], in0=XN[:, b, :], scalar=prstd[:, s, b:b + 1],
                                                  in1=GROW[:], op0=ALU.mult, op1=ALU.mult))
                    dve.tensor_tensor(X[:, b, :], X[:, b, :], XN[:, b, :], ALU.add).then_inc(x_ready, 1)
                    if b > 0:
                        reciprocal_root(following, b - 1)
                reciprocal_root(following, NB - 1)

            def head_decays(h):
                dve.tensor_scalar(cposh[h % 2][0:72, :], cpos[0:72, :], headsel[0:72, h:h + 1], None, ALU.mult)
                dve.tensor_scalar(cnegh[h % 2][0:72, :], cneg[0:72, :], headsel[0:72, h:h + 1], None, ALU.mult).then_inc(head_ready, 1)

            def attention(lo, hi):
                for u in range(lo, hi + 4):
                    if u < hi:
                        kind, h, b, n = unit(u)
                        dve.wait_ge(sc_done, u + 1)
                        src, mx = score_bank[u % 4][:, 0:n], nmax[:, u:u + 1]
                        if kind == "chk":
                            if b == 0:
                                dve.wait_ge(rel_landed[h % 4], 16 * (h // 4 + 1))
                                link(dve.memset(relb[0:SPAN, h % 4, 0:SPAN], NEG))
                            if u - 2 >= lo:
                                dve.wait_ge(p_ready, u - 1)
                            link(dve.tensor_tensor_reduce(out=biased[:, u % 2, 0:n], in0=src, in1=relb[:, h % 4, n - 1::-1],
                                                          scale=1.0, scalar=-3e38, op0=ALU.add, op1=ALU.max, accum_out=mx))
                            dve.tensor_scalar(mx, mx, -1.0, None, ALU.mult).then_inc(mx_ready, 1)
                        elif kind == "swa":
                            link(dve.tensor_reduce(mx, src, AX.X, ALU.max))
                            dve.tensor_scalar(mx, mx, sinks[:, h:h + 1], -1.0, ALU.max, ALU.mult).then_inc(mx_ready, 1)
                        else:
                            dve.tensor_reduce(mx, src, AX.X, ALU.max, negate=True).then_inc(mx_ready, 1)
                        if kind == "fox" and b == 0 and 1 <= h < HEADS - 1:
                            head_decays(h + 1)
                    v = u - 4
                    if v >= lo:
                        kind, h, b, n = unit(v)
                        dve.wait_ge(p_ready, v + 1)
                        if kind == "swa":
                            link(dve.tensor_tensor(rsum[:, v:v + 1], rsum[:, v:v + 1], skx[:, v:v + 1], ALU.add))
                        link(dve.reciprocal(rinv[:, v:v + 1], rsum[:, v:v + 1]))
                        dve.wait_ge(pv_done, v + 1)
                        w = MEM_HD if kind == "mem" else HD
                        at = h * w + (COLS if kind == "chk" else 0)
                        dve.tensor_scalar(XN[:, b, at:at + w], bank[5 + v % 2][:, 0:w], rinv[:, v:v + 1], None,
                                          ALU.mult).then_inc(y_done, 1)

            normed(N_MIX)
            split_T(N_MIX, gcol[:, GC_MIX, :])
            dve.wait_ge(c_ready, 1)
            for r in range(48):
                dve.wait_ge(ada_landed[r % 3], 16 * (r // 3 + 1))
                dve.tensor_tensor_reduce(out=ada[:, r % 3, :], in0=ada[:, r % 3, :], in1=crow, scale=1.0, scalar=0.0,
                                         op0=ALU.mult, op1=ALU.add, accum_out=mod[:, r:r + 1]).then_inc(ada_used, 1)
                if r % 10 == 2:
                    split(C_IN + 3 + r // 5)
            dve.wait_ge(ada_used, 48)
            dve.wait_ge(consts_landed, 112)
            link(dve.tensor_tensor(mod[:], mod[:], bada[:], ALU.add))
            for i, (scale, gc) in enumerate(((8, GC_ATT2), (32, GC_PEER))):
                dve.scalar_tensor_tensor(out=scol[:, i, :], in0=mod[:, scale:scale + KT], scalar=1.0, in1=gcol[:, gc, :],
                                         op0=ALU.add, op1=ALU.mult)
            dve.wait_ge(masks_ready, 1)
            fz, fe = XN[0:72, 0, 0:512], XN[0:72, 0, 512:1024]
            fc, fr = XN[0:72, 1, 0:512], XN[0:72, 1, 512:1024]
            dve.wait_ge(f_log, 1)
            link(dve.scalar_tensor_tensor(out=fz, in0=fz, scalar=0.0, in1=fe, op0=ALU.min, op1=ALU.subtract))
            dve.memset(fe, 1.0)
            link(dve.memset(fr, 1.0))
            link(dve.tensor_tensor_scan(fc, fe, fz, 0.0, ALU.mult, ALU.add))
            for part in range(3):
                rows = slice(32 * part, 32 * part + HEADS)
                low = cposh[0][0:72, :]
                link(dve.tensor_copy(low, fc))
                dve.tensor_copy(cpos[rows, :], low[rows, :])
                dve.tensor_scalar(cneg[rows, :], low[rows, :], -1.0, None, ALU.mult)
                link(dve.tensor_tensor(fr, fc, low, ALU.subtract))
                link(dve.tensor_copy(fc, fr))
            head_decays(0)
            head_decays(1)
            attention(U_FOX, U_MEM)

            for b in range(NB):
                for half in range(2):
                    i = STATS[N_Y] + 2 * b + half
                    y = XN[:, b, half * COLS:(half + 1) * COLS]
                    dve.wait_ge(ss_ready, i + 1)
                    link(dve.reciprocal(rstd[:, i:i + 1], ssq[:, i:i + 1]))
                    ins = dve.tensor_scalar(y, y, rstd[:, i:i + 1], None, ALU.mult)
                ins.then_inc(xn_ready, 1)
            for b in range(MB):
                i = STATS[N_MEM] + b
                dve.wait_ge(ss_ready, i + 1)
                link(dve.reciprocal(rstd[:, i:i + 1], ssq[:, i:i + 1]))
                dve.tensor_scalar(MX[:, b, :], MX[:, b, :], rstd[:, i:i + 1], None, ALU.mult).then_inc(xn_ready, 1)
            split_T(N_Y, gcol[:, GC_Y, :])
            add_post(0, rows_landed, 80, N_MEMPRE)
            split_T(N_MEMPRE, gcol[:, GC_MEMPRE, :])
            split(C_MQ + 1, C_MQ + 3)
            attention(U_MEM, U_SWA)
            split_T(N_MEMY)
            split(C_MO + 3)
            add_post(1, row1_landed, 16, N_FF)
            split_T(N_FF, gcol[:, GC_FF, :])
            for i in range(2 * C_ROUND):
                r, j = i // C_ROUND, i % C_ROUND
                if j < FF_T // 2:
                    for t in (2 * j, 2 * j + 1):
                        src = bank[(G_FF1 + G_ROUND * r + t) % 4][:]
                        dve.wait_ge(squared, FF_T * r + t + 1)
                        link(dve.tensor_copy(FHH[:, t, :], src))
                        dve.tensor_tensor(FHL[:, t, :], src, FHH[:, t, :].bitcast(F32), ALU.subtract).then_inc(proj_out, 1)
                elif r == 1 and j == 11:
                    for b in range(NB):
                        add_rounds(0, b)
                if C_FF1 + i + 3 < C_IN2:
                    split(C_FF1 + i + 3)
            add_post(2, row2_landed, 16, N_ATT2)
            split_T(N_ATT2)
            split(C_IN2 + 3, C_IN2 + 4, C_IN2 + 5)
            dve.wait_ge(z_log, 1)
            link(dve.scalar_tensor_tensor(out=decay, in0=decay, scalar=0.0, in1=fade[:, 0], op0=ALU.min, op1=ALU.subtract))
            link(dve.memset(fade[:, 1, 0, :], 1.0))
            for j in range(2):
                dve.tensor_tensor_scan(fade[:, 0, j, :], fade[:, 1, 0, :], decay[:, j, :], 0.0, ALU.mult, ALU.add).then_inc(decay_ready, 1)
            dve.wait_ge(decay_ready, 2)
            link(dve.tensor_copy(decay, fade[:, 0]))
            for i, gate in enumerate((16, 40)):
                for k in range(KT):
                    ins = dve.tensor_scalar(diag[:, i, k * P:(k + 1) * P], ident[:], mod[:, gate + k:gate + k + 1], None, ALU.mult)
                ins.then_inc(diag_ready, 1)
            split(C_IN2 + 8)
            dve.wait_ge(rows_landed, 80)
            for b in range(NB):
                dve.wait_ge(proj_out, G_IN2 + 18 + b + 1)
                dve.tensor_tensor(gg[:, b, :], gg[:, b, :], NWROW[:], ALU.mult).then_inc(gg_ready, 1)
            attention(U_SWA, U_END)

            def fading(l):
                m = GLA_HALVES[l]
                if l >= 2:
                    dve.wait_ge(gk_ready, l - 1)
                    dve.wait_ge(gq_ready, l - 1)
                src = decay.rearrange("p j t -> p (j t)").rearrange("p (g r) -> p g r", r=2 * m)
                f = fade[:, l % 2].rearrange("p j t -> p (j t)")
                dst = f.rearrange("p (g r) -> p g r", r=2 * m)
                link(dve.tensor_tensor(dst, src, src[:, :, m - 1:m].broadcast_to(src.shape), ALU.subtract))
                dve.scalar_tensor_tensor(out=f, in0=f, scalar=-1.0, in1=f, op0=ALU.mult, op1=ALU.max).then_inc(fade_in, 1)

            def queries(l):
                dve.wait_ge(fade_out, l + 1)
                if l >= 2:
                    dve.wait_ge(ga_done, NB * (l - 1) + NB)
                dve.tensor_tensor(gq2[:, l % 2], gqT, fade[:, l % 2], ALU.mult).then_inc(gq_ready, 1)

            dve.wait_ge(level_ready, 1)
            fading(0)
            fading(1)
            for n in range(8 * NB):
                l, b = n // NB, n % NB
                if b == 0:
                    queries(l)
                    if l == 7:
                        queries(8)
                if b == 2 and l + 2 < len(GLA_HALVES):
                    fading(l + 2)
                dve.wait_ge(ga_done, n + 1)
                mask = levelmask[:, l:l + 1, :].broadcast_to([P, 2, P])
                if l >= 2:
                    dve.wait_ge(ga_added, n - 2 * NB + 1)
                to, ready = (attd[:, b, :], ga_out) if l == 0 else (masked[:, n % 4, :], ga_masked)
                for r in range(2):
                    half = slice(2 * P * r, 2 * P * (r + 1))
                    ins = dve.tensor_tensor(to[:, half].rearrange("p (h t) -> p h t", h=2),
                                            bank[2 * (n % 4) + r][:, 0:2 * P].rearrange("p (h t) -> p h t", h=2), mask, ALU.mult)
                ins.then_inc(ready, 1)
            dve.wait_ge(gg_ready, NB)
            for b in range(NB):
                dve.wait_ge(go_sq, b + 1)
                dve.tensor_reduce(ssy[:, b, :], masked[:, b, :].rearrange("p (h e) -> p h e", h=GLA_HEADS), AX.X, ALU.add).then_inc(go_ss, 1)
                dve.wait_ge(go_rms, b + 1)
                link(dve.reciprocal(rsy[:, b, :], ssy[:, b, :]))
                for h in range(GLA_HEADS):
                    s = slice(h * GLA_DV, (h + 1) * GLA_DV)
                    ins = dve.scalar_tensor_tensor(out=XN[:, b, COLS + h * GLA_DV:COLS + (h + 1) * GLA_DV], in0=bank[4 + b][:, s],
                                                   scalar=rsy[:, b, h:h + 1], in1=gg[:, b, s], op0=ALU.mult, op1=ALU.mult)
                ins.then_inc(go_ready, 1)
            def add_mixed(b):
                dve.wait_ge(proj_out, late("out", b, 1) + 1)
                link(dve.tensor_tensor(XN[:, b, :], XN[:, b, :], GATE[:, 0, :], ALU.mult))
                dve.tensor_tensor(X[:, b, :], X[:, b, :], XN[:, b, :], ALU.add).then_inc(x_ready, 1)

            for b in range(2):
                add_mixed(b)
                reciprocal_root(N_PEER, b)

            def best_half(vals, pos, src, rest, n):
                for i in range(n):
                    ins = dve.max(vals[:, i, 0:8], src(i))
                link(ins)
                for i in range(n):
                    dve.max_index(pos[:, i, 0:8], vals[:, i, 0:8], src(i))
                    ins = dve.match_replace(rest[:, i, :], vals[:, i, 0:8], src(i), -3e38)
                return ins

            def other_half(vals, pos, rest, n):
                for i in range(n):
                    ins = dve.max(vals[:, i, 8:16], rest[:, i, :])
                link(ins)
                for i in range(n):
                    ins = dve.max_index(pos[:, i, 8:16], vals[:, i, 8:16], rest[:, i, :])
                return ins

            def sums(dst, first, second):
                off = 0
                for a0, na, nb in CAND_PARTS:
                    for h in range(2) if na > 1 else (slice(0, 2),):
                        if na > 1:
                            shape = [P, na, nb]
                            to = dst[:, h, off:off + na * nb].rearrange("p (a b) -> p a b", b=nb)
                            ins = dve.tensor_tensor(to, first[:, h, a0:a0 + na, None].broadcast_to(shape),
                                                    second[:, h, None, 0:nb].broadcast_to(shape), ALU.add)
                        else:
                            ins = dve.tensor_tensor(dst[:, :, off:off + nb], second[:, :, 0:nb],
                                                    first[:, :, a0:a0 + 1].broadcast_to([P, 2, nb]), ALU.add)
                    off += na * nb
                return ins

            halves_v = topv.rearrange("p (h s) k -> p s h k", s=2)
            halves_i = topf.rearrange("p (h s) k -> p s h k", s=2)

            def pick(b, q, step):
                ls, hs = slice(4 * q, 4 * q + 4), slice(2 * q, 2 * q + 2)
                if step == 0:
                    dve.wait_ge(sub_done, QUARTERS * b + q + 1)
                    link(best_half(topv[:, ls, :], topi[:, ls, :], lambda i: bank[4 + q][:, i * P:(i + 1) * P], left, 4))
                elif step == 1:
                    other_half(topv[:, ls, :], topi[:, ls, :], left, 4).then_inc(top_done, 1)
                    dve.wait_ge(top_done, QUARTERS * b + q + 1)
                elif step == 2:
                    sums(cand, halves_v[:, 0, hs], halves_v[:, 1, hs])
                    link(dve.tensor_copy(topf, topi[:, ls, :]))
                    link(dve.tensor_scalar(halves_i[:, 0], halves_i[:, 0], float(N_KEYS), None, ALU.mult))
                    link(sums(cande, halves_i[:, 0], halves_i[:, 1]))
                    link(best_half(bestv[:, hs, :], bestp, lambda i: cand[:, i, :], candl, 2))
                    link(other_half(bestv[:, hs, :], bestp, candl, 2))
                    link(dve.tensor_copy(bestf, bestp))
                else:
                    shape = [P, TOPK, CAND]
                    for i in range(2):
                        ins = dve.tensor_tensor(onehot[i], iota[:, None, :].broadcast_to(shape),
                                                bestf[:, i, :, None].broadcast_to(shape), ALU.is_equal)
                    link(ins)
                    for i in range(2):
                        ins = dve.tensor_tensor(onehot[i], onehot[i], cande[:, i, None, :].broadcast_to(shape), ALU.mult)
                    link(ins)
                    for i in range(2):
                        ins = dve.tensor_reduce(eid[:, i, :], onehot[i], AX.X, ALU.add)
                    link(ins)
                    dve.tensor_copy(expert[:, b % 2, 2 * TOPK * q:2 * TOPK * (q + 1)].rearrange("p (h k) -> p h k", k=TOPK),
                                    eid).then_inc(expert_ready, 1)
                    if q == QUARTERS - 1:
                        dve.tensor_tensor(gates, bestv, bestv[:, :, 0:1].broadcast_to([P, PEER_HEADS, TOPK]), ALU.subtract).then_inc(gate_in, 1)

            def hidden(b, c):
                base = TURNS * 2 * b + 2 * c
                with dve.Fori(0, 2) as it:
                    for k in range(RING):
                        dve.wait_ge(row_landed[k], it * 16 + 16 * (base + 1))
                        dve.tensor_tensor_reduce(out=ring[k], in0=ring[k], in1=XN[:, b, :], scale=1.0, scalar=0.0,
                                                 op0=ALU.mult, op1=ALU.add, accum_out=hslot[:, k:k + 1]).then_inc(slot_free[k], 1)
                    dve.wait_ge(slot_free[RING - 1], it + (base + 2))
                    dve.tensor_copy(hid[:, bass.ds(it * RING + 2 * RING * c, RING)], hslot).then_inc(hid_copied, 1)
                    dve.wait_ge(hid_copied, it + (TURNS * b + 2 * c + 1))

            def prepare(b):
                dve.wait_ge(gate_exp, b + 1)
                link(dve.tensor_reduce(gsum, gates, AX.X, ALU.add))
                link(dve.reciprocal(ginv, gsum))
                dve.tensor_tensor(gates, gates, ginv[:, :, None].broadcast_to([P, PEER_HEADS, TOPK]), ALU.mult)
                if b > 0:
                    dve.wait_ge(fin_x, b)
                link(dve.memset(acc, 0.0))

            def weights(b):
                dve.wait_ge(hid_gelu, b + 1)
                dve.tensor_tensor(wgt, hid, gates.rearrange("p h k -> p (h k)"), ALU.mult).then_inc(wgt_ready, 1)
                dve.wait_ge(wgt_ready, b + 1)

            def weighted(b, t):
                base = TURNS * (2 * b + 1)
                mine = [k for k in range(RING) if k not in SHARED]
                for i, k in enumerate(mine):
                    dve.wait_ge(row_landed[k], t * 16 + 16 * (base + 1))
                    dve.wait_ge(slot_free[mine[i - 1]], t + (base + (2 if i else 1)))
                    dve.scalar_tensor_tensor(out=acc, in0=ring[k], scalar=wgt[:, bass.ds(t * RING + k, 1)],
                                             in1=acc, op0=ALU.mult, op1=ALU.add).then_inc(slot_free[k], 1)

            def add_experts(b):
                for k in (RING - 1, RING - 2):
                    dve.wait_ge(slot_free[k], TURNS * 2 * (b + 1) + 1)
                for half in range(2):
                    s = slice(half * COLS, (half + 1) * COLS)
                    ins = dve.tensor_tensor(acc[:, s], acc[:, s], bank[half][:], ALU.add)
                link(ins)
                link(dve.tensor_tensor(acc, acc, GATE[:, 1, :], ALU.mult))
                dve.tensor_tensor(X[:, b, :], X[:, b, :], acc, ALU.add).then_inc(fin_x, 1)

            def final_norm(b):
                dve.wait_ge(row3_landed, 16)
                dve.wait_ge(fin_rms, b + 1)
                link(dve.reciprocal(rstd[:, 30 + b:31 + b], ssq[:, 30 + b:31 + b]))
                dve.scalar_tensor_tensor(out=XN[:, b, :], in0=X[:, b, :], scalar=rstd[:, 30 + b:31 + b], in1=FINROW[:],
                                         op0=ALU.mult, op1=ALU.mult).then_inc(fin_ready, 1)

            dve.wait_ge(claimed, 1)
            for k in range(RING):
                dve.sem_inc(slot_free[k], 1)
            for step in range(4):
                pick(0, 0, step)
            for b in range(NB):
                dve.wait_ge(proj_out, late("token", b, 1) + 1)
                for c in range(CHUNKS):
                    if b == 0:
                        for i in range(4) if c == 0 else range(2 * c + 2, 2 * c + 4):
                            if i < 4 * (QUARTERS - 1):
                                pick(0, i // 4 + 1, i % 4)
                    if c == CHUNKS - 1:
                        prepare(b)
                    hidden(b, c)
                    if b == 1 and c in (1, 2):
                        reciprocal_root(N_PEER, c + 1)
                    if b > 0 and c == 0:
                        final_norm(b - 1)
                dve.sem_inc(hid_ready, 1)
                weights(b)
                if b + 1 < NB:
                    for t in range(TURNS):
                        weighted(b, t)
                        pick(b + 1, t // 4, t % 4)
                        if b == 0 and t in (4, 8):
                            add_mixed(1 + t // 4)
                else:
                    with dve.Fori(0, TURNS) as it:
                        weighted(b, it)
                add_experts(b)
            final_norm(NB - 1)


def pack(w, cols=HALF):
    k, n = w.shape
    return w.reshape(k // D, KT, P, n // cols, cols).transpose(3, 0, 2, 1, 4).reshape(-1, P, KT * cols)


def column(v, width=P):
    return v.reshape(-1, width).T


def layouts(i):
    w_in, w_in_2 = i["w_in"][0], i["w_in_2"][0]
    nf = HEADS * HD
    a = {}
    a["x"] = i["x"][0].reshape(NB, P, D)
    a["mem"] = i["mem"][0].reshape(MB, P, D).transpose(1, 0, 2)
    a["c"] = i["c_2"]
    main = np.concatenate([w_in[:, :3 * nf], w_in[:, 3 * nf + HEADS:]], axis=1)
    a["w_in"] = pack(main)
    f = np.zeros((D, 72), np.float32)
    bf = np.zeros((P, 1), np.float32)
    for part in range(3):
        f[:, 32 * part:32 * part + HEADS] = w_in[:, 3 * nf:3 * nf + HEADS]
        bf[32 * part:32 * part + HEADS, 0] = i["b_fgt"][0]
    a["w_fgt"] = f.reshape(KT, P, 72).transpose(1, 0, 2).reshape(P, -1)
    a["b_fgt"] = bf
    for n in ("w_out", "w_mk", "w_mv", "w_mq", "w_mo", "w_ff1", "w_ff2"):
        a[n] = pack(i[n][0])
    a["w_out_2"] = pack(i["w_out_2"][0], COLS)
    a["w_pq"] = pack(i["peer_wq_2"][0], COLS)
    aq = w_in_2[:, :512].reshape(D, 2, 4, HD).transpose(0, 2, 1, 3).reshape(D, 512)
    ak, av, gq, gk, gv, gg, glr = np.split(w_in_2[:, 512:], np.cumsum([128, 128, 256, 256, 512, 512]), axis=1)
    third = np.concatenate([gk, glr, np.zeros((D, 512 - 256 - GLA_RANK), np.float32)], axis=1)
    a["w_in_2"] = pack(np.concatenate([aq, ak, av, gq, third, gv, gg], axis=1))
    rel = np.clip(np.arange(REL_W) - (P - 1), -MAX_REL, MAX_REL) + MAX_REL
    a["rel"] = i["rel_bias"][0][:, rel]
    a["gain_cols"] = np.stack([column(v) for v in (
        i["g_mix_pre"][0], np.concatenate([i["g_fox_out"][0], i["g_chk_out"][0]]), i["g_mem_kv"][0],
        i["g_mem_pre"][0], i["g_ff_pre"][0], i["norm1_w_2"][0], i["norm2_w_2"][0])], axis=1)
    a["gain_rows"] = np.stack([i["g_mix_post"][0], i["g_mem_post"][0], i["g_ff_post"][0], i["final_norm_w_2"]])[:, None, :]
    a["gla_norm"] = i["gla_norm_w_2"]
    a["gla_gate_up"] = i["gla_gate_up_2"][0]
    a["gla_gate_bias"] = column(i["gla_gate_bias_2"][0])
    a["sinks"] = i["attn_sinks_2"]
    a["w_ada"] = i["w_ada_2"][0].T.reshape(48, P, D)
    a["b_ada"] = column(i["b_ada_2"][0])
    a["subkeys"] = i["peer_subkeys_2"][0].reshape(16, N_KEYS, P).transpose(2, 0, 1)
    a["peer_u"] = i["peer_u_2"][0]
    a["peer_v"] = i["peer_v_2"][0]
    return a


def kernel(**inputs):
    import concourse.bacc as bacc
    from concourse.bass_utils import run_bass_kernel_spmd

    nc = bacc.Bacc("TRN2", target_bir_lowering=False, num_devices=1)
    arrays, args = {}, {}
    for name, a in layouts({k: np.asarray(v) for k, v in inputs.items()}).items():
        a = np.ascontiguousarray(a)
        arrays[f"in_{name}"] = a
        args[name] = nc.dram_tensor(f"in_{name}", a.shape, mybir.dt.from_np(a.dtype), kind="ExternalInput").ap()
    out = nc.dram_tensor("out", (NB, P, D), F32, kind="ExternalOutput").ap()
    build(nc, args, out)
    r = run_bass_kernel_spmd(nc, [arrays], core_ids=[0])
    return r.results[0]["out"].reshape(1, TOK, D)
```
